# Optimizing a Trainium2 kernel written in Bass

```python
import math
import jax, jax.numpy as jnp
from jax import lax
import numpy as np

D_MODEL = 1024
BATCH = 1
SEQ = 512
DEPTH = 1

GRID_W = 64
ATT_HEADS = 8
ATT_KV_HEADS = 2
ATT_HEAD_DIM = 64
ATT_WIDTH = ATT_HEADS * ATT_HEAD_DIM
ATT_KV_WIDTH = ATT_KV_HEADS * ATT_HEAD_DIM
ROPE_AXIS_DIM = ATT_HEAD_DIM // 2
ROPE_THETA = 10000.0
Q_BLOCK = 128
HG_HEADS = 4
HG_F_DIM = 128
HG_I_DIM = 128
HG_F_WIDTH = HG_HEADS * HG_F_DIM
HG_WIDTH = HG_HEADS * HG_I_DIM
HG_CHUNK = 64
MIN_FORGET = 1e-6
N_BRANCHES = 2
N_EXPERTS = 16
EC_CAPACITY_FACTOR = 2
EXPERT_FF = 2048
NORM_EPS = 1e-6

IN_SPLITS = (ATT_WIDTH, ATT_KV_WIDTH, ATT_KV_WIDTH,
             HG_F_WIDTH, HG_F_WIDTH, HG_F_WIDTH,
             HG_WIDTH, HG_WIDTH,
             N_BRANCHES * D_MODEL)
IN_WIDTH = sum(IN_SPLITS)


def rms_norm(x, w):
    xf = x.astype(jnp.float32)
    y = xf * lax.rsqrt(jnp.mean(xf * xf, axis=-1, keepdims=True) + NORM_EPS)
    return (y * w.astype(jnp.float32)).astype(x.dtype)

def axial_rope_tables(seq_len):
    rows = seq_len // GRID_W
    row_id = jnp.repeat(jnp.arange(rows, dtype=jnp.float32), GRID_W)
    col_id = jnp.tile(jnp.arange(GRID_W, dtype=jnp.float32), rows)
    inv_freq = ROPE_THETA ** (-jnp.arange(0, ROPE_AXIS_DIM, 2, dtype=jnp.float32) / ROPE_AXIS_DIM)
    ang = jnp.stack([row_id[:, None] * inv_freq, col_id[:, None] * inv_freq], axis=1)
    return jnp.cos(ang), jnp.sin(ang)

def apply_axial_rope(x, cos, sin):
    B, S, H, hd = x.shape
    xr = x.reshape(B, S, H, 2, 2, ROPE_AXIS_DIM // 2)
    x1, x2 = xr[..., 0, :], xr[..., 1, :]
    cs, sn = cos[None, :, None], sin[None, :, None]
    out = jnp.stack([x1 * cs - x2 * sn, x2 * cs + x1 * sn], axis=-2)
    return out.reshape(B, S, H, hd)

def blocked_bidirectional_gqa(q, k, v):
    B, S, _, _ = q.shape
    G = ATT_HEADS // ATT_KV_HEADS
    n_blk = S // Q_BLOCK
    qb = q.reshape(B, n_blk, Q_BLOCK, ATT_KV_HEADS, G, ATT_HEAD_DIM).transpose(1, 0, 3, 4, 2, 5)
    kt = k.transpose(0, 2, 1, 3)
    vt = v.transpose(0, 2, 1, 3)
    scale = ATT_HEAD_DIM ** -0.5

    def one_block(qblk):
        s = jnp.einsum('bhgqd,bhkd->bhgqk', qblk, kt) * scale
        p = jax.nn.softmax(s, axis=-1)
        return jnp.einsum('bhgqk,bhkd->bhgqd', p, vt)

    o = lax.map(one_block, qb)
    return o.transpose(1, 0, 4, 2, 3, 5).reshape(B, S, ATT_WIDTH)

def gla_chunk_scan(q, k, v, log_f):
    B, S, H, Dk = q.shape
    Dv = v.shape[-1]
    n = S // HG_CHUNK

    def to_chunks(a):
        return a.reshape(B, n, HG_CHUNK, H, a.shape[-1]).transpose(1, 0, 3, 2, 4)

    qc, kc, vc, gc = to_chunks(q), to_chunks(k), to_chunks(v), to_chunks(log_f)
    lower = jnp.tril(jnp.ones((HG_CHUNK, HG_CHUNK), dtype=bool))[:, :, None]
    lower_f = lower.astype(jnp.float32)

    def step(state, inp):
        qi, ki, vi, gi = inp
        b = jnp.cumsum(gi, axis=-2)
        o_inter = jnp.einsum('bhcd,bhde->bhce', qi * jnp.exp(b), state)
        diff = b[:, :, :, None, :] - b[:, :, None, :, :]
        decay = jnp.exp(jnp.where(lower, diff, 0.0)) * lower_f
        scores = jnp.einsum('bhid,bhjd,bhijd->bhij', qi, ki, decay)
        o_intra = jnp.einsum('bhij,bhje->bhie', scores, vi)
        b_last = b[:, :, -1:, :]
        new_state = (jnp.exp(b_last[:, :, 0, :])[..., None] * state
                     + jnp.einsum('bhcd,bhce->bhde', ki * jnp.exp(b_last - b), vi))
        return new_state, o_inter + o_intra

    init = jnp.zeros((B, H, Dk, Dv), jnp.float32)
    _, o = lax.scan(step, init, (qc, kc, vc, gc))
    return o.transpose(1, 0, 3, 2, 4).reshape(B, S, H, Dv)

def hgrn2_forget(z, lb):
    f = lb + (1.0 - lb) * jax.nn.sigmoid(z)
    log_f = jnp.log(jnp.maximum(f, MIN_FORGET))
    one_minus_f = (1.0 - lb) * jax.nn.sigmoid(-z)
    return log_f, one_minus_f

def token_mixer(h, lb, w_in, q_norm_w, k_norm_w, hg_norm_w, w_branch_att, w_branch_hg, w_out,
                rope_cos, rope_sin):
    B, S, D = h.shape
    f32 = jnp.float32
    split_idx = np.cumsum(IN_SPLITS)[:-1].tolist()
    proj = jnp.einsum('bsd,de->bse', h, w_in)
    aq, ak, av, hq, hz_f, hz_b, hi, hgate, gate_logits = jnp.split(proj, split_idx, axis=-1)

    q = aq.astype(f32).reshape(B, S, ATT_HEADS, ATT_HEAD_DIM)
    k = ak.astype(f32).reshape(B, S, ATT_KV_HEADS, ATT_HEAD_DIM)
    v = av.astype(f32).reshape(B, S, ATT_KV_HEADS, ATT_HEAD_DIM)
    q = apply_axial_rope(rms_norm(q, q_norm_w), rope_cos, rope_sin)
    k = apply_axial_rope(rms_norm(k, k_norm_w), rope_cos, rope_sin)
    o_att = blocked_bidirectional_gqa(q, k, v)

    lb = lb.astype(f32)
    hqh = jax.nn.silu(hq.astype(f32)).reshape(B, S, HG_HEADS, HG_F_DIM)
    hv = hi.astype(f32).reshape(B, S, HG_HEADS, HG_I_DIM)
    logf_f, kf = hgrn2_forget(hz_f.astype(f32), lb[0])
    logf_b, kb = hgrn2_forget(hz_b.astype(f32), lb[1])
    shp = (B, S, HG_HEADS, HG_F_DIM)
    o_fwd = gla_chunk_scan(hqh, kf.reshape(shp), hv, logf_f.reshape(shp))
    flip = lambda a: jnp.flip(a, axis=1)
    o_bwd = flip(gla_chunk_scan(flip(hqh), flip(kb.reshape(shp)), flip(hv), flip(logf_b.reshape(shp))))
    o_h = rms_norm(o_fwd + o_bwd, hg_norm_w) * jax.nn.silu(
        hgate.astype(f32).reshape(B, S, HG_HEADS, HG_I_DIM))
    o_hg = o_h.reshape(B, S, HG_WIDTH)

    ya = jnp.einsum('bsw,wd->bsd', o_att.astype(h.dtype), w_branch_att)
    yh = jnp.einsum('bsw,wd->bsd', o_hg.astype(h.dtype), w_branch_hg)
    g = jax.nn.sigmoid(gate_logits.astype(f32)).reshape(B, S, N_BRANCHES, D)
    merged = (g[:, :, 0] * ya.astype(f32) + g[:, :, 1] * yh.astype(f32)).astype(h.dtype)
    return jnp.einsum('bsd,de->bse', merged, w_out)

def expert_choice_ffn(h, w_router, w_gate, w_up, w_down):
    B, S, D = h.shape
    cap = EC_CAPACITY_FACTOR * S // N_EXPERTS
    logits = jnp.einsum('bsd,de->bse', h.astype(jnp.float32), w_router.astype(jnp.float32))
    affinity = jax.nn.softmax(logits, axis=-1)
    top_w, top_idx = lax.top_k(affinity.transpose(0, 2, 1), cap)
    xe = jax.vmap(lambda hb, ib: hb[ib])(h, top_idx)
    hid = jax.nn.silu(jnp.einsum('becd,edf->becf', xe, w_gate)) * jnp.einsum('becd,edf->becf', xe, w_up)
    ye = jnp.einsum('becf,efd->becd', hid, w_down) * top_w[..., None].astype(h.dtype)
    combine = lambda yb, ib: jnp.zeros((S, D), h.dtype).at[ib.reshape(-1)].add(yb.reshape(-1, D))
    return jax.vmap(combine)(ye, top_idx)

def first_inputs(seed: int = 0) -> dict:
    key = jax.random.key(seed)
    ks = jax.random.split(key, 20)
    L, D = DEPTH, D_MODEL
    f32 = jnp.float32

    def nrm(k, shape, fan_in, scale=1.0):
        return jax.random.normal(k, shape, f32) * (scale * fan_in ** -0.5)

    def gain(k, shape):
        return 1.0 + 0.02 * jax.random.normal(k, shape, f32)

    return {
        "x": jax.random.normal(ks[0], (BATCH, SEQ, D), f32),
        "c": jax.random.normal(ks[1], (BATCH, D), f32),
        "ada_w": nrm(ks[2], (L, D, 6 * D), D, 0.5),
        "ada_b": 0.02 * jax.random.normal(ks[3], (L, 6 * D), f32),
        "norm_mix_w": gain(ks[4], (L, D)),
        "norm_ffn_w": gain(ks[5], (L, D)),
        "w_in": nrm(ks[6], (L, D, IN_WIDTH), D),
        "q_norm_w": gain(ks[7], (L, ATT_HEAD_DIM)),
        "k_norm_w": gain(ks[8], (L, ATT_HEAD_DIM)),
        "hg_lower_bounds": jax.random.normal(ks[9], (L, 2, HG_F_WIDTH), f32),
        "hg_norm_w": gain(ks[10], (L, HG_I_DIM)),
        "w_branch_att": nrm(ks[11], (L, ATT_WIDTH, D), ATT_WIDTH),
        "w_branch_hg": nrm(ks[12], (L, HG_WIDTH, D), HG_WIDTH),
        "w_out": nrm(ks[13], (L, D, D), D),
        "w_router": nrm(ks[14], (L, D, N_EXPERTS), D),
        "w_exp_gate": nrm(ks[15], (L, N_EXPERTS, D, EXPERT_FF), D),
        "w_exp_up": nrm(ks[16], (L, N_EXPERTS, D, EXPERT_FF), D),
        "w_exp_down": nrm(ks[17], (L, N_EXPERTS, EXPERT_FF, D), EXPERT_FF),
    }

def first_block(x, c, ada_w, ada_b, norm_mix_w, norm_ffn_w, w_in, q_norm_w, k_norm_w,
              hg_lower_bounds, hg_norm_w, w_branch_att, w_branch_hg, w_out, w_router,
              w_exp_gate, w_exp_up, w_exp_down):
    rope_cos, rope_sin = axial_rope_tables(x.shape[1])
    lb_soft = jax.nn.softmax(hg_lower_bounds.astype(jnp.float32), axis=0)
    lb_all = jnp.cumsum(lb_soft, axis=0) - lb_soft[0]
    c_act = jax.nn.silu(c)
    for l in range(DEPTH):
        mod = (jnp.einsum('bd,de->be', c_act, ada_w[l]) + ada_b[l])[:, None, :]
        shift1, scale1, gate1, shift2, scale2, gate2 = jnp.split(mod, 6, axis=-1)
        h = rms_norm(x, norm_mix_w[l]) * (1.0 + scale1) + shift1
        x = x + gate1 * token_mixer(h, lb_all[l], w_in[l], q_norm_w[l], k_norm_w[l], hg_norm_w[l],
                                    w_branch_att[l], w_branch_hg[l], w_out[l], rope_cos, rope_sin)
        h = rms_norm(x, norm_ffn_w[l]) * (1.0 + scale2) + shift2
        x = x + gate2 * expert_choice_ffn(h, w_router[l], w_exp_gate[l], w_exp_up[l], w_exp_down[l])
    return x


D_MIX = D_MODEL
C_CONV = D_MIX // 2
C_POOL = D_MIX - C_CONV
CONV_HEADS = 8
CONV_WIDTH = 31
POOL_WINDOWS = (2, 4, 8, 16)
N_POOL_GROUPS = len(POOL_WINDOWS)
POOL_GROUP = C_POOL // N_POOL_GROUPS
D_IN = 2 * C_CONV + C_POOL
D_FF = ((8 * D_MODEL // 3 + 255) // 256) * 256
RMS_EPS = 1e-6
LN_EPS = 1e-5


def rmsnorm(x, g):
    xf = x.astype(jnp.float32)
    y = xf * lax.rsqrt(jnp.mean(xf * xf, axis=-1, keepdims=True) + RMS_EPS)
    return (y * g.astype(jnp.float32)).astype(x.dtype)

def layernorm(x, g, b):
    xf = x.astype(jnp.float32)
    mu = jnp.mean(xf, axis=-1, keepdims=True)
    var = jnp.mean(jnp.square(xf - mu), axis=-1, keepdims=True)
    y = (xf - mu) * lax.rsqrt(var + LN_EPS)
    return (y * g.astype(jnp.float32) + b.astype(jnp.float32)).astype(x.dtype)

def conformer_conv_group(a, gate, w_dw, b_dw, ln_g, ln_b):
    u = a * jax.nn.sigmoid(gate)
    k = w_dw.astype(u.dtype)[:, None, :]
    v = lax.conv_general_dilated(
        u, k, window_strides=(1,), padding=[(CONV_WIDTH - 1, 0)],
        dimension_numbers=("NWC", "WIO", "NWC"),
        feature_group_count=C_CONV) + b_dw.astype(u.dtype)
    v = layernorm(v, ln_g, ln_b)
    return jax.nn.silu(v)

def multiscale_pool_group(p, w_pool, s_pool):
    seq = p.shape[1]
    pos = jnp.arange(seq)
    outs = []
    for i, w in enumerate(POOL_WINDOWS):
        seg = p[..., i * POOL_GROUP:(i + 1) * POOL_GROUP].astype(jnp.float32)
        cs = jnp.cumsum(seg, axis=1)
        lag = jnp.pad(cs, ((0, 0), (w, 0), (0, 0)))[:, :seq]
        cnt = jnp.minimum(pos + 1, w).astype(jnp.float32)[None, :, None]
        y = ((cs - lag) / cnt - seg).astype(p.dtype)
        outs.append(jnp.einsum("bsg,gh->bsh", y, w_pool[i]))
    return jnp.concatenate(outs, axis=-1) * s_pool

def swiglu(x, w_gate, w_up, w_down):
    return (jax.nn.silu(x @ w_gate) * (x @ w_up)) @ w_down

def second_inputs(seed: int = 0) -> dict:
    key = jax.random.key(seed)
    ks = jax.random.split(key, 20)
    f = jnp.float32
    n = lambda k, s, sc: jax.random.normal(k, s, f) * sc
    return {
        "x": jax.random.normal(ks[0], (BATCH, SEQ, D_MODEL), f),
        "g_mix": 1.0 + n(ks[1], (DEPTH, D_MODEL), 0.05),
        "w_in": n(ks[2], (DEPTH, D_MODEL, D_IN), D_MODEL ** -0.5),
        "b_in": n(ks[3], (DEPTH, D_IN), 0.02),
        "w_dw": n(ks[4], (DEPTH, CONV_WIDTH, C_CONV), CONV_WIDTH ** -0.5),
        "b_dw": n(ks[5], (DEPTH, C_CONV), 0.02),
        "ln_g": 1.0 + n(ks[6], (DEPTH, C_CONV), 0.05),
        "ln_b": n(ks[7], (DEPTH, C_CONV), 0.02),
        "w_pool": n(ks[8], (DEPTH, N_POOL_GROUPS, POOL_GROUP, POOL_GROUP), POOL_GROUP ** -0.5),
        "s_pool": 1.0 + n(ks[9], (DEPTH, C_POOL), 0.1),
        "w_out": n(ks[10], (DEPTH, D_MIX, D_MODEL), D_MIX ** -0.5),
        "g_ffn": 1.0 + n(ks[11], (DEPTH, D_MODEL), 0.05),
        "w_gate": n(ks[12], (DEPTH, D_MODEL, D_FF), D_MODEL ** -0.5),
        "w_up": n(ks[13], (DEPTH, D_MODEL, D_FF), D_MODEL ** -0.5),
        "w_down": n(ks[14], (DEPTH, D_FF, D_MODEL), D_FF ** -0.5),
        "g_final": 1.0 + n(ks[15], (D_MODEL,), 0.05),
    }

def second_block(x, g_mix, w_in, b_in, w_dw, b_dw, ln_g, ln_b, w_pool, s_pool,
              w_out, g_ffn, w_gate, w_up, w_down, g_final):
    h = x
    for l in range(DEPTH):
        xn = rmsnorm(h, g_mix[l])
        z = xn @ w_in[l] + b_in[l]
        a = z[..., :C_CONV]
        gate = z[..., C_CONV:2 * C_CONV]
        p = z[..., 2 * C_CONV:]
        y_conv = conformer_conv_group(a, gate, w_dw[l], b_dw[l], ln_g[l], ln_b[l])
        y_pool = multiscale_pool_group(p, w_pool[l], s_pool[l])
        y = jnp.concatenate([y_conv, y_pool], axis=-1)
        h = h + y @ w_out[l]
        h = h + swiglu(rmsnorm(h, g_ffn[l]), w_gate[l], w_up[l], w_down[l])
    return rmsnorm(h, g_final)


def setup_inputs(seed=0):
    out = dict(first_inputs(seed))
    for name, value in second_inputs(seed + 1).items():
        if name != "x":
            out[name + "_2"] = value
    return out


def reference(
    x, c, ada_w, ada_b, norm_mix_w, norm_ffn_w, w_in, q_norm_w, k_norm_w, hg_lower_bounds,
    hg_norm_w, w_branch_att, w_branch_hg, w_out, w_router, w_exp_gate, w_exp_up, w_exp_down,
    g_mix_2, w_in_2, b_in_2, w_dw_2, b_dw_2, ln_g_2, ln_b_2, w_pool_2, s_pool_2, w_out_2,
    g_ffn_2, w_gate_2, w_up_2, w_down_2, g_final_2,
):
    x = first_block(
        x, c, ada_w, ada_b, norm_mix_w, norm_ffn_w, w_in, q_norm_w, k_norm_w, hg_lower_bounds,
        hg_norm_w, w_branch_att, w_branch_hg, w_out, w_router, w_exp_gate, w_exp_up, w_exp_down,
    )
    return second_block(
        x, g_mix_2, w_in_2, b_in_2, w_dw_2, b_dw_2, ln_g_2, ln_b_2, w_pool_2, s_pool_2, w_out_2,
        g_ffn_2, w_gate_2, w_up_2, w_down_2, g_final_2,
    )


_drawn_inputs = setup_inputs


def setup_inputs(seed=0):
    import zlib

    import numpy as np

    out = dict(_drawn_inputs(seed))
    spreads = {}
    factors = {'ada_b': 4.084,
     'norm_mix_w': 8.0,
     'norm_ffn_w': 7.7,
     'q_norm_w': 8.0,
     'k_norm_w': 8.0,
     'hg_norm_w': 8.0,
     'b_in_2': 57.424,
     'b_dw_2': 115.526,
     'ln_b_2': 200.0,
     'g_mix_2': 8.0,
     'ln_g_2': 64.0,
     's_pool_2': 8.0,
     'g_ffn_2': 8.0}
    for name, (base, spread) in spreads.items():
        noise = np.random.default_rng([zlib.crc32(name.encode()), seed]).standard_normal(out[name].shape)
        drawn = base * np.exp(spread * noise) if base else spread * noise
        out[name] = __import__('jax').numpy.asarray(drawn.astype(out[name].dtype))
    for name, factor in factors.items():
        out[name] = (out[name] * factor).astype(out[name].dtype)
    return out
```

```python
from contextlib import ExitStack

import numpy as np

import concourse.bass as bass
from concourse import mybir

F32 = mybir.dt.float32
ALU = mybir.AluOpType
ACT = mybir.ActivationFunctionType
AX = mybir.AxisListType.X

S, D, TC = 512, 1024, 4
KD = D // 128
NE, CAP, FF = 16, 64, 2048
EPS = 1e-6
LEVELS = (1, 2, 4, 8, 16, 32, 64)
WIN = (2, 4, 8, 16)
FT = 22

CST = {}
_o = 0
for _n, _w in (("ident", 128), ("ones", 128), ("tri", 128), ("bo64", 128), ("rot", 128), ("o128", 128),
               ("o512", 128), ("iota", 64), ("popc", 64), ("ropec", 512), ("ropes", 512), ("eps6", 1), ("eps5", 1),
               ("lev", 128 * 7)):
    CST[_n] = (_o, _w)
    _o += _w
NCST = _o
VEC = {}
_o = 0
for _n, _w in (("nmw", 8), ("nfw", 8), ("qn", 1), ("kn", 1), ("lb", 8), ("hgw", 1), ("bin", 12), ("wdw", 124),
               ("bdw", 4), ("lng", 4), ("lnb", 4), ("spool", 4), ("gmix", 8), ("gffn", 8), ("c", 8),
               ("wr", 128), ("wpool", 512)):
    VEC[_n] = (_o, _w)
    _o += _w
NVEC = _o


class Queue:

    def __init__(self, name):
        self.name, self.items, self.count, self.seen = name, [], 0, {}

    def wait(self, marks):
        for m in marks:
            if m is not None and self.seen.get(m[0], 0) < m[1]:
                self.seen[m[0]] = m[1]
                self.items.append(("wait", m))

    def do(self, fn, *marks):
        self.wait(marks)
        self.count += 1
        self.items.append(("inc", fn, (self.name, 1)))
        return (self.name, self.count)

    def quiet(self, fn, *marks):
        self.wait(marks)
        self.items.append(("run", fn))

    def dma(self, fn, sem, value, *marks):
        self.wait(marks)
        self.items.append(("inc", fn, (sem, 16)))
        return (sem, value)

    def emit(self, eng, sems):
        for it in self.items:
            if it[0] == "wait":
                eng.wait_ge(sems[it[1][0]], it[1][1])
            elif it[0] == "run":
                it[1](eng)
            else:
                it[1](eng).then_inc(sems[it[2][0]], it[2][1])


def build(nc, t, out):
    with ExitStack() as ctx:
        AR = 52800
        A = ctx.enter_context(nc.sbuf_tensor("arena", [128, AR], F32))
        PS = ctx.enter_context(nc.psum_tensor("ps", [128, 8, 512], F32))

        pe, dve, act, pool, sp = (Queue(n) for n in ("pe", "dve", "act", "pool", "sp"))
        dsems = {}

        def load(q, dst, src, sem, *marks):
            dsems[sem] = dsems.get(sem, 0) + 16
            return q.dma(lambda e: e.dma_start(dst, src), sem, dsems[sem], *marks)

        top = [0]

        def take(n):
            o = top[0]
            top[0] += n
            assert top[0] <= AR, top[0]
            return o

        def at(o, n):
            return A[:, o:o + n]

        def raw(o, dims):
            b = A[:, o:o + 1]
            return bass.AP(b.tensor, b.offset, [b.ap[0]] + [list(d) for d in dims])

        def bank(b, n=512, o=0):
            return PS[:, b, o:o + n]

        o_cst, o_vec = take(NCST), take(NVEC)

        def cst(n):
            return at(o_cst + CST[n][0], CST[n][1])

        def vec(n):
            return at(o_vec + VEC[n][0], VEC[n][1])

        def vcol(n, i):
            return at(o_vec + VEC[n][0] + i, 1)

        ident, ones, tri = cst("ident"), cst("ones"), cst("tri")
        sm = take(900)
        sm_top = [sm]

        def small(n):
            o = sm_top[0]
            sm_top[0] += n
            assert sm_top[0] <= sm + 900
            return o

        gate1_o, gate2_o = take(1024), take(1024)
        base = top[0]

        W = 2048
        NR0 = 6
        ring_o = [take(W) for _ in range(NR0)]
        work = top[0]
        chunks = []
        pos = [0]
        slots = list(range(NR0))
        last_user = {s: None for s in slots}
        slot_free = {s: () for s in slots}
        uses = {s: 0 for s in slots}

        class Chunk:
            pass

        def chunk(src, shape):
            c = Chunk()
            s = slots[pos[0] % len(slots)]
            pos[0] += 1
            uses[s] += 1
            c.slot, c.prev, c.first = s, last_user[s], slot_free[s]
            last_user[s] = c
            c.released = None
            c.mark = (f"r{s}", 16 * uses[s])
            ap = at(ring_o[s], W)
            c.ap = ap.rearrange("p (k n) -> p k n", k=shape[0]) if shape[0] > 1 else ap
            c.src = src
            chunks.append(c)
            return c

        def add_slot(o, marks):
            s = len(ring_o)
            ring_o.append(o)
            slots.append(s)
            last_user[s], uses[s], slot_free[s] = None, 0, tuple(marks)

        def col_chunk(w, n):
            return chunk(w[:, n * 256:(n + 1) * 256].rearrange("(k p) n -> p k n", p=128), (8, 256))

        m_cst = load(act, at(o_cst, NCST), t["cst"], "l_cst")
        m_vec = load(act, at(o_vec, NVEC), t["vec"], "l_vec")

        def reuse(lst):
            out = []
            for x in lst:
                out += list(x) if isinstance(x, list) else [x]
            return out

        bfree = {b: [] for b in range(8)}

        class Work:

            def __init__(self, start):
                self.o = start

            def take(self, n):
                o = self.o
                self.o += n
                assert self.o <= AR, self.o
                return o

        wk = Work(work)
        hT = wk.take(4096)
        QQ, KK = wk.take(2048), wk.take(2048)
        TTa, TTb = wk.take(2048), wk.take(1024)
        q0 = wk.take(1024)
        PT = wk.take(4096)
        Vp = wk.take(1024)
        qT = wk.take(2048)
        kd = wk.take(1024)
        va = wk.take(512)
        Pb = wk.take(1024)
        PTa = wk.take(2048)
        oatt = wk.take(2048)
        ohg = wk.take(2048)
        sgh = wk.take(1024)
        tmp = wk.take(2048)
        x_o, xs_o = QQ, PT
        assert PT + 4096 <= qT and QQ + 4096 <= PT
        acc_o, adab_o = tmp, PTa

        xv = t["x"].rearrange("b (c p) d -> p (b c) d", p=128)
        m_x = load(act, at(x_o, 4096).rearrange("p (c d) -> p c d", c=4), xv, "l_x")
        m_ab = load(act, A[0:1, adab_o:adab_o + 2048], t["ada_b"][:, 0:2048], "l_ab")

        csg, cact = small(8), small(8)
        a = act.do(lambda e: e.activation(at(csg, 8), vec("c"), ACT.Sigmoid), m_vec)
        m_c = dve.do(lambda e: e.tensor_tensor(at(cact, 8), at(csg, 8), vec("c"), ALU.mult), a, m_vec)

        lbe, lbr, lbs, lbv, oml = small(8), small(8), small(8), small(8), small(8)
        b = dve.do(lambda e: e.tensor_tensor(at(lbe, 8), vec("lb"), vec("lb"), ALU.subtract), m_vec)
        a = act.do(lambda e: e.activation(at(lbs, 8), at(lbe, 8), ACT.Exp), b)
        b = dve.do(lambda e: e.reciprocal(at(lbr, 8), at(lbs, 8)), a)
        b = dve.do(lambda e: e.tensor_tensor(at(lbs, 8), at(lbs, 8), at(lbr, 8), ALU.mult), b)
        b = dve.do(lambda e: e.tensor_tensor(at(lbv, 8), at(lbs, 8), at(lbs, 8), ALU.subtract), b)
        m_lb = dve.do(lambda e: e.tensor_scalar(at(oml, 8), at(lbv, 8), -1.0, 1.0, ALU.mult, ALU.add), b)

        def rms(x, xs, marks, free, scr, scr_marks):
            st = small(8)
            outm = []
            for c in range(TC):
                a = act.do(lambda e, c=c: e.activation(at(scr + 1024 * (c % 2), 1024), at(x + 1024 * c, 1024), ACT.Square,
                                                       scale=1.0 / 32, accum_out=at(st + c, 1)),
                           marks[c], *(scr_marks if c == 0 else ()))
                _, b = rsqrt(at(st + 4 + c, 1), at(st + c, 1), "eps6", a)
                outm.append(dve.do(lambda e, c=c: e.tensor_scalar(at(xs + 1024 * c, 1024), at(x + 1024 * c, 1024),
                                                                  at(st + 4 + c, 1), None, ALU.mult),
                                   b, *(free if c == 0 else ())))
            return outm

        def rsqrt(dst, src, eps, *marks):
            a = act.do(lambda e: e.activation(dst, src, ACT.Sqrt, bias=cst(eps)), *marks, m_cst)
            return a, dve.do(lambda e: e.reciprocal(dst, dst), a)

        def turn(xs, marks, dst, scale, shift, sc_marks, free, banks):
            outm = []
            for k in range(KD):
                bk = banks[k % len(banks)]
                for c in range(TC):
                    f = lambda e, k=k, c=c, bk=bk: e.transpose(bank(bk, 128, 128 * c), at(xs + 1024 * c + 128 * k, 128), ident)
                    if c < TC - 1:
                        pe.quiet(f, m_cst, marks[c], *(bfree[bk] if c == 0 else ()))
                    else:
                        p = pe.do(f, m_cst, marks[c])
                fr = free if k == 0 else ()
                if k % 2 == 0:
                    m = dve.do(lambda e, k=k, bk=bk: e.tensor_scalar(
                        at(dst + 512 * k, 512), bank(bk), scale(k), shift(k) if shift else None, ALU.mult,
                        *((ALU.add,) if shift else ())), p, *sc_marks, *fr)
                elif shift:
                    m = act.do(lambda e, k=k, bk=bk: e.activation(at(dst + 512 * k, 512), bank(bk), ACT.Identity,
                                                                  bias=shift(k), scale=scale(k)), p, *sc_marks, *free)
                else:
                    m = act.do(lambda e, k=k, bk=bk: e.activation(at(dst + 512 * k, 512), bank(bk), ACT.Copy,
                                                                  scale=scale(k)), p, *sc_marks, *free)
                bfree[bk] = [m]
                outm.append(m)
            return outm

        ada_free = [None]

        def ada(j, *marks):
            for k in range(KD):
                c = chunk(t["ada_w"][k * 128:(k + 1) * 128, j * 2048:(j + 1) * 2048], (1, 2048))
                if k == 0:
                    m = dve.do(lambda e, c=c: e.tensor_scalar(at(acc_o, 2048), c.ap, at(cact, 1), None, ALU.mult),
                               c.mark, m_c, ada_free[0], *marks)
                else:
                    m = dve.do(lambda e, c=c, k=k: e.scalar_tensor_tensor(
                        out=at(acc_o, 2048), in0=c.ap, scalar=at(cact + k, 1), in1=at(acc_o, 2048),
                        op0=ALU.mult, op1=ALU.add), c.mark, m)
                c.released = m
            return m

        def ada_cols(half, m, m_bias, bk, o):
            for i in range(8):
                n = half * 1024 + 128 * i
                pe.quiet(lambda e, n=n, i=i: e.matmul(bank(bk, 1, o + i), at(acc_o + n, 128), ones[:, 0:1], start=True, stop=False),
                         m, m_cst, *(bfree[bk] if i == 0 else ()))
                p = pe.do(lambda e, n=n, i=i: e.matmul(bank(bk, 1, o + i), A[0:1, adab_o + n:adab_o + n + 128],
                                                       A[0:1, o_cst + CST["ones"][0]:o_cst + CST["ones"][0] + 1],
                                                       start=False, stop=True), m_bias)
            return p

        def ada_row(half, m, m_bias, dst):
            for i in range(2):
                n = half * 1024 + 512 * i
                bk = 2 + i
                pe.quiet(lambda e, n=n, bk=bk: e.matmul(bank(bk), ones, at(acc_o + n, 512), start=True, stop=False),
                         m, m_cst, *bfree[bk])
                p = pe.do(lambda e, n=n, bk=bk: e.matmul(bank(bk), A[0:1, o_cst + CST["ones"][0]:o_cst + CST["ones"][0] + 128],
                                                         A[0:1, adab_o + n:adab_o + n + 512], start=False, stop=True), m_bias)
                r = act.do(lambda e, i=i, bk=bk: e.activation(at(dst + 512 * i, 512), bank(bk), ACT.Copy), p)
                bfree[bk] = [r]
            return p, r

        def scale_shift(bk, o_sh, o_sc, p, wname):
            sh, sc = small(8), small(8)
            m1 = dve.do(lambda e: e.tensor_copy(at(sh, 8), bank(bk, 8, o_sh)), p)
            m2 = dve.do(lambda e: e.scalar_tensor_tensor(out=at(sc, 8), in0=bank(bk, 8, o_sc), scalar=1.0, in1=vec(wname),
                                                         op0=ALU.add, op1=ALU.mult), p, m_vec)
            bfree[bk] = [m2]
            return sh, sc, m2

        scr1 = ohg - 0
        m_xs = rms(x_o, xs_o, [m_x] * 4, (), oatt, ())
        m_acc = ada(0)
        p = ada_cols(0, m_acc, m_ab, 7, 0)
        p = ada_cols(1, m_acc, m_ab, 7, 8)
        sh1, sc1, m_ss1 = scale_shift(7, 0, 8, p, "nmw")
        ada_free[0] = p
        m_hT = turn(xs_o, m_xs, hT, lambda k: at(sc1 + k, 1), lambda k: at(sh1 + k, 1), [m_ss1], (), [0, 1, 2, 3])
        hTk = lambda k: at(hT + 512 * k, 512)
        p_turn = (pe.name, pe.count)

        dbank = [0]

        def next_bank(banks):
            dbank[0] += 1
            return banks[dbank[0] % len(banks)]

        def dense_T(bk, c, j, rhs, marks, nk=8, off=0, release=True):
            for k in range(nk):
                f = lambda e, k=k: e.matmul(bank(bk), c.ap[:, off + k, 128 * j:128 * j + 128], rhs(k),
                                            start=(k == 0), stop=(k == nk - 1))
                mk = [c.mark, marks[k]] + (bfree[bk] if k == 0 else [])
                if k < nk - 1:
                    pe.quiet(f, *mk)
                else:
                    p = pe.do(f, *mk)
            if release:
                c.released = p
            return p

        def dense_tok(bk, c, tc, n, lhs, marks, o=0):
            for k in range(8):
                f = lambda e, k=k: e.matmul(bank(bk, n, o), lhs(k, tc), c.ap[:, k, 0:n], start=(k == 0), stop=(k == 7))
                mk = [c.mark, marks[k]] + (bfree[bk] if k == 0 else [])
                if k < 7:
                    pe.quiet(f, *mk)
                else:
                    p = pe.do(f, *mk)
            c.released = p
            return p

        hT_lhs = lambda k, tc: at(hT + 512 * k + 128 * tc, 128)
        w_in = t["w_in"]
        DB = [0, 1]
        tmp_free = {i: None for i in range(4)}
        ti = [0]

        def tmp_get():
            i = ti[0] % 4
            ti[0] += 1
            return i, tmp + 512 * i

        hg_free = {"QQ": [p_turn], "KK": [p_turn], "TTa": [p_turn], "TTb": [p_turn], "q0": [p_turn], "PT": [p_turn],
                   "V": [p_turn], "sgh": [p_turn]}
        st = {}

        def hg_proj(pr):
            q_m, f_m, k_m = [None] * 2, {}, {}
            c = col_chunk(w_in, 3 + pr)
            for j in range(2):
                bk = next_bank(DB)
                p = dense_T(bk, c, j, hTk, m_hT)
                i, o = tmp_get()
                a = act.do(lambda e, bk=bk, o=o: e.activation(at(o, 512), bank(bk), ACT.Sigmoid), p, tmp_free[i])
                q_m[j] = dve.do(lambda e, bk=bk, o=o, j=j: e.tensor_tensor(at(q0 + 512 * j, 512), at(o, 512), bank(bk), ALU.mult),
                                a, *hg_free["q0"])
                bfree[bk] = [q_m[j]]
                tmp_free[i] = q_m[j]
                yield
            for dr in range(2):
                c = col_chunk(w_in, 5 + 2 * dr + pr)
                for j in range(2):
                    bk = next_bank(DB)
                    p = dense_T(bk, c, j, hTk, m_hT)
                    v = 4 * dr + 2 * pr + j
                    to = TTa + 1024 * (1 - dr) + 512 * j
                    ko = KK + 1024 * dr + 512 * j
                    qo = QQ + 1024 * (1 - dr) + 512 * j
                    a1 = act.do(lambda e, bk=bk, to=to: e.activation(at(to, 512), bank(bk), ACT.Sigmoid), p, *hg_free["TTa"])
                    a2 = act.do(lambda e, bk=bk, ko=ko: e.activation(at(ko, 512), bank(bk), ACT.Sigmoid, scale=-1.0),
                                *hg_free["KK"])
                    bfree[bk] = [a2]
                    b = dve.do(lambda e, to=to, v=v: e.tensor_scalar(at(to, 512), at(to, 512), at(oml + v, 1), at(lbv + v, 1),
                                                                     ALU.mult, ALU.add), a1, m_lb)
                    b = dve.do(lambda e, to=to: e.tensor_scalar(at(to, 512), at(to, 512), 1e-6, None, ALU.max), b)
                    f_m[dr, j] = b
                    k_m[dr, j] = dve.do(lambda e, ko=ko, v=v: e.tensor_scalar(at(ko, 512), at(ko, 512), at(oml + v, 1), None, ALU.mult), a2)
                    st["q1"] = dve.do(lambda e, qo=qo, to=to, j=j: e.tensor_tensor(at(qo, 512), at(q0 + 512 * j, 512), at(to, 512), ALU.mult),
                                      b, q_m[j], *hg_free["QQ"])
                    yield
            c = col_chunk(w_in, 9 + pr)
            for h in range(2):
                bk = next_bank(DB)
                for tc in (2 * h, 2 * h + 1):
                    p = dense_tok(bk, c, tc, 256, hT_lhs, m_hT, 256 * (tc % 2))
                m = act.do(lambda e, bk=bk, h=h: e.activation(at(Vp + 512 * h, 512), bank(bk), ACT.Copy), p, *hg_free["V"])
                bfree[bk] = [m]
                st["v"] = m
                yield
            c = col_chunk(w_in, 11 + pr)
            for j in range(2):
                bk = next_bank(DB)
                p = dense_T(bk, c, j, hTk, m_hT)
                i, o = tmp_get()
                a = act.do(lambda e, bk=bk, o=o: e.activation(at(o, 512), bank(bk), ACT.Sigmoid), p, tmp_free[i])
                m = dve.do(lambda e, bk=bk, o=o, j=j: e.tensor_tensor(at(sgh + 512 * j, 512), at(o, 512), bank(bk), ALU.mult),
                           a, *hg_free["sgh"])
                bfree[bk] = [m]
                tmp_free[i] = m
                st["sgh"] = m
                yield

        HB = [2, 3]

        def level_mask(li):
            return raw(o_cst + CST["lev"][0] + 128 * li, [(0, 4), (1, 128)]).bitcast(mybir.dt.uint32)

        def hg_levels(pr):
            state = st["q1"]
            diag = lambda hh: raw(PT + 2048 * hh, [(640, 4), (1, 128)])
            pt_m = [None] * 2
            for hh in range(2):
                bk = next_bank(HB)
                for c in range(TC):
                    o = 512 * hh + 128 * c
                    pe.quiet(lambda e, bk=bk, c=c, o=o: e.matmul(bank(bk, 128, 128 * c), at(KK + o, 128), at(q0 + o, 128),
                                                                 start=True, stop=False), state, *bfree[bk])
                    p = pe.do(lambda e, bk=bk, c=c, o=o: e.matmul(bank(bk, 128, 128 * c), at(KK + 1024 + o, 128), at(q0 + o, 128),
                                                                  start=False, stop=True))
                pt_m[hh] = act.do(lambda e, bk=bk, hh=hh: e.activation(
                    diag(hh), bank(bk).rearrange("p (c i) -> p c i", c=4), ACT.Copy), p, *hg_free["PT"])
                bfree[bk] = [pt_m[hh]]
            hg_free["q0"] = [p]
            kc = None
            tcur, tnext = TTa, TTb
            tn = 1024
            yield
            for li, h in enumerate(LEVELS + (128, 256)):
                if h <= 64:
                    kc = pool.do(lambda e, h=h: e.tensor_copy(
                        raw(KC, [(h, 2), (2 * h, 512 // h), (1, h)]),
                        raw(KK, [(1024 + h, 2), (2 * h, 512 // h), (1, h)])), state, st.get("kc"))
                    for hh in range(2):
                        bk = next_bank(HB)
                        for c in range(TC):
                            o = 512 * hh + 128 * c
                            dims = [(2 * h, 64 // h), (1024 + h, 2), (1, h)]
                            f = lambda e, bk=bk, c=c, o=o, dims=dims: e.matmul(
                                bank(bk, 128, 128 * c), at(KC + o, 128), raw(QQ + o, dims), start=True, stop=True)
                            if c < 3:
                                pe.quiet(f, kc, *(bfree[bk] if c == 0 else ()))
                            else:
                                p = st["kc"] = pe.do(f, kc)
                        pt_m[hh] = dve.do(lambda e, bk=bk, hh=hh, li=li: e.copy_predicated(
                            diag(hh), level_mask(li),
                            bank(bk).rearrange("p (c i) -> p c i", c=4)), p, pt_m[hh], m_cst)
                        bfree[bk] = [pt_m[hh]]
                elif h == 128:
                    for hh in range(2):
                        bk = next_bank(HB)
                        for c in range(TC):
                            ic = c ^ 1
                            ko = KK + 1024 * (c & 1) + 512 * hh + 128 * c
                            qo = QQ + 1024 * (1 - (c & 1)) + 512 * hh + 128 * ic
                            f = lambda e, bk=bk, c=c, ko=ko, qo=qo: e.matmul(
                                bank(bk, 128, 128 * c), at(ko, 128), at(qo, 128), start=True, stop=True)
                            if c < 3:
                                pe.quiet(f, state, *(bfree[bk] if c == 0 else ()))
                            else:
                                p = pe.do(f, state)
                        for par in range(2):
                            m = act.do(lambda e, bk=bk, hh=hh, par=par: e.activation(
                                raw(PT + 2048 * hh + (128, 512)[par], [(1280, 2), (1, 128)]),
                                raw_ps(bk, 128 * par, [(256, 2), (1, 128)]), ACT.Copy), p, *hg_free["PT"])
                        bfree[bk] = [m]
                else:
                    for hh in range(2):
                        for dr in range(2):
                            bk = next_bank(HB)
                            for n in range(2):
                                c = 2 * dr + n
                                ko = KK + 1024 * dr + 512 * hh + 128 * c
                                qo = QQ + 1024 * (1 - dr) + 512 * hh + 256 * (1 - dr)
                                p = pe.do(lambda e, bk=bk, n=n, ko=ko, qo=qo: e.matmul(
                                    bank(bk, 256, 256 * n), at(ko, 128), at(qo, 256), start=True, stop=True),
                                    state, *(bfree[bk] if n == 0 else ()))
                            m = act.do(lambda e, bk=bk, hh=hh, dr=dr: e.activation(
                                raw(PT + 2048 * hh + 1024 * dr + 256 * (1 - dr), [(512, 2), (1, 256)]),
                                bank(bk).rearrange("p (n i) -> p n i", n=2), ACT.Copy), p, *hg_free["PT"])
                            bfree[bk] = [m]
                        st["pt", hh] = [m, pt_m[hh]]
                    hg_free["QQ"] = hg_free["KK"] = [p]
                if h < 256:
                    nb = 1024 // (2 * h)
                    own = state if h == 1 else st["t"]
                    d1 = dve.do(lambda e, h=h, nb=nb, tcur=tcur, tn=tn: e.tensor_tensor(
                        raw(QQ, [(1024 + h, 2), (2 * h, nb), (1, h)]), raw(QQ, [(1024 + h, 2), (2 * h, nb), (1, h)]),
                        raw(tcur + 1, [(tn - 1, 2), (2, nb), (0, h)]), ALU.mult), p, own, state, kc)
                    d2 = dve.do(lambda e, h=h, nb=nb, tcur=tcur, tn=tn: e.tensor_tensor(
                        raw(KK, [(2 * h, nb), (1, h)]), raw(KK, [(2 * h, nb), (1, h)]),
                        raw(tcur + tn + 1, [(2, nb), (0, h)]), ALU.mult))
                    d3 = dve.do(lambda e, h=h, nb=nb, tcur=tcur, tn=tn: e.tensor_tensor(
                        raw(KK + 1024 + h, [(2 * h, nb), (1, h)]), raw(KK + 1024 + h, [(2 * h, nb), (1, h)]),
                        raw(tcur, [(2, nb), (0, h)]), ALU.mult))
                    state = d3
                    if h < 128:
                        st["t"] = dve.do(lambda e, tcur=tcur, tnext=tnext, tn=tn: e.tensor_tensor(
                            at(tnext, tn), raw(tcur, [(2, tn)]), raw(tcur + 1, [(2, tn)]), ALU.mult), own,
                            *(hg_free["TTb"] if h == 1 else ()))
                        tcur, tnext, tn = tnext, tcur, tn // 2
                    else:
                        hg_free["TTa"] = hg_free["TTb"] = [d3]
                yield

        def raw_ps(bk, o, dims):
            b = PS[:, bk, o:o + 1]
            return bass.AP(b.tensor, b.offset, [b.ap[0]] + [list(d) for d in dims])

        ohg_m = [None] * 4
        hgt = wk.take(1024)
        KC = wk.take(1024)

        def hg_out(pr):
            for hh in range(2):
                bk = next_bank(HB)
                for jc in range(TC):
                    f = lambda e, bk=bk, jc=jc, hh=hh: e.matmul(bank(bk), at(Vp + 256 * jc + 128 * hh, 128),
                                                                at(PT + 2048 * hh + 512 * jc, 512), start=(jc == 0), stop=(jc == 3))
                    if jc < 3:
                        pe.quiet(f, st["v"], *st["pt", hh], *bfree[bk])
                    else:
                        p = pe.do(f)
                hg_free["PT"], hg_free["V"] = [p], [p]
                yield
                o = ohg + 512 * (2 * pr + hh)
                a = act.do(lambda e, bk=bk: e.activation(at(hgt, 512), bank(bk), ACT.Square), p, st.get("hgt"), st.get("hgt2"))
                bk2 = next_bank(HB)
                p2 = pe.do(lambda e, bk2=bk2: e.matmul(bank(bk2), cst("o128"), at(hgt, 512), start=True, stop=True), a, *bfree[bk2])
                a2, b = rsqrt(at(hgt + 512, 512), bank(bk2), "eps6", p2, st.get("hgt"))
                bfree[bk2] = [a2]
                b = dve.do(lambda e, bk=bk, o=o: e.scalar_tensor_tensor(out=at(o, 512), in0=bank(bk), scalar=vcol("hgw", 0),
                                                                        in1=at(hgt + 512, 512), op0=ALU.mult, op1=ALU.mult), b, p)
                bfree[bk] = [b]
                st["hgt"] = b
                st["hgt2"] = p2
                ohg_m[2 * pr + hh] = dve.do(lambda e, o=o, hh=hh: e.tensor_tensor(at(o, 512), at(o, 512), at(sgh + 512 * hh, 512), ALU.mult),
                                            b, st["sgh"])
                hg_free["sgh"] = [ohg_m[2 * pr + hh]]
                yield

        q_marks, kd_marks = [None] * 4, [None] * 2

        def head_norm(bk, p, wcol, put):
            i, o = tmp_get()
            i2, o2 = tmp_get()
            a = act.do(lambda e: e.activation(at(o, 512), bank(bk), ACT.Square), p, tmp_free[i])
            b2 = next_bank(AB)
            p2 = pe.do(lambda e: e.matmul(bank(b2), cst("bo64"), at(o, 512), start=True, stop=True), a, *bfree[b2])
            a2, b = rsqrt(at(o, 512), bank(b2), "eps6", p2)
            bfree[b2] = [a2]
            b = dve.do(lambda e: e.scalar_tensor_tensor(out=at(o2, 512), in0=bank(bk), scalar=wcol, in1=at(o, 512),
                                                        op0=ALU.mult, op1=ALU.mult), b, tmp_free[i2], p)
            bfree[bk] = [b]
            b3 = next_bank(AB)
            p3 = pe.do(lambda e: e.matmul(bank(b3), cst("rot"), at(o2, 512), start=True, stop=True), b, *bfree[b3])
            r = dve.do(lambda e: e.tensor_tensor(at(o, 512), bank(b3), cst("ropes"), ALU.mult), p3)
            bfree[b3] = [r]
            g = pool.do(lambda e: e.tensor_tensor(at(o2, 512), at(o2, 512), cst("ropec"), ALU.mult), b, p3, m_cst)
            m = put(o, o2, r, g)
            tmp_free[i] = tmp_free[i2] = m

        AB = [4, 5]

        def at_proj():
            for n in range(2):
                c = col_chunk(w_in, n)
                for j in range(2):
                    bk = next_bank(DB)
                    p = dense_T(bk, c, j, hTk, m_hT)
                    yield
                    q = 2 * n + j

                    def put(o, o2, r, g, q=q):
                        q_marks[q] = dve.do(lambda e: e.tensor_tensor(at(qT + 512 * q, 512), at(o, 512), at(o2, 512), ALU.add), r, g, p_turn)
                        return q_marks[q]
                    head_norm(bk, p, vcol("qn", 0), put)
                    yield
            c = col_chunk(w_in, 2)
            bk = next_bank(DB)
            p = dense_T(bk, c, 0, hTk, m_hT)

            def put(o, o2, r, g):
                b = dve.do(lambda e: e.tensor_tensor(at(o2, 512), at(o, 512), at(o2, 512), ALU.add), r, g, p_turn)
                for kv in range(2):
                    for half in range(2):
                        m = act.do(lambda e, kv=kv, half=half: e.activation(
                            A[64 * half:64 * half + 64, kd + 512 * kv:kd + 512 * kv + 512],
                            A[64 * kv:64 * kv + 64, o2:o2 + 512], ACT.Copy), b)
                    kd_marks[kv] = m
                return m
            head_norm(bk, p, vcol("kn", 0), put)
            yield
            bk = next_bank(DB)
            for tc in range(TC):
                for k in range(8):
                    f = lambda e, k=k, tc=tc, bk=bk, c=c: e.matmul(bank(bk, 128, 128 * tc), hT_lhs(k, tc), c.ap[:, k, 128:256],
                                                                   start=(k == 0), stop=(k == 7))
                    if k < 7:
                        pe.quiet(f, m_hT[k], *bfree[bk])
                    else:
                        p = pe.do(f, m_hT[k])
            c.released = p
            st["va"] = act.do(lambda e, bk=bk: e.activation(at(va, 512), bank(bk), ACT.Copy), p, p_turn)
            bfree[bk] = [st["va"]]
            yield

        oatt_m = [None] * 4
        ast = small(4 * 8)

        def attention():
            pfree = [None, None]
            ptfree = None
            n = 0
            stn = 0
            for h in range(8):
                g, po = h // 4, 64 * (h % 2)
                pt_done = []
                for ic in range(TC):
                    bk = AB[n % 2]
                    P = Pb + 512 * (n % 2)
                    so = ast + 4 * (stn % 8)
                    stn += 1
                    p = pe.do(lambda e, bk=bk, h=h, g=g, po=po, ic=ic: e.matmul(
                        bank(bk), A[po:po + 64, qT + 512 * (h // 2) + 128 * ic:qT + 512 * (h // 2) + 128 * ic + 128],
                        A[po:po + 64, kd + 512 * g:kd + 512 * g + 512], start=True, stop=True),
                        q_marks[h // 2], kd_marks[g], *bfree[bk])
                    b = dve.do(lambda e, bk=bk, so=so: e.tensor_reduce(at(so, 1), bank(bk), AX, ALU.max), p)
                    b = dve.do(lambda e, so=so: e.tensor_scalar(at(so + 1, 1), at(so, 1), -0.125, None, ALU.mult), b)
                    a = act.do(lambda e, bk=bk, so=so, P=P: e.activation(at(P, 512), bank(bk), ACT.Exp, bias=at(so + 1, 1),
                                                                         scale=0.125, accum_out=at(so + 2, 1)), b, pfree[n % 2])
                    bfree[bk] = [a]
                    b = dve.do(lambda e, so=so: e.reciprocal(at(so + 3, 1), at(so + 2, 1)), a)
                    b = dve.do(lambda e, so=so, P=P: e.tensor_scalar(at(P, 512), at(P, 512), at(so + 3, 1), None, ALU.mult), b)
                    for jc in range(TC):
                        f = lambda e, P=P, jc=jc: e.transpose(bank(6, 128, 128 * jc), at(P + 128 * jc, 128), ident)
                        if jc < 3:
                            pe.quiet(f, b, *bfree[6])
                        else:
                            p = pe.do(f)
                    pfree[n % 2] = p
                    m = act.do(lambda e, ic=ic: e.activation(raw(PTa + 128 * ic, [(512, 4), (1, 128)]),
                                                             bank(6).rearrange("p (j i) -> p j i", j=4), ACT.Copy), p, ptfree)
                    bfree[6] = [m]
                    pt_done.append(m)
                    n += 1
                    yield
                for jc in range(TC):
                    f = lambda e, jc=jc, g=g, po=po: e.matmul(PS[po:po + 64, 7, :], at(va + 128 * jc + 64 * g, 64),
                                                              at(PTa + 512 * jc, 512), start=(jc == 0), stop=(jc == 3))
                    if jc < 3:
                        pe.quiet(f, st["va"], *pt_done, *(bfree[7] if h % 2 == 0 else ()))
                    else:
                        p = pe.do(f)
                ptfree = p
                if h % 2:
                    oatt_m[h // 2] = act.do(lambda e, h=h: e.activation(at(oatt + 512 * (h // 2), 512), bank(7), ACT.Copy), p, *m_xs)
                    bfree[7] = [oatt_m[h // 2]]
                yield

        def weave(*gens):
            gens = list(gens)
            while gens:
                for g in list(gens):
                    try:
                        next(g)
                    except StopIteration:
                        gens.remove(g)

        def seq(*gens):
            for g in gens:
                yield from g

        weave(hg_proj(0))
        weave(seq(hg_levels(0), hg_out(0)), at_proj())
        weave(hg_proj(1))
        weave(seq(hg_levels(1), hg_out(1)), attention())

        mg = QQ
        MBK = [0, 1, 2, 3, 4, 5, 6, 7]
        mg_m = [None] * 8
        mt = [PT + 512 * i for i in range(8)]
        phase_m = [ohg_m[0], ohg_m[1], ohg_m[2], ohg_m[3]] + oatt_m
        hg_end = hg_free["QQ"] + hg_free["PT"] + hg_free["TTa"] + hg_free["q0"]
        c_att = c_hg = None
        for half in range(4):
            c0 = col_chunk(w_in, 13 + half)
            c1 = col_chunk(w_in, 17 + half)
            if half % 2 == 0:
                cols = slice(512 * (half // 2), 512 * (half // 2) + 512)
                c_att = chunk(t["w_branch_att"][:, cols].rearrange("(k p) n -> p k n", p=128), (4, 512))
                c_hg = chunk(t["w_branch_hg"][:, cols].rearrange("(k p) n -> p k n", p=128), (4, 512))
            for j in range(2):
                d = 2 * half + j
                bb = [4 * (d % 2) + i for i in range(4)]
                fr = hg_end if d < 2 else ()
                s0, s1 = mt[4 * (d % 2)], mt[4 * (d % 2) + 1]
                p0 = dense_T(bb[0], c0, j, hTk, m_hT)
                a0 = act.do(lambda e, s0=s0, b=bb[0]: e.activation(at(s0, 512), bank(b), ACT.Sigmoid), p0, *fr, mg_m[d - 2] if d >= 2 else None)
                bfree[bb[0]] = [a0]
                p1 = dense_T(bb[1], c1, j, hTk, m_hT)
                a1 = act.do(lambda e, s1=s1, b=bb[1]: e.activation(at(s1, 512), bank(b), ACT.Sigmoid), p1, mg_m[d - 2] if d >= 2 else None)
                bfree[bb[1]] = [a1]
                jj = 2 * (half % 2) + j
                p2 = dense_T(bb[2], c_att, jj, lambda k: at(oatt + 512 * k, 512), oatt_m, nk=4)
                b2 = dve.do(lambda e, s0=s0, b=bb[2]: e.tensor_tensor(at(s0, 512), at(s0, 512), bank(b), ALU.mult), p2, a0)
                bfree[bb[2]] = [b2]
                p3 = dense_T(bb[3], c_hg, jj, lambda k: at(ohg + 512 * k, 512), ohg_m, nk=4)
                b3 = dve.do(lambda e, s1=s1, b=bb[3]: e.tensor_tensor(at(s1, 512), at(s1, 512), bank(b), ALU.mult), p3, a1)
                bfree[bb[3]] = [b3]
                mg_m[d] = dve.do(lambda e, s0=s0, s1=s1, d=d: e.tensor_tensor(at(mg + 512 * d, 512), at(s0, 512), at(s1, 512), ALU.add),
                                 b2, b3, *fr)

        acc_w = [tmp_free[i] for i in range(4)]
        m_ab = load(act, A[0:1, adab_o:adab_o + 2048], t["ada_b"][:, 2048:4096], "l_ab", *oatt_m, (pe.name, pe.count))
        m_acc = ada(1, *acc_w)
        p, m_g1 = ada_row(0, m_acc, m_ab, gate1_o)
        p = ada_cols(1, m_acc, m_ab, 7, 0)
        ada_free[0] = p
        sh2 = small(8)
        m_sh2 = dve.do(lambda e: e.tensor_copy(at(sh2, 8), bank(7, 8)), p)
        m_ab = load(act, A[0:1, adab_o:adab_o + 2048], t["ada_b"][:, 4096:6144], "l_ab", p)
        m_acc = ada(2)
        bfree[7] = [m_sh2]
        p = ada_cols(0, m_acc, m_ab, 7, 0)
        sc2 = small(8)
        m_sc2 = dve.do(lambda e: e.scalar_tensor_tensor(out=at(sc2, 8), in0=bank(7, 8), scalar=1.0, in1=vec("nfw"),
                                                        op0=ALU.add, op1=ALU.mult), p, m_vec)
        bfree[7] = [m_sc2]
        p_ada, m_g2 = ada_row(1, m_acc, m_ab, gate2_o)

        X = hT
        X = AR - 4096
        m_x2 = None
        res_t = PT

        def residual_out(w, lhs, marks, X, xm, gate, gate_m, tmps, t_free, banks):
            res = list(xm)
            for n in range(4):
                c = col_chunk(w, n)
                for h in range(2):
                    bk = next_bank(banks)
                    for tc in (2 * h, 2 * h + 1):
                        p = dense_tok(bk, c, tc, 256, lhs, marks, 256 * (tc % 2))
                    xa = raw(X + 2048 * h + 256 * n, [(1024, 2), (1, 256)])
                    pv = bank(bk).rearrange("p (a n) -> p a n", a=2)
                    if gate is None:
                        m = dve.do(lambda e, xa=xa, pv=pv: e.tensor_tensor(xa, xa, pv, ALU.add), p, *xm)
                        bfree[bk] = [m]
                    else:
                        i = (2 * n + h) % 2
                        ta = at(tmps + 512 * i, 512).rearrange("p (a n) -> p a n", a=2)
                        b = dve.do(lambda e, ta=ta, pv=pv, n=n: e.tensor_tensor(
                            ta, pv, raw(gate + 256 * n, [(0, 2), (1, 256)]), ALU.mult), p, gate_m, t_free[i])
                        bfree[bk] = [b]
                        m = dve.do(lambda e, xa=xa, ta=ta: e.tensor_tensor(xa, xa, ta, ALU.add), b, *xm)
                        t_free[i] = m
                    res[2 * h] = res[2 * h + 1] = m
            return res

        X = qT
        assert X + 4096 <= oatt
        m_x2 = load(act, at(X, 4096).rearrange("p (c d) -> p c d", c=4), xv, "l_x", *oatt_m, (pe.name, pe.count))
        mg_lhs = lambda k, tc: at(mg + 512 * k + 128 * tc, 128)
        m_X = residual_out(t["w_out"], mg_lhs, mg_m, X, [m_x2] * 4, gate1_o, m_g1, PT, [mg_m[7], mg_m[7]], [0, 1, 2, 3, 4, 5])
        p_wout = (pe.name, pe.count)

        w1 = Work(hT)
        xs2 = w1.take(4096)
        h2T = w1.take(4096)
        assert w1.o <= X
        m_xs2 = rms(X, xs2, m_X, [p_wout], oatt, [p_wout])
        m_h2 = turn(xs2, m_xs2, h2T, lambda k: at(sc2 + k, 1), lambda k: at(sh2 + k, 1), [m_sc2, m_sh2], [p_wout], [0, 1, 2, 3])
        lg, aff, rst = small(64), small(64), small(16)
        for tc in range(TC):
            for k in range(KD):
                f = lambda e, tc=tc, k=k: e.matmul(bank(4, 16, 16 * tc), at(h2T + 512 * k + 128 * tc, 128),
                                                   at(o_vec + VEC["wr"][0] + 16 * k, 16), start=(k == 0), stop=(k == 7))
                if k < 7:
                    pe.quiet(f, m_h2[k], *bfree[4])
                else:
                    p = pe.do(f, m_h2[k])
        p_lg = p
        r3 = lambda o: at(o, 64).rearrange("p (c e) -> p c e", c=4)
        r16 = lambda o: raw(o, [(1, 4), (0, 16)])
        b = dve.do(lambda e: e.tensor_reduce(at(rst, 4), bank(4, 64).rearrange("p (c e) -> p c e", c=4), AX, ALU.max), p)
        b = dve.do(lambda e: e.tensor_tensor(r3(lg), bank(4, 64).rearrange("p (c e) -> p c e", c=4), r16(rst), ALU.subtract), b)
        bfree[4] = [b]
        a = act.do(lambda e: e.activation(at(lg, 64), at(lg, 64), ACT.Exp), b)
        b = dve.do(lambda e: e.tensor_reduce(at(rst + 4, 4), r3(lg), AX, ALU.add), a)
        b = dve.do(lambda e: e.reciprocal(at(rst + 8, 4), at(rst + 4, 4)), b)
        m_aff = dve.do(lambda e: e.tensor_tensor(r3(aff), r3(lg), r16(rst + 8), ALU.mult), b)
        w2 = Work(X + 4096)
        affT, wkT, m8, mskT = w2.take(512), w2.take(512), small(8), small(64)
        for tc in range(TC):
            f = lambda e, tc=tc: e.transpose(PS[0:16, 5, 128 * tc:128 * tc + 128], at(aff + 16 * tc, 16), ident)
            if tc < 3:
                pe.quiet(f, m_aff, *bfree[5], *m_xs2)
            else:
                p = pe.do(f)
        m = dve.do(lambda e: e.tensor_copy(A[0:16, affT:affT + 512], PS[0:16, 5, :]), p, *m_xs2)
        bfree[5] = [m]
        for r in range(CAP // 8):
            src = affT if r % 2 == 0 else wkT
            dst = wkT if r % 2 == 0 else affT
            m = dve.do(lambda e, src=src: e.max(A[0:16, m8:m8 + 8], A[0:16, src:src + 512]), m)
            m = dve.do(lambda e, src=src, dst=dst: e.match_replace(A[0:16, dst:dst + 512], A[0:16, m8:m8 + 8],
                                                                   A[0:16, src:src + 512], -1.0), m)
        m = dve.do(lambda e: e.tensor_scalar(A[0:16, wkT:wkT + 512], A[0:16, affT:affT + 512], 0.0, None, ALU.is_lt), m)
        for tc in range(TC):
            f = lambda e, tc=tc: e.transpose(bank(5, 16, 16 * tc), A[0:16, wkT + 128 * tc:wkT + 128 * tc + 128],
                                             A[0:16, o_cst:o_cst + 16])
            if tc < 3:
                pe.quiet(f, m, *bfree[5])
            else:
                p = pe.do(f)
        m_msk = dve.do(lambda e: e.tensor_copy(at(mskT, 64), bank(5, 64)), p)
        bfree[5] = [m_msk]
        for tc in range(TC):
            for c in range(tc + 1):
                f = lambda e, tc=tc, c=c: e.matmul(bank(4, 16, 16 * tc), tri if c == tc else ones, at(mskT + 16 * c, 16),
                                                   start=(c == 0), stop=(c == tc))
                if c < tc:
                    pe.quiet(f, m_msk, *bfree[4])
                else:
                    p = pe.do(f, m_msk, *bfree[4])
        posf = small(64)
        b = dve.do(lambda e: e.scalar_tensor_tensor(out=at(posf, 64), in0=bank(4, 64), scalar=1.0, in1=at(mskT, 64),
                                                    op0=ALU.add, op1=ALU.mult), p, m_msk)
        bfree[4] = [b]
        m_pos = dve.do(lambda e: e.tensor_scalar(at(posf, 64), at(posf, 64), -1.0, None, ALU.add), b)
        route_end = [m_pos, p]

        w1 = Work(xs2 + 4096)
        sg, hid = w1.take(2048), w1.take(2048)
        assert w1.o <= X
        w2 = Work(X + 4096)
        xeT = [w2.take(512), w2.take(512)]
        hidT = [w2.take(1024), w2.take(1024)]
        YE = w2.take(1024)
        OH = [w2.take(256), w2.take(256)]
        OHW = w2.take(512)
        OHWT = w2.take(512)
        ctmp = [w2.take(512), w2.take(512)]
        while w2.o + W <= AR:
            add_slot(w2.take(W), [p_wout] + [p_lg] + m_xs2 + route_end)
        xe_free, oh_free, hid_free, hidT_free = [None] * 2, [None] * 2, list(route_end), [None] * 2
        ohw_free, ohwt_free, ye_free, ct_free = None, None, None, [None] * 2
        iota = cst("iota")
        sg_free = list(route_end) + m_h2 + [p_lg]
        for ex in range(NE):
            z = ex % 2
            for c in range(TC):
                b = dve.do(lambda e, c=c, ex=ex, z=z: e.tensor_scalar(
                    at(OH[z] + 64 * c, 64), iota, at(posf + 16 * c + ex, 1), None, ALU.is_equal), m_pos, oh_free[z], *route_end)
            for c in range(TC):
                bw = dve.do(lambda e, c=c, ex=ex, z=z: e.tensor_scalar(
                    at(OHW + 128 * c + 64 * z, 64), iota, at(posf + 16 * c + ex, 1), at(aff + 16 * c + ex, 1),
                    ALU.is_equal, ALU.mult), ohw_free)
            for k in range(KD):
                for c in range(TC):
                    f = lambda e, k=k, c=c, z=z: e.matmul(bank(5, 64, 64 * k), at(xs2 + 1024 * c + 128 * k, 128),
                                                          at(OH[z] + 64 * c, 64), start=(c == 0), stop=(c == 3))
                    if (k, c) != (7, 3):
                        pe.quiet(f, b, *bfree[5])
                    else:
                        p = pe.do(f)
            oh_free[z] = p
            xm = []
            for k in range(KD):
                xm.append(act.do(lambda e, k=k, z=z: e.activation(at(xeT[z] + 64 * k, 64), bank(5, 64, 64 * k), ACT.Identity,
                                                                  bias=at(sh2 + k, 1), scale=at(sc2 + k, 1)), p, xe_free[z], *route_end))
            bfree[5] = [xm[-1]]
            for k in range(KD):
                cg = chunk(t["w_exp_gate"][ex, k * 128:(k + 1) * 128, :], (1, 2048))
                cu = chunk(t["w_exp_up"][ex, k * 128:(k + 1) * 128, :], (1, 2048))
                for fb in range(4):
                    for gu, c in ((0, cg), (1, cu)):
                        f = lambda e, gu=gu, c=c, fb=fb, k=k, z=z: e.matmul(
                            PS[64 * gu:64 * gu + 64, fb, :], at(xeT[z] + 64 * k, 64), c.ap[:, 512 * fb:512 * fb + 512],
                            start=(k == 0), stop=(k == 7))
                        if fb == 3:
                            c.released = pe.do(f, c.mark, xm[k], *(bfree[fb] if k == 0 else ()))
                        else:
                            pe.quiet(f, c.mark, xm[k], *(bfree[fb] if k == 0 else ()))
            p = (pe.name, pe.count)
            xe_free[z] = p
            for fb in range(4):
                a = act.do(lambda e, fb=fb: e.activation(A[64:128, sg + 512 * fb:sg + 512 * fb + 512], PS[0:64, fb, :], ACT.Silu),
                           p, *sg_free)
                m = dve.do(lambda e, fb=fb: e.tensor_tensor(
                    A[64:128, hid + 512 * fb:hid + 512 * fb + 512], A[64:128, sg + 512 * fb:sg + 512 * fb + 512],
                    PS[64:128, fb, :], ALU.mult), a, p, *hid_free)
                bfree[fb] = [m]
                bk = 6 + fb % 2
                for q in range(4):
                    f = lambda e, fb=fb, q=q, bk=bk: e.transpose(
                        bank(bk, 64, 64 * q), A[64:128, hid + 512 * fb + 128 * q:hid + 512 * fb + 128 * q + 128],
                        A[64:128, o_cst + 64:o_cst + 128])
                    if q < 3:
                        pe.quiet(f, m, *bfree[bk])
                    else:
                        pt = pe.do(f)
                hm = act.do(lambda e, fb=fb, bk=bk, z=z: e.activation(at(hidT[z] + 256 * fb, 256), bank(bk, 256), ACT.Copy),
                            pt, hidT_free[z], *route_end)
                bfree[bk] = [hm]
            sg_free, hid_free = [m], [pt]
            for n in range(8):
                cd = chunk(t["w_exp_down"][ex, n * 256:(n + 1) * 256, :].rearrange("(k p) n -> p k n", p=128), (2, 1024))
                for k in range(2):
                    for dh in range(2):
                        f = lambda e, n=n, k=k, dh=dh, cd=cd, z=z: e.matmul(
                            PS[64 * dh:64 * dh + 64, 4, :], at(hidT[z] + 64 * (2 * n + k), 64), cd.ap[:, k, 512 * dh:512 * dh + 512],
                            start=(n + k == 0), stop=(n + k == 8))
                        if (k, dh) == (1, 1):
                            p = cd.released = pe.do(f, cd.mark, hm, *bfree[4])
                        else:
                            pe.quiet(f, cd.mark, hm, *bfree[4])
            hidT_free[z] = p
            ym = []
            for dh in range(2):
                f = lambda e, dh=dh, z=z: e.activation(A[64 * z:64 * z + 64, YE + 512 * dh:YE + 512 * dh + 512],
                                                       PS[64 * dh:64 * dh + 64, 4, :], ACT.Copy)
                ym.append(act.do(f, p, ye_free, *route_end))
            bfree[4] = [ym[-1]]
            if z == 1:
                for c in range(TC):
                    f = lambda e, c=c: e.transpose(bank(5, 128, 128 * c), at(OHW + 128 * c, 128), ident)
                    if c < 3:
                        pe.quiet(f, bw, *bfree[5])
                    else:
                        p = pe.do(f)
                ohw_free = p
                m_oht = act.do(lambda e: e.activation(at(OHWT, 512), bank(5), ACT.Copy), p, ohwt_free, *route_end)
                bfree[5] = [m_oht]
                for tc in range(TC):
                    for dh in range(2):
                        bk = 6 + dh
                        p = pe.do(lambda e, tc=tc, dh=dh, bk=bk: e.matmul(
                            bank(bk), at(OHWT + 128 * tc, 128), at(YE + 512 * dh, 512), start=True, stop=True),
                            m_oht, ym[-1], *bfree[bk])
                        b = dve.do(lambda e, dh=dh, bk=bk: e.tensor_tensor(at(ctmp[dh], 512), bank(bk), at(gate2_o + 512 * dh, 512),
                                                                           ALU.mult), p, m_g2, ct_free[dh], *route_end)
                        bfree[bk] = [b]
                        xa = at(X + 1024 * tc + 512 * dh, 512)
                        ct_free[dh] = pool.do(lambda e, xa=xa, dh=dh: e.tensor_tensor(xa, xa, at(ctmp[dh], 512), ALU.add), b, *m_xs2)
                        m_X[tc] = ct_free[dh]
                ohwt_free = ye_free = p
        p_ex = p
        ex_end = [p_ex, m_X[3], ym[-1], (dve.name, dve.count), (act.name, act.count)]

        del slots[NR0:]
        extra = [last_user[s] for s in range(NR0, len(ring_o))]
        extra_m = [c.released for c in extra if c is not None]
        end = ex_end + extra_m
        xnT = xs2
        w1 = Work(xnT + 4096)
        U = w1.take(4 * 542)
        cv = w1.take(2048)
        yT_conv = w1.take(2048)
        tp = w1.take(2048)
        assert w1.o <= X
        w2 = Work(X + 4096)
        psb = w2.take(2048 + 64)
        yT_pool = w2.take(2048)
        gf_o = gate1_o
        m_gf = load(act, at(gf_o, 1024), bass.AP(t["g_final_2"].tensor, t["g_final_2"].offset, [[0, 128], [1, 1024]]), "l_gf", *end)

        xsn = xnT + 4096 - 4096
        xs3 = U
        assert xs3 + 4096 <= tp
        m_xs = rms(X, xs3, m_X, end, tp, end)
        m_xn = turn(xs3, m_xs, xnT, lambda k: vcol("gmix", k), None, [m_vec], end, [0, 1, 2, 3])
        p_t = (pe.name, pe.count)
        xn = lambda k: at(xnT + 512 * k, 512)
        pads = dve.do(lambda e: e.memset(raw(U, [(542, 4), (1, 30)]), 0.0), p_t)
        padp = dve.do(lambda e: e.memset(raw(psb, [(528, 4), (1, 16)]), 0.0), *end)
        u_m = [None] * 4
        tfree = [p_t, p_t, p_t, p_t]
        tn_ = [0]

        def tget():
            i = tn_[0] % 4
            tn_[0] += 1
            return i, tp + 512 * i

        def second_in():
            for n in range(2):
                cg = col_chunk(t["w_in_2"], 2 + n)
                ca = col_chunk(t["w_in_2"], n)
                for j in range(2):
                    ti_ = 2 * n + j
                    bg = next_bank([0, 1, 2, 3])
                    p = dense_T(bg, cg, j, xn, m_xn)
                    i, o = tget()
                    a = act.do(lambda e, bg=bg, o=o, ti_=ti_: e.activation(at(o, 512), bank(bg), ACT.Sigmoid, bias=vcol("bin", 4 + ti_)),
                               p, tfree[i])
                    bfree[bg] = [a]
                    ba = next_bank([0, 1, 2, 3])
                    p = dense_T(ba, ca, j, xn, m_xn)
                    u_m[ti_] = dve.do(lambda e, ba=ba, o=o, ti_=ti_: e.scalar_tensor_tensor(
                        out=at(U + 542 * ti_ + 30, 512), in0=bank(ba), scalar=vcol("bin", ti_), in1=at(o, 512),
                        op0=ALU.add, op1=ALU.mult), p, a, p_t)
                    bfree[ba] = [u_m[ti_]]
                    tfree[i] = u_m[ti_]
                    yield
            for n in range(2):
                c = col_chunk(t["w_in_2"], 4 + n)
                for j in range(2):
                    g = 2 * n + j
                    bk = next_bank([0, 1, 2, 3])
                    p = dense_T(bk, c, j, xn, m_xn)
                    po = psb + 528 * g + 16
                    w = WIN[g]
                    m = act.do(lambda e, bk=bk, po=po, g=g: e.activation(at(po, 512), bank(bk), ACT.Identity, bias=vcol("bin", 8 + g)),
                               p, *end)
                    bfree[bk] = [m]
                    i, o = tget()
                    i2, o2 = tget()
                    src, span = po - 16, 528
                    h = 1
                    cur = src
                    fl = [m, padp, tfree[i], tfree[i2]]
                    nxt = [o, o2]
                    width = 512
                    first = 16
                    dsto = pool_t
                    lead = w - 2
                    n0 = 0
                    cur_o, cur_lead = po, 16
                    while h < w:
                        left = w - 2 * h
                        d_o = dsto[n0 % 2] + 16
                        m = pool.do(lambda e, d_o=d_o, left=left, cur_o=cur_o, h=h: e.tensor_tensor(
                            at(d_o - left, 512 + left), at(cur_o - left, 512 + left), at(cur_o - left - h, 512 + left), ALU.add),
                            m, padp, *pt_free, *end)
                        cur_o = d_o
                        h *= 2
                        n0 += 1
                    b = dve.do(lambda e, cur_o=cur_o, g=g: e.tensor_tensor(at(cur_o, 16), at(cur_o, 16),
                                                                           at(o_cst + CST["popc"][0] + 16 * g, 16), ALU.mult), m)
                    m = dve.do(lambda e, cur_o=cur_o, po=po, w=w: e.scalar_tensor_tensor(
                        out=at(po, 512), in0=at(cur_o, 512), scalar=1.0 / w, in1=at(po, 512), op0=ALU.mult, op1=ALU.subtract), b)
                    pt_free[:] = [m]
                    bk = next_bank([0, 1, 2, 3])
                    p = pe.do(lambda e, bk=bk, g=g, po=po: e.matmul(bank(bk), at(o_vec + VEC["wpool"][0] + 128 * g, 128), at(po, 512),
                                                                    start=True, stop=True), m, *bfree[bk])
                    y_m[4 + g] = act.do(lambda e, bk=bk, g=g: e.activation(at(yT_pool + 512 * g, 512), bank(bk), ACT.Copy,
                                                                           scale=vcol("spool", g)), p, *end)
                    bfree[bk] = [y_m[4 + g]]
                    yield

        pool_t = [w2.take(544), w2.take(544)]
        pt_free = []
        y_m = [None] * 8
        cv_m = [None] * 4

        def conv():
            for i in range(4):
                for k in range(31):
                    wc = at(o_vec + VEC["wdw"][0] + 31 * i + k, 1)
                    u = at(U + 542 * i + k, 512)
                    v = at(cv + 512 * i, 512)
                    if k == 0:
                        m = dve.do(lambda e, u=u, v=v, wc=wc, i=i: e.tensor_scalar(v, u, wc, vcol("bdw", i), ALU.mult, ALU.add),
                                   u_m[i], pads, p_t)
                    else:
                        m = dve.do(lambda e, u=u, v=v, wc=wc: e.scalar_tensor_tensor(out=v, in0=u, scalar=wc, in1=v,
                                                                                     op0=ALU.mult, op1=ALU.add), m)
                cv_m[i] = m
                yield

        weave(second_in())
        weave(conv())
        for i in range(4):
            f = lambda e, i=i: e.matmul(bank(4), cst("o512"), at(cv + 512 * i, 512), start=(i == 0), stop=(i == 3))
            p = pe.do(f, cv_m[i], *bfree[4])
        d_m, s_m = [], []
        for i in range(4):
            d_m.append(dve.do(lambda e, i=i: e.tensor_tensor(at(cv + 512 * i, 512), at(cv + 512 * i, 512), bank(4), ALU.subtract), p))
            s_m.append(act.do(lambda e, i=i: e.activation(at(tp + 512 * i, 512), at(cv + 512 * i, 512), ACT.Square), d_m[i], *tfree, *pt_free))
        bfree[4] = [d_m[-1]]
        for i in range(4):
            p = pe.do(lambda e, i=i: e.matmul(bank(5), cst("o512"), at(tp + 512 * i, 512), start=(i == 0), stop=(i == 3)), s_m[i], *bfree[5])
        rs = U
        a2, m = rsqrt(at(rs, 512), bank(5), "eps5", p, *cv_m)
        bfree[5] = [a2]
        for i in range(4):
            b = dve.do(lambda e, i=i: e.tensor_tensor(at(cv + 512 * i, 512), at(cv + 512 * i, 512), at(rs, 512), ALU.mult), m, s_m[i])
            y_m[i] = act.do(lambda e, i=i: e.activation(at(yT_conv + 512 * i, 512), at(cv + 512 * i, 512), ACT.Silu,
                                                        bias=vcol("lnb", i), scale=vcol("lng", i)), b, p_t)
        y_lhs = lambda k, tc: at((yT_conv + 512 * k if k < 4 else yT_pool + 512 * (k - 4)) + 128 * tc, 128)
        m_X = residual_out(t["w_out_2"], y_lhs, y_m, X, m_X, None, None, None, None, [0, 1, 2, 3, 6, 7])
        p_o2 = (pe.name, pe.count)

        end2 = [p_o2, (act.name, act.count), (dve.name, dve.count)]
        xs4 = X + 4096
        hid_o = xnT + 4096
        scr = xs4 + 4096
        m_xs = rms(X, xs4, m_X, end2, scr, end2)
        m_xn = turn(xs4, m_xs, xnT, lambda k: vcol("gffn", k), None, [m_vec], end2, [0, 1, 2, 3])
        p_t = (pe.name, pe.count)
        assert hid_o + FT * 512 + 2048 <= X
        tq = hid_o + FT * 512
        tqf = [None] * 4
        hm = [None] * FT
        for n in range(FT // 2):
            cg = col_chunk(t["w_gate_2"], n)
            cu = col_chunk(t["w_up_2"], n)
            for j in range(2):
                f_ = 2 * n + j
                o = tq + 512 * (f_ % 4)
                bg = next_bank([0, 1, 2, 3])
                p = dense_T(bg, cg, j, xn, m_xn)
                a = act.do(lambda e, bg=bg, o=o: e.activation(at(o, 512), bank(bg), ACT.Silu), p, tqf[f_ % 4], *end2)
                bfree[bg] = [a]
                bu = next_bank([0, 1, 2, 3])
                p = dense_T(bu, cu, j, xn, m_xn)
                hm[f_] = dve.do(lambda e, bu=bu, o=o, f_=f_: e.tensor_tensor(at(hid_o + 512 * f_, 512), at(o, 512), bank(bu), ALU.mult),
                                p, a, p_t)
                bfree[bu] = [hm[f_]]
                tqf[f_ % 4] = hm[f_]
        for n in range(FT // 2):
            c = chunk(t["w_down_2"][n * 256:(n + 1) * 256, :].rearrange("(k p) n -> p k n", p=128), (2, 1024))
            for k in range(2):
                f_ = 2 * n + k
                for tc in range(TC):
                    for dh in range(2):
                        f = lambda e, c=c, k=k, f_=f_, tc=tc, dh=dh: e.matmul(
                            bank(2 * tc + dh), at(hid_o + 512 * f_ + 128 * tc, 128), c.ap[:, k, 512 * dh:512 * dh + 512],
                            start=(f_ == 0), stop=(f_ == FT - 1))
                        if (k, tc, dh) == (1, 3, 1) or f_ == FT - 1:
                            p = pe.do(f, c.mark, hm[f_], *(bfree[2 * tc + dh] if f_ == 0 else ()))
                            if f_ == FT - 1:
                                st["dn", tc, dh] = p
                        else:
                            pe.quiet(f, c.mark, hm[f_], *(bfree[2 * tc + dh] if f_ == 0 else ()))
            c.released = p
        fin = small(8)
        so = xnT
        ov = out.rearrange("b (c p) d -> p (b c) d", p=128)
        p_last = p
        for tc in range(TC):
            for dh in range(2):
                xa = at(X + 1024 * tc + 512 * dh, 512)
                m = dve.do(lambda e, xa=xa, tc=tc, dh=dh: e.tensor_tensor(xa, xa, bank(2 * tc + dh), ALU.add), st["dn", tc, dh], m_X[tc])
            a = act.do(lambda e, tc=tc: e.activation(at(so + 1024 * tc, 1024), at(X + 1024 * tc, 1024), ACT.Square, scale=1.0 / 32,
                                                     accum_out=at(fin + tc, 1)), m, hm[FT - 1])
            _, b = rsqrt(at(fin + 4 + tc, 1), at(fin + tc, 1), "eps6", a)
            b = dve.do(lambda e, tc=tc: e.scalar_tensor_tensor(out=at(so + 1024 * tc, 1024), in0=at(X + 1024 * tc, 1024),
                                                               scalar=at(fin + 4 + tc, 1), in1=at(gf_o, 1024),
                                                               op0=ALU.mult, op1=ALU.mult), b, m_gf)
            load(act, ov[:, tc, :], at(so + 1024 * tc, 1024), "l_out", b)
        act.wait([("l_out", 64)])

        for c in chunks:
            marks = list(c.first) + ([c.prev.released] if c.prev is not None else [])
            sp.dma(lambda e, c=c: e.dma_start(c.ap, c.src), c.mark[0], c.mark[1], *marks)

        sems = {n: ctx.enter_context(nc.semaphore(n)) for n in
                ["pe", "dve", "act", "pool"] + list(dsems) + [f"r{s}" for s in range(len(ring_o))]}
        block = ctx.enter_context(nc.Block())

        @block.sync
        def _(e):
            sp.emit(e, sems)

        @block.scalar
        def _(e):
            act.emit(e, sems)

        @block.vector
        def _(e):
            dve.emit(e, sems)

        @block.gpsimd
        def _(e):
            pool.emit(e, sems)

        @block.tensor
        def _(e):
            pe.emit(e, sems)


def constants():
    p = np.arange(128)
    c = np.zeros((128, NCST), np.float32)

    def put(n, v):
        c[:, CST[n][0]:CST[n][0] + CST[n][1]] = v
    put("ident", np.eye(128))
    put("ones", 1.0)
    put("tri", p[:, None] < p[None, :])
    put("bo64", (p[:, None] // 64 == p[None, :] // 64) / 64.0)
    rot = np.zeros((128, 128))
    for m in range(128):
        if m % 32 < 16:
            rot[m + 16, m] = -1.0
        else:
            rot[m - 16, m] = 1.0
    put("rot", rot)
    put("o128", 1.0 / 128)
    put("o512", 1.0 / 512)
    put("iota", np.arange(64)[None, :])
    tt = np.arange(16)
    put("popc", np.concatenate([w / np.minimum(tt + 1, w) for w in WIN])[None, :])
    f = np.float32
    inv = (f(10000.0) ** (-np.arange(0, 32, 2, dtype=f) / f(32))).astype(f)
    tok = np.arange(S)
    where = np.stack([(tok // 64).astype(f), (tok % 64).astype(f)])
    d = p % 64
    ang = (where[d // 32] * inv[d % 16][:, None]).astype(f)
    put("ropec", np.cos(ang))
    put("ropes", np.sin(ang))
    put("eps6", 1e-6)
    put("eps5", 1e-5)
    x = p[:, None] ^ p[None, :]
    put("lev", np.concatenate([x >= h for h in LEVELS], 1))
    return c


_BIG = ["ada_w", "w_in", "w_branch_att", "w_branch_hg", "w_out", "w_exp_gate", "w_exp_up", "w_exp_down",
        "w_in_2", "w_out_2", "w_gate_2", "w_up_2", "w_down_2"]


def kernel(**inputs):
    import concourse.bacc as _bacc
    from concourse.bass_utils import run_bass_kernel_spmd as _run

    g = {n: np.ascontiguousarray(v) for n, v in inputs.items()}
    arrays = {"x": g["x"], "ada_b": g["ada_b"], "g_final_2": g["g_final_2"]}
    for n in _BIG:
        arrays[n] = g[n].reshape(g[n].shape[1:])

    def cols(a, k):
        return np.ascontiguousarray(a).reshape(k, 128).T
    parts = {
        "nmw": cols(g["norm_mix_w"], 8), "nfw": cols(g["norm_ffn_w"], 8),
        "qn": np.concatenate([g["q_norm_w"][0]] * 2)[:, None], "kn": np.concatenate([g["k_norm_w"][0]] * 2)[:, None],
        "lb": cols(g["hg_lower_bounds"], 8), "hgw": cols(g["hg_norm_w"], 1), "bin": cols(g["b_in_2"], 12),
        "wdw": g["w_dw_2"][0].T.reshape(4, 128, 31).transpose(1, 0, 2).reshape(128, 124),
        "bdw": cols(g["b_dw_2"], 4), "lng": cols(g["ln_g_2"], 4), "lnb": cols(g["ln_b_2"], 4),
        "spool": cols(g["s_pool_2"], 4), "gmix": cols(g["g_mix_2"], 8), "gffn": cols(g["g_ffn_2"], 8), "c": cols(g["c"], 8),
        "wr": g["w_router"][0].reshape(8, 128, 16).transpose(1, 0, 2).reshape(128, 128),
        "wpool": g["w_pool_2"][0].transpose(1, 0, 2).reshape(128, 512),
    }
    arrays["vec"] = np.ascontiguousarray(np.concatenate([parts[n] for n in VEC], 1))
    arrays["cst"] = constants()

    nc = _bacc.Bacc("TRN2", target_bir_lowering=False, num_devices=1)
    feed, t = {}, {}
    for n, a in arrays.items():
        feed[f"in_{n}"] = a
        t[n] = nc.dram_tensor(f"in_{n}", a.shape, mybir.dt.from_np(a.dtype), kind="ExternalInput").ap()
    out = nc.dram_tensor("out_0", (1, S, D), F32, kind="ExternalOutput").ap()
    build(nc, t, out)
    r = _run(nc, [feed], core_ids=[0])
    return r.results[0]["out_0"]
```

```python
from contextlib import ExitStack

import numpy as np

import concourse.bass as bass
from concourse import mybir

F32 = mybir.dt.float32
F32R = mybir.dt.float32r
ALU = mybir.AluOpType
ACT = mybir.ActivationFunctionType
AX = mybir.AxisListType.X

S, D, TC = 512, 1024, 4
BASE = 16512
KD = D // 128
NE, CAP, FF = 16, 64, 2048
EPS = 1e-6
LEVELS = (1, 2, 4, 8, 16, 32, 64)
WIN = (2, 4, 8, 16)
FT = 22

CST = {}
_o = 0
for _n, _w in (("ident", 128), ("ones", 128), ("tri", 128), ("bo64", 128), ("rot", 128), ("o128", 128),
               ("o512", 128), ("iota", 64), ("popc", 64), ("ropec", 512), ("ropes", 512), ("eps6", 1), ("eps5", 1),
               ("lev", 128 * 7)):
    CST[_n] = (_o, _w)
    _o += _w
NCST = _o
VEC = {}
_o = 0
for _n, _w in (("nmw", 8), ("nfw", 8), ("qn", 1), ("kn", 1), ("lb", 8), ("hgw", 1), ("bin", 12), ("wdw", 124),
               ("bdw", 4), ("lng", 4), ("lnb", 4), ("spool", 4), ("gmix", 8), ("gffn", 8), ("c", 8),
               ("wr", 128), ("wpool", 512)):
    VEC[_n] = (_o, _w)
    _o += _w
NVEC = _o


HEAD = -(-(NCST + NVEC + 900) // 8) * 8 + 2048
W, NR0 = 2048, 6
AR = 52992


class Arena:

    def __init__(self, nc):
        self.parts = []
        for name, start, end in (("stay", 0, HEAD), ("ring", HEAD, HEAD + NR0 * W), ("work", HEAD + NR0 * W, AR)):
            self.parts.append((start, end, nc.alloc_sbuf_tensor_at(name, [128, end - start], F32, offset=BASE + 4 * start)))

    def __getitem__(self, where):
        rows, cols = where
        for start, end, tensor in self.parts:
            if start <= cols.start < end:
                assert cols.stop <= end
                return tensor[rows, cols.start - start:cols.stop - start]


class Queue:

    def __init__(self, name):
        self.name, self.items, self.count, self.seen = name, [], 0, {}

    def wait(self, marks):
        for m in marks:
            if m is not None and self.seen.get(m[0], 0) < m[1]:
                self.seen[m[0]] = m[1]
                self.items.append(("wait", m))

    def do(self, fn, *marks):
        self.wait(marks)
        self.count += 1
        self.items.append(("inc", fn, (self.name, 1)))
        return (self.name, self.count)

    def quiet(self, fn, *marks):
        self.wait(marks)
        self.items.append(("run", fn))

    def dma(self, fn, sem, value, *marks):
        self.wait(marks)
        self.items.append(("inc", fn, (sem, 16)))
        return (sem, value)

    def emit(self, eng, sems):
        for it in self.items:
            if it[0] == "wait":
                eng.wait_ge(sems[it[1][0]], it[1][1])
            elif it[0] == "run":
                it[1](eng)
            else:
                it[1](eng).then_inc(sems[it[2][0]], it[2][1])


def build(nc, t, out):
    with ExitStack() as ctx:
        A = Arena(nc)
        PS = ctx.enter_context(nc.psum_tensor("ps", [128, 8, 512], F32))

        pe, dve, act, pool, sp = (Queue(n) for n in ("pe", "dve", "act", "pool", "sp"))
        dsems = {}

        def load(q, dst, src, sem, *marks):
            dsems[sem] = dsems.get(sem, 0) + 16
            return q.dma(lambda e: e.dma_start(dst, src), sem, dsems[sem], *marks)

        top = [0]

        def take(n):
            o = top[0]
            top[0] += n
            assert top[0] <= AR, top[0]
            return o

        def at(o, n):
            return A[:, o:o + n]

        def part(name, o, n, dtype=F32R):
            return nc.alloc_sbuf_tensor_at(name, [128, n], dtype, offset=BASE + 4 * o)

        def raw(o, dims):
            b = A[:, o:o + 1]
            return bass.AP(b.tensor, b.offset, [b.ap[0]] + [list(d) for d in dims])

        def bank(b, n=512, o=0):
            return PS[:, b, o:o + n]

        o_cst, o_vec = take(NCST), take(NVEC)

        def cst(n):
            return at(o_cst + CST[n][0], CST[n][1])

        def vec(n):
            return at(o_vec + VEC[n][0], VEC[n][1])

        def vcol(n, i):
            return at(o_vec + VEC[n][0] + i, 1)

        ident, ones, tri = cst("ident"), cst("ones"), cst("tri")
        sm = take(900)
        sm_top = [sm]

        def small(n):
            o = sm_top[0]
            sm_top[0] += n
            assert sm_top[0] <= sm + 900
            return o

        take(-top[0] % 8)
        gate1_o, gate2_o = take(1024), take(1024)
        base = top[0]

        assert top[0] == HEAD
        ring_o = [take(W) for _ in range(NR0)]
        work = top[0]
        chunks = []
        pos = [0]
        slots = list(range(NR0))
        last_user = {s: None for s in slots}
        slot_free = {s: () for s in slots}
        uses = {s: 0 for s in slots}

        class Chunk:
            pass

        def chunk(src, shape):
            c = Chunk()
            s = slots[pos[0] % len(slots)]
            pos[0] += 1
            parts = src if isinstance(src, list) else [src]
            uses[s] += len(parts)
            c.slot, c.prev, c.first = s, last_user[s], slot_free[s]
            last_user[s] = c
            c.released = None
            c.mark = (f"r{s}", 16 * uses[s])
            ap = at(ring_o[s], W)
            c.flat = ap
            c.ap = ap.rearrange("p (k n) -> p k n", k=shape[0]) if shape[0] > 1 else ap
            n = shape[0] // len(parts)
            c.parts = [(c.ap if len(parts) == 1 else c.ap[:, n * i:n * i + n, :], v) for i, v in enumerate(parts)]
            chunks.append(c)
            return c

        def add_slot(o, marks):
            s = len(ring_o)
            ring_o.append(o)
            slots.append(s)
            last_user[s], uses[s], slot_free[s] = None, 0, tuple(marks)

        def col_chunk(w, n):
            return chunk(w[:, n * 256:(n + 1) * 256].rearrange("(k p) n -> p k n", p=128), (8, 256))

        m_cst = load(act, at(o_cst, NCST), t["cst"], "l_cst")
        m_vec = load(act, at(o_vec, NVEC), t["vec"], "l_vec")

        def reuse(lst):
            out = []
            for x in lst:
                out += list(x) if isinstance(x, list) else [x]
            return out

        bfree = {b: [] for b in range(8)}

        def split(src, hi, lo, *marks, free=()):
            a = act.do(lambda e: e.activation(hi, src, ACT.Copy), *marks, *free)
            return dve.do(lambda e: e.tensor_tensor(lo, src, hi.bitcast(F32), ALU.subtract), a, *marks, *free)

        class Work:

            def __init__(self, start):
                self.o = start

            def take(self, n):
                o = self.o
                self.o += n
                assert self.o <= AR, self.o
                return o

        wk = Work(work)
        hT = wk.take(4096)
        QQ, KK = wk.take(2048), wk.take(2048)
        TTa, TTb = wk.take(2048), wk.take(1024)
        q0 = wk.take(1024)
        PT = wk.take(4096)
        Vp = wk.take(1024)
        qT = wk.take(2048)
        kd = wk.take(1024)
        va = wk.take(512)
        Pb = wk.take(1536)
        PTa = wk.take(2048)
        oatt = wk.take(2048)
        ohg = wk.take(2048)
        sgh = wk.take(1024)
        tmp = wk.take(2048)
        x_o, xs_o = QQ, PT
        assert PT + 4096 <= qT and QQ + 4096 <= PT
        acc_o, adab_o = tmp, PTa

        xv = t["x"].rearrange("b (c p) d -> p (b c) d", p=128)
        m_x = load(act, at(x_o, 4096).rearrange("p (c d) -> p c d", c=4), xv, "l_x")
        m_ab = load(act, A[0:1, adab_o:adab_o + 2048], t["ada_b"][:, 0:2048], "l_ab")

        csg, cact = small(8), small(8)
        a = act.do(lambda e: e.activation(at(csg, 8), vec("c"), ACT.Sigmoid), m_vec)
        m_c = dve.do(lambda e: e.tensor_tensor(at(cact, 8), at(csg, 8), vec("c"), ALU.mult), a, m_vec)

        lbe, lbr, lbs, lbv, oml = small(8), small(8), small(8), small(8), small(8)
        b = dve.do(lambda e: e.tensor_tensor(at(lbe, 8), vec("lb"), vec("lb"), ALU.subtract), m_vec)
        a = act.do(lambda e: e.activation(at(lbs, 8), at(lbe, 8), ACT.Exp), b)
        b = dve.do(lambda e: e.reciprocal(at(lbr, 8), at(lbs, 8)), a)
        b = dve.do(lambda e: e.tensor_tensor(at(lbs, 8), at(lbs, 8), at(lbr, 8), ALU.mult), b)
        b = dve.do(lambda e: e.tensor_tensor(at(lbv, 8), at(lbs, 8), at(lbs, 8), ALU.subtract), b)
        m_lb = dve.do(lambda e: e.tensor_scalar(at(oml, 8), at(lbv, 8), -1.0, 1.0, ALU.mult, ALU.add), b)

        def rms(x, xs, marks, free, scr, scr_marks):
            st = small(8)
            outm = []
            for c in range(TC):
                a = act.do(lambda e, c=c: e.activation(at(scr + 1024 * (c % 2), 1024), at(x + 1024 * c, 1024), ACT.Square,
                                                       scale=1.0 / 32, accum_out=at(st + c, 1)),
                           marks[c], *(scr_marks if c == 0 else ()))
                _, b = rsqrt(at(st + 4 + c, 1), at(st + c, 1), "eps6", a)
                outm.append(dve.do(lambda e, c=c: e.tensor_scalar(at(xs + 1024 * c, 1024), at(x + 1024 * c, 1024),
                                                                  at(st + 4 + c, 1), None, ALU.mult),
                                   b, *(free if c == 0 else ())))
            return outm

        def rsqrt(dst, src, eps, *marks):
            a = act.do(lambda e: e.activation(dst, src, ACT.Sqrt, bias=cst(eps)), *marks, m_cst)
            return a, dve.do(lambda e: e.reciprocal(dst, dst), a)

        def rsqrt_tile(dst, src, eps, *marks):
            a = act.do(lambda e: e.activation(dst, src, ACT.Ln, bias=cst(eps)), *marks, m_cst)
            return a, act.do(lambda e: e.activation(dst, dst, ACT.Exp, scale=-0.5), a)

        def turn(xs, marks, dst, scale, shift, sc_marks, free, banks):
            outm = []
            for k in range(KD):
                bk = banks[k % len(banks)]
                for c in range(TC):
                    f = lambda e, k=k, c=c, bk=bk: e.transpose(bank(bk, 128, 128 * c), at(xs + 1024 * c + 128 * k, 128), ident)
                    if c < TC - 1:
                        pe.quiet(f, m_cst, marks[c], *(bfree[bk] if c == 0 else ()))
                    else:
                        p = pe.do(f, m_cst, marks[c])
                fr = free if k == 0 else ()
                if k % 2 == 0:
                    m = dve.do(lambda e, k=k, bk=bk: e.tensor_scalar(
                        dst(k), bank(bk), scale(k), shift(k) if shift else None, ALU.mult,
                        *((ALU.add,) if shift else ())), p, *sc_marks, *fr)
                elif shift:
                    m = act.do(lambda e, k=k, bk=bk: e.activation(dst(k), bank(bk), ACT.Identity,
                                                                  bias=shift(k), scale=scale(k)), p, *sc_marks, *free)
                else:
                    m = act.do(lambda e, k=k, bk=bk: e.activation(dst(k), bank(bk), ACT.Copy,
                                                                  scale=scale(k)), p, *sc_marks, *free)
                bfree[bk] = [m]
                outm.append(m)
            return outm

        ada_free = [None]

        ada_m = [None]

        def ada_steps(j, acc_o, *marks):
            for k in range(KD):
                c = chunk(t["ada_w"][k * 128:(k + 1) * 128, j * 2048:(j + 1) * 2048], (1, 2048))
                if k == 0:
                    m = dve.do(lambda e, c=c: e.tensor_scalar(at(acc_o, 2048), c.ap, at(cact, 1), None, ALU.mult),
                               c.mark, m_c, ada_free[0], *marks)
                else:
                    m = dve.do(lambda e, c=c, k=k: e.scalar_tensor_tensor(
                        out=at(acc_o, 2048), in0=c.ap, scalar=at(cact + k, 1), in1=at(acc_o, 2048),
                        op0=ALU.mult, op1=ALU.add), c.mark, m)
                c.released = ada_m[0] = m
                yield

        def ada_cols(acc_o, half, m, m_bias, bk, o):
            for i in range(8):
                n = half * 1024 + 128 * i
                pe.quiet(lambda e, n=n, i=i: e.matmul(bank(bk, 1, o + i), at(acc_o + n, 128), ones[:, 0:1], start=True, stop=False),
                         m, m_cst, *(bfree[bk] if i == 0 else ()))
                p = pe.do(lambda e, n=n, i=i: e.matmul(bank(bk, 1, o + i), A[0:1, adab_o + n:adab_o + n + 128],
                                                       A[0:1, o_cst + CST["ones"][0]:o_cst + CST["ones"][0] + 1],
                                                       start=False, stop=True), m_bias)
            return p

        def ada_row(acc_o, half, m, m_bias, dst):
            for i in range(2):
                n = half * 1024 + 512 * i
                bk = 2 + i
                pe.quiet(lambda e, n=n, bk=bk: e.matmul(bank(bk), ones, at(acc_o + n, 512), start=True, stop=False),
                         m, m_cst, *bfree[bk])
                p = pe.do(lambda e, n=n, bk=bk: e.matmul(bank(bk), A[0:1, o_cst + CST["ones"][0]:o_cst + CST["ones"][0] + 128],
                                                         A[0:1, adab_o + n:adab_o + n + 512], start=False, stop=True), m_bias)
                r = act.do(lambda e, i=i, bk=bk: e.activation(at(dst + 512 * i, 512), bank(bk), ACT.Copy), p)
                bfree[bk] = [r]
            return p, r

        def scale_shift(bk, o_sh, o_sc, p, wname):
            sh, sc = small(8), small(8)
            m1 = dve.do(lambda e: e.tensor_copy(at(sh, 8), bank(bk, 8, o_sh)), p)
            m2 = dve.do(lambda e: e.scalar_tensor_tensor(out=at(sc, 8), in0=bank(bk, 8, o_sc), scalar=1.0, in1=vec(wname),
                                                         op0=ALU.add, op1=ALU.mult), p, m_vec)
            bfree[bk] = [m2]
            return sh, sc, m2

        scr1 = ohg - 0
        m_xs = rms(x_o, xs_o, [m_x] * 4, (), oatt, ())
        for _ in ada_steps(0, acc_o):
            pass
        m_acc = ada_m[0]
        p = ada_cols(acc_o, 0, m_acc, m_ab, 7, 0)
        p = ada_cols(acc_o, 1, m_acc, m_ab, 7, 8)
        sh1, sc1, m_ss1 = scale_shift(7, 0, 8, p, "nmw")
        ada_free[0] = p
        m_hT = turn(xs_o, m_xs, lambda k: at(hT + 512 * k, 512), lambda k: at(sc1 + k, 1), lambda k: at(sh1 + k, 1), [m_ss1], (), [0, 1, 2, 3])
        hTk = lambda k: at(hT + 512 * k, 512)
        p_turn = (pe.name, pe.count)

        dbank = [0]

        def next_bank(banks):
            dbank[0] += 1
            return banks[dbank[0] % len(banks)]

        def dense_T(bk, c, j, rhs, marks, nk=8, off=0, release=True):
            for k in range(nk):
                f = lambda e, k=k: e.matmul(bank(bk), c.ap[:, off + k, 128 * j:128 * j + 128], rhs(k),
                                            start=(k == 0), stop=(k == nk - 1))
                mk = [c.mark, marks[k]] + (bfree[bk] if k == 0 else [])
                if k < nk - 1:
                    pe.quiet(f, *mk)
                else:
                    p = pe.do(f, *mk)
            if release:
                c.released = p
            return p

        def dense_tok(bk, c, tc, n, lhs, marks, o=0):
            for k in range(8):
                f = lambda e, k=k: e.matmul(bank(bk, n, o), lhs(k, tc), c.ap[:, k, 0:n], start=(k == 0), stop=(k == 7))
                mk = [c.mark, marks[k]] + (bfree[bk] if k == 0 else [])
                if k < 7:
                    pe.quiet(f, *mk)
                else:
                    p = pe.do(f, *mk)
            c.released = p
            return p

        hT_lhs = lambda k, tc: at(hT + 512 * k + 128 * tc, 128)
        w_in = t["w_in"]
        DB = [0, 1]
        tmp_free = {i: None for i in range(4)}
        ti = [0]

        def tmp_get():
            i = ti[0] % 4
            ti[0] += 1
            return i, tmp + 512 * i

        hg_free = {"QQ": [p_turn], "KK": [p_turn], "TTa": [p_turn], "TTb": [p_turn], "q0": [p_turn], "PT": [p_turn],
                   "V": [p_turn], "sgh": [p_turn]}
        st = {}

        def hg_proj(pr):
            q_m, f_m, k_m = [None] * 2, {}, {}
            c = col_chunk(w_in, 3 + pr)
            for j in range(2):
                bk = next_bank(DB)
                p = dense_T(bk, c, j, hTk, m_hT)
                i, o = tmp_get()
                a = act.do(lambda e, bk=bk, o=o: e.activation(at(o, 512), bank(bk), ACT.Sigmoid), p, tmp_free[i])
                q_m[j] = dve.do(lambda e, bk=bk, o=o, j=j: e.tensor_tensor(at(q0 + 512 * j, 512), at(o, 512), bank(bk), ALU.mult),
                                a, *hg_free["q0"])
                bfree[bk] = [q_m[j]]
                tmp_free[i] = q_m[j]
                yield
            for dr in range(2):
                c = col_chunk(w_in, 5 + 2 * dr + pr)
                for j in range(2):
                    bk = next_bank(DB)
                    p = dense_T(bk, c, j, hTk, m_hT)
                    v = 4 * dr + 2 * pr + j
                    to = TTa + 1024 * (1 - dr) + 512 * j
                    ko = KK + 1024 * dr + 512 * j
                    qo = QQ + 1024 * (1 - dr) + 512 * j
                    a1 = act.do(lambda e, bk=bk, to=to: e.activation(at(to, 512), bank(bk), ACT.Sigmoid), p, *hg_free["TTa"])
                    a2 = act.do(lambda e, bk=bk, ko=ko: e.activation(at(ko, 512), bank(bk), ACT.Sigmoid, scale=-1.0),
                                *hg_free["KK"])
                    bfree[bk] = [a2]
                    b = dve.do(lambda e, to=to, v=v: e.tensor_scalar(at(to, 512), at(to, 512), at(oml + v, 1), at(lbv + v, 1),
                                                                     ALU.mult, ALU.add), a1, m_lb)
                    b = dve.do(lambda e, to=to: e.tensor_scalar(at(to, 512), at(to, 512), 1e-6, None, ALU.max), b)
                    f_m[dr, j] = b
                    k_m[dr, j] = dve.do(lambda e, ko=ko, v=v: e.tensor_scalar(at(ko, 512), at(ko, 512), at(oml + v, 1), None, ALU.mult), a2)
                    st["q1"] = dve.do(lambda e, qo=qo, to=to, j=j: e.tensor_tensor(at(qo, 512), at(q0 + 512 * j, 512), at(to, 512), ALU.mult),
                                      b, q_m[j], *hg_free["QQ"])
                    yield
            c = col_chunk(w_in, 9 + pr)
            for h in range(2):
                bk = next_bank(DB)
                for tc in (2 * h, 2 * h + 1):
                    p = dense_tok(bk, c, tc, 256, hT_lhs, m_hT, 256 * (tc % 2))
                m = act.do(lambda e, bk=bk, h=h: e.activation(at(Vp + 512 * h, 512), bank(bk), ACT.Copy), p, *hg_free["V"])
                bfree[bk] = [m]
                st["v"] = m
                yield

        def hg_gate(pr):
            c = col_chunk(w_in, 11 + pr)
            for j in range(2):
                bk = next_bank(DB)
                p = dense_T(bk, c, j, hTk, m_hT)
                i, o = tmp_get()
                a = act.do(lambda e, bk=bk, o=o: e.activation(at(o, 512), bank(bk), ACT.Sigmoid), p, tmp_free[i])
                m = dve.do(lambda e, bk=bk, o=o, j=j: e.tensor_tensor(at(sgh + 512 * j, 512), at(o, 512), bank(bk), ALU.mult),
                           a, *hg_free["sgh"])
                bfree[bk] = [m]
                tmp_free[i] = m
                st["sgh"] = m
                yield


        def level_mask(li):
            return raw(o_cst + CST["lev"][0] + 128 * li, [(0, 4), (1, 128)]).bitcast(mybir.dt.uint32)

        def hg_levels(pr, HB):
            state = st["q1"]
            diag = lambda hh: raw(PT + 2048 * hh, [(640, 4), (1, 128)])
            pt_m = [None] * 2
            for hh in range(2):
                bk = next_bank(HB)
                for c in range(TC):
                    o = 512 * hh + 128 * c
                    pe.quiet(lambda e, bk=bk, c=c, o=o: e.matmul(bank(bk, 128, 128 * c), at(KK + o, 128), at(q0 + o, 128),
                                                                 start=True, stop=False), state, *bfree[bk])
                    p = pe.do(lambda e, bk=bk, c=c, o=o: e.matmul(bank(bk, 128, 128 * c), at(KK + 1024 + o, 128), at(q0 + o, 128),
                                                                  start=False, stop=True))
                pt_m[hh] = act.do(lambda e, bk=bk, hh=hh: e.activation(
                    diag(hh), bank(bk).rearrange("p (c i) -> p c i", c=4), ACT.Copy), p, *hg_free["PT"])
                bfree[bk] = [pt_m[hh]]
            hg_free["q0"] = [p]
            pm, kc = [None] * 2, None
            tcur, tnext = TTa, TTb
            tn = 1024
            yield
            for li, h in enumerate(LEVELS + (128, 256)):
                if h <= 64:
                    kc = act.do(lambda e, h=h: e.activation(
                        raw(KC, [(h, 2), (2 * h, 512 // h), (1, h)]),
                        raw(KK, [(1024 + h, 2), (2 * h, 512 // h), (1, h)]), ACT.Copy), state, st.get("kc"))
                    bks = []
                    for hh in range(2):
                        bk = next_bank(HB)
                        bks.append((hh, bk))
                        for c in range(TC):
                            o = 512 * hh + 128 * c
                            dims = [(2 * h, 64 // h), (1024 + h, 2), (1, h)]
                            f = lambda e, bk=bk, c=c, o=o, dims=dims: e.matmul(
                                bank(bk, 128, 128 * c), at(KC + o, 128), raw(QQ + o, dims), start=True, stop=True)
                            if c < 3:
                                pe.quiet(f, kc, *(bfree[bk] if c == 0 else ()))
                            else:
                                p = st["kc"] = pe.do(f)
                        pm[hh] = p
                elif h == 128:
                    for hh in range(2):
                        bk = next_bank(HB)
                        for c in range(TC):
                            ic = c ^ 1
                            ko = KK + 1024 * (c & 1) + 512 * hh + 128 * c
                            qo = QQ + 1024 * (1 - (c & 1)) + 512 * hh + 128 * ic
                            f = lambda e, bk=bk, c=c, ko=ko, qo=qo: e.matmul(
                                bank(bk, 128, 128 * c), at(ko, 128), at(qo, 128), start=True, stop=True)
                            if c < 3:
                                pe.quiet(f, state, *(bfree[bk] if c == 0 else ()))
                            else:
                                p = pe.do(f, state)
                        for par in range(2):
                            m = act.do(lambda e, bk=bk, hh=hh, par=par: e.activation(
                                raw(PT + 2048 * hh + (128, 512)[par], [(1280, 2), (1, 128)]),
                                raw_ps(bk, 128 * par, [(256, 2), (1, 128)]), ACT.Copy), p, *hg_free["PT"])
                        bfree[bk] = [m]
                else:
                    for hh in range(2):
                        for dr in range(2):
                            bk = next_bank(HB)
                            for n in range(2):
                                c = 2 * dr + n
                                ko = KK + 1024 * dr + 512 * hh + 128 * c
                                qo = QQ + 1024 * (1 - dr) + 512 * hh + 256 * (1 - dr)
                                p = pe.do(lambda e, bk=bk, n=n, ko=ko, qo=qo: e.matmul(
                                    bank(bk, 256, 256 * n), at(ko, 128), at(qo, 256), start=True, stop=True),
                                    state, *(bfree[bk] if n == 0 else ()))
                            m = act.do(lambda e, bk=bk, hh=hh, dr=dr: e.activation(
                                raw(PT + 2048 * hh + 1024 * dr + 256 * (1 - dr), [(512, 2), (1, 256)]),
                                bank(bk).rearrange("p (n i) -> p n i", n=2), ACT.Copy), p, *hg_free["PT"])
                            bfree[bk] = [m]
                        st["pt", hh] = [m, pt_m[hh]]
                    hg_free["QQ"] = hg_free["KK"] = [p]
                if h < 256:
                    nb = 1024 // (2 * h)
                    own = state if h == 1 else st["t"]
                    d1 = dve.do(lambda e, h=h, nb=nb, tcur=tcur, tn=tn: e.tensor_tensor(
                        raw(QQ, [(1024 + h, 2), (2 * h, nb), (1, h)]), raw(QQ, [(1024 + h, 2), (2 * h, nb), (1, h)]),
                        raw(tcur + 1, [(tn - 1, 2), (2, nb), (0, h)]), ALU.mult), p, own, state, kc)
                    d2 = dve.do(lambda e, h=h, nb=nb, tcur=tcur, tn=tn: e.tensor_tensor(
                        raw(KK, [(2 * h, nb), (1, h)]), raw(KK, [(2 * h, nb), (1, h)]),
                        raw(tcur + tn + 1, [(2, nb), (0, h)]), ALU.mult))
                    d3 = dve.do(lambda e, h=h, nb=nb, tcur=tcur, tn=tn: e.tensor_tensor(
                        raw(KK + 1024 + h, [(2 * h, nb), (1, h)]), raw(KK + 1024 + h, [(2 * h, nb), (1, h)]),
                        raw(tcur, [(2, nb), (0, h)]), ALU.mult))
                    state = d3
                    if h < 128:
                        st["t"] = dve.do(lambda e, tcur=tcur, tnext=tnext, tn=tn: e.tensor_tensor(
                            at(tnext, tn), raw(tcur, [(2, tn)]), raw(tcur + 1, [(2, tn)]), ALU.mult), own,
                            *(hg_free["TTb"] if h == 1 else ()))
                        tcur, tnext, tn = tnext, tcur, tn // 2
                    else:
                        hg_free["TTa"] = hg_free["TTb"] = [d3]
                if h <= 64:
                    for hh, bk in bks:
                        pt_m[hh] = dve.do(lambda e, bk=bk, hh=hh, li=li: e.copy_predicated(
                            diag(hh), level_mask(li),
                            bank(bk).rearrange("p (c i) -> p c i", c=4)), pm[hh], pt_m[hh], m_cst)
                        bfree[bk] = [pt_m[hh]]
                yield

        def raw_ps(bk, o, dims):
            b = PS[:, bk, o:o + 1]
            return bass.AP(b.tensor, b.offset, [b.ap[0]] + [list(d) for d in dims])

        ohg_m = [None] * 4
        hgt = wk.take(1024)
        KC = wk.take(1024)

        def hg_out(pr, HB):
            for hh in range(2):
                bk, bk2 = next_bank(HB), next_bank(HB)
                for jc in range(TC):
                    f = lambda e, bk=bk, jc=jc, hh=hh: e.matmul(bank(bk), at(Vp + 256 * jc + 128 * hh, 128),
                                                                at(PT + 2048 * hh + 512 * jc, 512), start=(jc == 0), stop=(jc == 3))
                    if jc < 3:
                        pe.quiet(f, st["v"], *st["pt", hh], *bfree[bk])
                    else:
                        p = pe.do(f)
                hg_free["PT"], hg_free["V"] = [p], [p]
                yield
                o = ohg + 512 * (2 * pr + hh)
                a = act.do(lambda e, bk=bk: e.activation(at(hgt, 512), bank(bk), ACT.Square), p, st.get("hgt"), st.get("hgt2"))
                p2 = pe.do(lambda e, bk2=bk2: e.matmul(bank(bk2), cst("o128"), at(hgt, 512), start=True, stop=True), a, *bfree[bk2])
                a2, b = rsqrt_tile(at(hgt + 512, 512), bank(bk2), "eps6", p2, st.get("hgt"))
                bfree[bk2] = [a2]
                b = dve.do(lambda e, bk=bk, o=o: e.scalar_tensor_tensor(out=at(o, 512), in0=bank(bk), scalar=vcol("hgw", 0),
                                                                        in1=at(hgt + 512, 512), op0=ALU.mult, op1=ALU.mult), b, p)
                bfree[bk] = [b]
                st["hgt"] = b
                st["hgt2"] = p2
                ohg_m[2 * pr + hh] = dve.do(lambda e, o=o, hh=hh: e.tensor_tensor(at(o, 512), at(o, 512), at(sgh + 512 * hh, 512), ALU.mult),
                                            b, st["sgh"])
                hg_free["sgh"] = [ohg_m[2 * pr + hh]]
                yield

        q_marks, kd_marks = [None] * 4, [None] * 2

        def head_norm(bk, p, wcol, put):
            i, o = tmp_get()
            i2, o2 = tmp_get()
            a = act.do(lambda e: e.activation(at(o, 512), bank(bk), ACT.Square), p, tmp_free[i])
            b2 = next_bank(AB)
            p2 = pe.do(lambda e: e.matmul(bank(b2), cst("bo64"), at(o, 512), start=True, stop=True), a, *bfree[b2])
            a2, b = rsqrt_tile(at(o, 512), bank(b2), "eps6", p2)
            bfree[b2] = [a2]
            b = dve.do(lambda e: e.scalar_tensor_tensor(out=at(o2, 512), in0=bank(bk), scalar=wcol, in1=at(o, 512),
                                                        op0=ALU.mult, op1=ALU.mult), b, tmp_free[i2], p)
            bfree[bk] = [b]
            b3 = next_bank(AB)
            p3 = pe.do(lambda e: e.matmul(bank(b3), cst("rot"), at(o2, 512), start=True, stop=True), b, *bfree[b3])
            r = dve.do(lambda e: e.tensor_tensor(at(o, 512), bank(b3), cst("ropes"), ALU.mult), p3)
            bfree[b3] = [r]
            g = pool.do(lambda e: e.tensor_tensor(at(o2, 512), at(o2, 512), cst("ropec"), ALU.mult), b, p3, m_cst)
            m = put(o, o2, r, g)
            tmp_free[i] = tmp_free[i2] = m

        AB = [4, 5]

        def at_proj():
            for n in range(2):
                c = col_chunk(w_in, n)
                for j in range(2):
                    bk = next_bank(DB)
                    p = dense_T(bk, c, j, hTk, m_hT)
                    yield
                    q = 2 * n + j

                    def put(o, o2, r, g, q=q):
                        q_marks[q] = dve.do(lambda e: e.tensor_tensor(at(qT + 512 * q, 512), at(o, 512), at(o2, 512), ALU.add), r, g, p_turn)
                        return q_marks[q]
                    head_norm(bk, p, vcol("qn", 0), put)
                    yield
            c = col_chunk(w_in, 2)
            bk = next_bank(DB)
            p = dense_T(bk, c, 0, hTk, m_hT)

            def put(o, o2, r, g):
                b = dve.do(lambda e: e.tensor_tensor(at(o2, 512), at(o, 512), at(o2, 512), ALU.add), r, g, p_turn)
                for kv in range(2):
                    for half in range(2):
                        m = act.do(lambda e, kv=kv, half=half: e.activation(
                            A[64 * half:64 * half + 64, kd + 512 * kv:kd + 512 * kv + 512],
                            A[64 * kv:64 * kv + 64, o2:o2 + 512], ACT.Copy), b)
                    kd_marks[kv] = m
                return m
            head_norm(bk, p, vcol("kn", 0), put)
            yield
            bk = next_bank(DB)
            for tc in range(TC):
                for k in range(8):
                    f = lambda e, k=k, tc=tc, bk=bk, c=c: e.matmul(bank(bk, 128, 128 * tc), hT_lhs(k, tc), c.ap[:, k, 128:256],
                                                                   start=(k == 0), stop=(k == 7))
                    if k < 7:
                        pe.quiet(f, m_hT[k], *bfree[bk])
                    else:
                        p = pe.do(f, m_hT[k])
            c.released = p
            st["va"] = act.do(lambda e, bk=bk: e.activation(at(va, 512), bank(bk), ACT.Copy), p, p_turn)
            bfree[bk] = [st["va"]]
            yield

        oatt_m = [None] * 4
        ast = small(4 * 8)

        def attention():
            pfree = [None] * 3
            SB = [3, 4, 5]
            ptfree = None
            steps = [(h, ic) for h in range(8) for ic in range(TC)]
            ready = {}
            pt_done = []

            def scores(n):
                h, ic = steps[n]
                g, po = h // 4, 64 * (h % 2)
                bk, P, so = SB[n % 3], Pb + 512 * (n % 3), ast + 4 * (n % 8)
                qo = qT + 512 * (h // 2) + 128 * ic
                p = pe.do(lambda e: e.matmul(bank(bk), A[po:po + 64, qo:qo + 128], A[po:po + 64, kd + 512 * g:kd + 512 * g + 512],
                                             start=True, stop=True), q_marks[h // 2], kd_marks[g], *bfree[bk])
                b = dve.do(lambda e: e.tensor_reduce(at(so, 1), bank(bk), AX, ALU.max), p)
                b = dve.do(lambda e: e.tensor_scalar(at(so + 1, 1), at(so, 1), -0.125, None, ALU.mult), b)
                a = act.do(lambda e: e.activation(at(P, 512), bank(bk), ACT.Exp, bias=at(so + 1, 1), scale=0.125,
                                                  accum_out=at(so + 2, 1)), b, pfree[n % 3])
                bfree[bk] = [a]
                b = dve.do(lambda e: e.reciprocal(at(so + 3, 1), at(so + 2, 1)), a)
                ready[n] = dve.do(lambda e: e.tensor_scalar(at(P, 512), at(P, 512), at(so + 3, 1), None, ALU.mult), b)

            scores(0)
            yield
            scores(1)
            yield
            for n, (h, ic) in enumerate(steps):
                g, po = h // 4, 64 * (h % 2)
                if n + 2 < len(steps):
                    scores(n + 2)
                    yield
                P = Pb + 512 * (n % 3)
                for jc in range(TC):
                    f = lambda e, P=P, jc=jc: e.transpose(bank(6, 128, 128 * jc), at(P + 128 * jc, 128), ident)
                    if jc < 3:
                        pe.quiet(f, ready[n], *bfree[6])
                    else:
                        p = pe.do(f)
                pfree[n % 3] = p
                m = act.do(lambda e, ic=ic: e.activation(raw(PTa + 128 * ic, [(512, 4), (1, 128)]),
                                                         bank(6).rearrange("p (j i) -> p j i", j=4), ACT.Copy), p, ptfree)
                bfree[6] = [m]
                pt_done.append(m)
                if ic < TC - 1:
                    continue
                yield
                for jc in range(TC):
                    f = lambda e, jc=jc, g=g, po=po: e.matmul(PS[po:po + 64, 7, :], at(va + 128 * jc + 64 * g, 64),
                                                              at(PTa + 512 * jc, 512), start=(jc == 0), stop=(jc == 3))
                    if jc < 3:
                        pe.quiet(f, st["va"], *pt_done, *(bfree[7] if h % 2 == 0 else ()))
                    else:
                        p = pe.do(f)
                ptfree = p
                pt_done = []
                if h % 2:
                    oatt_m[h // 2] = act.do(lambda e, h=h: e.activation(at(oatt + 512 * (h // 2), 512), bank(7), ACT.Copy), p, *m_xs)
                    bfree[7] = [oatt_m[h // 2]]

        def weave(*gens, until=None):
            gens = [g if isinstance(g, tuple) else (g, 1) for g in gens]
            while gens:
                for g in list(gens):
                    for _ in range(g[1]):
                        try:
                            next(g[0])
                        except StopIteration:
                            gens.remove(g)
                            if g[0] is until:
                                return
                            break

        def seq(*gens):
            for g in gens:
                yield from g

        weave(hg_proj(0))
        weave(seq(hg_levels(0, [2, 3, 6, 7]), hg_out(0, [2, 3, 6, 7])), seq(hg_gate(0), at_proj()))
        att, hg = attention(), hg_proj(1)
        weave(hg, (att, 2), until=hg)
        weave(seq(hg_levels(1, [0, 1, 2]), hg_out(1, [0, 1, 2])), (att, 2), seq(hg_gate(1)))

        mg = QQ
        MBK = [0, 1, 2, 3, 4, 5, 6, 7]
        mg_m = [None] * 8
        mt = [PT + 512 * i for i in range(8)]
        phase_m = [ohg_m[0], ohg_m[1], ohg_m[2], ohg_m[3]] + oatt_m
        hg_end = hg_free["QQ"] + hg_free["PT"] + hg_free["TTa"] + hg_free["q0"]
        acc2 = TTa
        m_ab = load(act, A[0:1, adab_o:adab_o + 2048], t["ada_b"][:, 2048:4096], "l_ab", *oatt_m, (pe.name, pe.count))
        sh2, sc2 = small(8), small(8)
        gen = ada_steps(1, acc2, *hg_end)
        for half in range(4):
            c0 = col_chunk(w_in, 13 + half)
            c1 = col_chunk(w_in, 17 + half)
            cols = slice(256 * half, 256 * half + 256)
            cb = chunk([t[n][:, cols].rearrange("(k p) n -> p k n", p=128) for n in ("w_branch_att", "w_branch_hg")], (8, 256))
            for j in range(2):
                d = 2 * half + j
                bb = [4 * (d % 2) + i for i in range(4)]
                fr = hg_end if d < 2 else ()
                s0, s1 = mt[4 * (d % 2)], mt[4 * (d % 2) + 1]
                p0 = dense_T(bb[0], c0, j, hTk, m_hT)
                a0 = act.do(lambda e, s0=s0, b=bb[0]: e.activation(at(s0, 512), bank(b), ACT.Sigmoid), p0, *fr, mg_m[d - 2] if d >= 2 else None)
                bfree[bb[0]] = [a0]
                p1 = dense_T(bb[1], c1, j, hTk, m_hT)
                a1 = act.do(lambda e, s1=s1, b=bb[1]: e.activation(at(s1, 512), bank(b), ACT.Sigmoid), p1, mg_m[d - 2] if d >= 2 else None)
                bfree[bb[1]] = [a1]
                p2 = dense_T(bb[2], cb, j, lambda k: at(oatt + 512 * k, 512), oatt_m, nk=4)
                b2 = dve.do(lambda e, s0=s0, b=bb[2]: e.tensor_tensor(at(s0, 512), at(s0, 512), bank(b), ALU.mult), p2, a0)
                bfree[bb[2]] = [b2]
                p3 = dense_T(bb[3], cb, j, lambda k: at(ohg + 512 * k, 512), ohg_m, nk=4, off=4)
                b3 = dve.do(lambda e, s1=s1, b=bb[3]: e.tensor_tensor(at(s1, 512), at(s1, 512), bank(b), ALU.mult), p3, a1)
                bfree[bb[3]] = [b3]
                mg_m[d] = dve.do(lambda e, s0=s0, s1=s1, d=d: e.tensor_tensor(at(mg + 512 * d, 512), at(s0, 512), at(s1, 512), ALU.add),
                                 b2, b3, *fr)
                next(gen)
                next(gen)
            if half == 1:
                p, m_g1 = ada_row(acc2, 0, ada_m[0], m_ab, gate1_o)
                p = ada_cols(acc2, 1, ada_m[0], m_ab, 7, 0)
                ada_free[0] = p
                m_sh2 = dve.do(lambda e: e.tensor_copy(at(sh2, 8), bank(7, 8)), p)
                bfree[7] = [m_sh2]
                m_ab = load(act, A[0:1, adab_o:adab_o + 2048], t["ada_b"][:, 4096:6144], "l_ab", p)
                gen = ada_steps(2, acc2)
            if half == 3:
                p = ada_cols(acc2, 0, ada_m[0], m_ab, 7, 0)
                m_sc2 = dve.do(lambda e: e.scalar_tensor_tensor(out=at(sc2, 8), in0=bank(7, 8), scalar=1.0, in1=vec("nfw"),
                                                                op0=ALU.add, op1=ALU.mult), p, m_vec)
                bfree[7] = [m_sc2]
                p_ada, m_g2 = ada_row(acc2, 1, ada_m[0], m_ab, gate2_o)

        p_branch = (pe.name, pe.count)
        X = hT
        X = AR - 4096
        m_x2 = None
        res_t = PT

        def residual_out(w, lhs, marks, X, xm, gate, gate_m, tmps, t_free, banks):
            res = list(xm)
            for n in range(4):
                c = col_chunk(w, n)
                for h in range(2):
                    bk = next_bank(banks)
                    for tc in (2 * h, 2 * h + 1):
                        p = dense_tok(bk, c, tc, 256, lhs, marks, 256 * (tc % 2))
                    xa = raw(X + 2048 * h + 256 * n, [(1024, 2), (1, 256)])
                    pv = bank(bk).rearrange("p (a n) -> p a n", a=2)
                    if gate is None:
                        m = dve.do(lambda e, xa=xa, pv=pv: e.tensor_tensor(xa, xa, pv, ALU.add), p, *xm)
                        bfree[bk] = [m]
                    else:
                        i = (2 * n + h) % 2
                        ta = at(tmps + 512 * i, 512).rearrange("p (a n) -> p a n", a=2)
                        b = dve.do(lambda e, ta=ta, pv=pv, n=n: e.tensor_tensor(
                            ta, pv, raw(gate + 256 * n, [(0, 2), (1, 256)]), ALU.mult), p, gate_m, t_free[i])
                        bfree[bk] = [b]
                        m = dve.do(lambda e, xa=xa, ta=ta: e.tensor_tensor(xa, xa, ta, ALU.add), b, *xm)
                        t_free[i] = m
                    res[2 * h] = res[2 * h + 1] = m
            return res

        X = qT
        assert X + 4096 <= oatt
        m_x2 = load(act, at(X, 4096).rearrange("p (c d) -> p c d", c=4), xv, "l_x", *oatt_m, (pe.name, pe.count))
        mg_lhs = lambda k, tc: at(mg + 512 * k + 128 * tc, 128)
        m_X = residual_out(t["w_out"], mg_lhs, mg_m, X, [m_x2] * 4, gate1_o, m_g1, PT, [mg_m[7], mg_m[7]], [0, 1, 2, 3, 4, 5])
        p_wout = (pe.name, pe.count)

        w1 = Work(hT)
        xs2 = w1.take(4096)
        h2T = w1.take(4096)
        assert w1.o <= X
        m_xs2 = rms(X, xs2, m_X, [p_wout], oatt, [p_wout])
        m_h2 = turn(xs2, m_xs2, lambda k: at(h2T + 512 * k, 512), lambda k: at(sc2 + k, 1), lambda k: at(sh2 + k, 1), [m_sc2, m_sh2], [p_wout], [0, 1, 2, 3])
        lg, aff, rst = small(64), small(64), small(16)
        for tc in range(TC):
            for k in range(KD):
                f = lambda e, tc=tc, k=k: e.matmul(bank(4, 16, 16 * tc), at(h2T + 512 * k + 128 * tc, 128),
                                                   at(o_vec + VEC["wr"][0] + 16 * k, 16), start=(k == 0), stop=(k == 7))
                if k < 7:
                    pe.quiet(f, m_h2[k], *bfree[4])
                else:
                    p = pe.do(f, m_h2[k])
        p_lg = p
        r3 = lambda o: at(o, 64).rearrange("p (c e) -> p c e", c=4)
        r16 = lambda o: raw(o, [(1, 4), (0, 16)])
        b = dve.do(lambda e: e.tensor_reduce(at(rst, 4), bank(4, 64).rearrange("p (c e) -> p c e", c=4), AX, ALU.max), p)
        b = dve.do(lambda e: e.tensor_tensor(r3(lg), bank(4, 64).rearrange("p (c e) -> p c e", c=4), r16(rst), ALU.subtract), b)
        bfree[4] = [b]
        a = act.do(lambda e: e.activation(at(lg, 64), at(lg, 64), ACT.Exp), b)
        b = dve.do(lambda e: e.tensor_reduce(at(rst + 4, 4), r3(lg), AX, ALU.add), a)
        b = dve.do(lambda e: e.reciprocal(at(rst + 8, 4), at(rst + 4, 4)), b)
        m_aff = dve.do(lambda e: e.tensor_tensor(r3(aff), r3(lg), r16(rst + 8), ALU.mult), b)
        w2 = Work(X + 4096)
        affT, wkT, m8, mskT = w2.take(512), w2.take(512), small(8), small(64)
        for tc in range(TC):
            f = lambda e, tc=tc: e.transpose(PS[0:16, 5, 128 * tc:128 * tc + 128], at(aff + 16 * tc, 16), ident)
            if tc < 3:
                pe.quiet(f, m_aff, *bfree[5], *m_xs2)
            else:
                p = pe.do(f)
        m = dve.do(lambda e: e.tensor_copy(A[0:16, affT:affT + 512], PS[0:16, 5, :]), p, *m_xs2)
        bfree[5] = [m]
        for r in range(CAP // 8):
            src = affT if r % 2 == 0 else wkT
            dst = wkT if r % 2 == 0 else affT
            m = dve.do(lambda e, src=src: e.max(A[0:16, m8:m8 + 8], A[0:16, src:src + 512]), m)
            m = dve.do(lambda e, src=src, dst=dst: e.match_replace(A[0:16, dst:dst + 512], A[0:16, m8:m8 + 8],
                                                                   A[0:16, src:src + 512], -1.0), m)
        m = dve.do(lambda e: e.tensor_scalar(A[0:16, wkT:wkT + 512], A[0:16, affT:affT + 512], 0.0, None, ALU.is_lt), m)
        for tc in range(TC):
            f = lambda e, tc=tc: e.transpose(bank(5, 16, 16 * tc), A[0:16, wkT + 128 * tc:wkT + 128 * tc + 128],
                                             A[0:16, o_cst:o_cst + 16])
            if tc < 3:
                pe.quiet(f, m, *bfree[5])
            else:
                p = pe.do(f)
        m_msk = dve.do(lambda e: e.tensor_copy(at(mskT, 64), bank(5, 64)), p)
        bfree[5] = [m_msk]
        for tc in range(TC):
            for c in range(tc + 1):
                f = lambda e, tc=tc, c=c: e.matmul(bank(4, 16, 16 * tc), tri if c == tc else ones, at(mskT + 16 * c, 16),
                                                   start=(c == 0), stop=(c == tc))
                if c < tc:
                    pe.quiet(f, m_msk, *bfree[4])
                else:
                    p = pe.do(f, m_msk, *bfree[4])
        posf = small(64)
        b = dve.do(lambda e: e.scalar_tensor_tensor(out=at(posf, 64), in0=bank(4, 64), scalar=1.0, in1=at(mskT, 64),
                                                    op0=ALU.add, op1=ALU.mult), p, m_msk)
        bfree[4] = [b]
        m_pos = dve.do(lambda e: e.tensor_scalar(at(posf, 64), at(posf, 64), -1.0, None, ALU.add), b)
        route_end = [m_pos, p]

        w1 = Work(xs2 + 4096)
        sg, hid = w1.take(2048), w1.take(2048)
        oldest = pos[0] % NR0
        old = slots[oldest:] + slots[:oldest]
        for _ in range((X - w1.o) // W):
            add_slot(w1.take(W), [p_wout, p_ada, *m_X])
        assert w1.o <= X
        w2 = Work(X + 4096)
        xeT = [w2.take(512), w2.take(512)]
        hidT = [w2.take(1024), w2.take(1024)]
        YE = w2.take(1024)
        OH = [w2.take(256), w2.take(256)]
        OHW = w2.take(512)
        OHWT = w2.take(512)
        while w2.o + W <= AR:
            add_slot(w2.take(W), [p_branch])
        n_w1 = (X - xs2 - 8192) // W
        slots[:] = slots[NR0 + n_w1:] + old + slots[NR0:NR0 + n_w1]
        pos[0] = 0
        xe_free, oh_free, hid_free, hidT_free = [None] * 2, [None] * 2, list(route_end), [None] * 2
        ohw_free, ohwt_free, ye_free, ct_free = None, None, None, [None] * 2
        iota = cst("iota")
        sg_free = list(route_end) + m_h2 + [p_lg]
        one_hot = {}
        xe_m = {}

        def gather(ex):
            nonlocal ohw_free
            z = ex % 2
            for c in range(TC):
                b = dve.do(lambda e, c=c: e.tensor_scalar(
                    at(OH[z] + 64 * c, 64), iota, at(posf + 16 * c + ex, 1), None, ALU.is_equal), m_pos, oh_free[z], *route_end)
            for k in range(KD):
                for c in range(TC):
                    bk = 5 - k // 4
                    f = lambda e, k=k, c=c, bk=bk: e.matmul(bank(bk, 64, 64 * (k % 4)), at(xs2 + 1024 * c + 128 * k, 128),
                                                            at(OH[z] + 64 * c, 64), start=(c == 0), stop=(c == 3))
                    if (k % 4, c) != (3, 3):
                        pe.quiet(f, b, *bfree[bk])
                    else:
                        p = pe.do(f)
                        if k == 3:
                            p5 = p
            oh_free[z] = p
            xe_m[ex] = []
            for k in range(KD):
                if k >= 4:
                    m = dve.do(lambda e, k=k: e.tensor_scalar(at(xeT[z] + 64 * k, 64), bank(4, 64, 64 * (k - 4)), at(sc2 + k, 1),
                                                              at(sh2 + k, 1), ALU.mult, ALU.add), p, xe_free[z], *route_end)
                    bfree[4] = [m]
                else:
                    m = act.do(lambda e, k=k: e.activation(at(xeT[z] + 64 * k, 64), bank(5, 64, 64 * k), ACT.Identity,
                                                           bias=at(sh2 + k, 1), scale=at(sc2 + k, 1)), p5, xe_free[z], *route_end)
                    bfree[5] = [m]
                xe_m[ex].append(m)
            for c in range(TC):
                one_hot[ex] = dve.do(lambda e, c=c: e.tensor_scalar(
                    at(OHW + 128 * c + 64 * z, 64), iota, at(posf + 16 * c + ex, 1), at(aff + 16 * c + ex, 1),
                    ALU.is_equal, ALU.mult), ohw_free, *route_end)
            if z == 1:
                for c in range(TC):
                    f = lambda e, c=c: e.transpose(bank(5, 128, 128 * c), at(OHW + 128 * c, 128), ident)
                    if c < 3:
                        pe.quiet(f, one_hot[ex], *bfree[5])
                    else:
                        p = pe.do(f)
                ohw_free = p
                one_hot["T"] = act.do(lambda e: e.activation(at(OHWT, 512), bank(5), ACT.Copy), p, ohwt_free, *route_end)
                bfree[5] = [one_hot["T"]]

        def combine(ym):
            for tc in range(TC):
                for dh in range(2):
                    bk = 6 + dh
                    p = pe.do(lambda e, tc=tc, dh=dh, bk=bk: e.matmul(
                        bank(bk), at(OHWT + 128 * tc, 128), at(YE + 512 * dh, 512), start=True, stop=True),
                        one_hot["T"], *ym, *bfree[bk])
                    xa = at(X + 1024 * tc + 512 * dh, 512)
                    m = dve.do(lambda e, xa=xa, bk=bk: e.tensor_tensor(xa, xa, bank(bk), ALU.add), p, *m_xs2)
                    bfree[bk] = [m]
                    m_X[tc] = m
            return p

        gather(0)
        ym = pending = None
        for ex in range(NE):
            z = ex % 2
            for k in range(KD):
                cg = chunk(t["w_exp_gate"][ex, k * 128:(k + 1) * 128, :], (1, 2048))
                cu = chunk(t["w_exp_up"][ex, k * 128:(k + 1) * 128, :], (1, 2048))
                for fb in range(4):
                    for gu, c in ((0, cg), (1, cu)):
                        f = lambda e, gu=gu, c=c, fb=fb, k=k, z=z: e.matmul(
                            PS[64 * gu:64 * gu + 64, fb, :], at(xeT[z] + 64 * k, 64), c.ap[:, 512 * fb:512 * fb + 512],
                            start=(k == 0), stop=(k == 7))
                        if fb == 3:
                            c.released = pe.do(f, c.mark, xe_m[ex][k], *(bfree[fb] if k == 0 else ()))
                        else:
                            pe.quiet(f, c.mark, xe_m[ex][k], *(bfree[fb] if k == 0 else ()))
                if k == 3 and pending:
                    ohwt_free = ye_free = combine(pending)
                    pending = None
            p = (pe.name, pe.count)
            xe_free[z] = p
            hg = []
            for fb in range(4):
                a = act.do(lambda e, fb=fb: e.activation(A[64:128, sg + 512 * fb:sg + 512 * fb + 512], PS[0:64, fb, :], ACT.Silu),
                           p, *sg_free)
                m = dve.do(lambda e, fb=fb: e.tensor_tensor(
                    A[64:128, hid + 512 * fb:hid + 512 * fb + 512], A[64:128, sg + 512 * fb:sg + 512 * fb + 512],
                    PS[64:128, fb, :], ALU.mult), a, p, *hid_free)
                bfree[fb] = [m]
                hg.append(m)
            sg_free = [m]
            if ex + 1 < NE:
                gather(ex + 1)
            for fb in range(4):
                bk = 6 + fb % 2
                for q in range(4):
                    f = lambda e, fb=fb, q=q, bk=bk: e.transpose(
                        bank(bk, 64, 64 * q), A[64:128, hid + 512 * fb + 128 * q:hid + 512 * fb + 128 * q + 128],
                        A[64:128, o_cst + 64:o_cst + 128])
                    if q < 3:
                        pe.quiet(f, hg[fb], *bfree[bk])
                    else:
                        pt = pe.do(f)
                hm = act.do(lambda e, fb=fb, bk=bk, z=z: e.activation(at(hidT[z] + 256 * fb, 256), bank(bk, 256), ACT.Copy),
                            pt, hidT_free[z], *route_end)
                bfree[bk] = [hm]
            hid_free = [pt]
            for n in range(8):
                cd = chunk(t["w_exp_down"][ex, n * 256:(n + 1) * 256, :].rearrange("(k p) n -> p k n", p=128), (2, 1024))
                for k in range(2):
                    for dh in range(2):
                        f = lambda e, n=n, k=k, dh=dh, cd=cd, z=z: e.matmul(
                            PS[64 * dh:64 * dh + 64, 4, :], at(hidT[z] + 64 * (2 * n + k), 64), cd.ap[:, k, 512 * dh:512 * dh + 512],
                            start=(n + k == 0), stop=(n + k == 8))
                        if (k, dh) == (1, 1):
                            p = cd.released = pe.do(f, cd.mark, hm, *bfree[4])
                        else:
                            pe.quiet(f, cd.mark, hm, *bfree[4])
            hidT_free[z] = p
            if z == 0:
                ym = []
            for dh in range(2):
                ym.append(dve.do(lambda e, dh=dh, z=z: e.tensor_tensor(
                    A[64 * z:64 * z + 64, YE + 512 * dh:YE + 512 * dh + 512], PS[64 * dh:64 * dh + 64, 4, :],
                    A[64 * dh:64 * dh + 64, gate2_o + 512 * dh:gate2_o + 512 * dh + 512], ALU.mult),
                    p, ye_free, m_g2, *route_end))
            bfree[4] = ym[-1:]
            if z == 1:
                pending = ym
        p = combine(pending)
        p_ex = p
        ex_end = [p_ex, m_X[3], ym[-1], (dve.name, dve.count), (act.name, act.count)]

        slots[:] = list(range(NR0))
        extra = [last_user[s] for s in range(NR0, len(ring_o))]
        extra_m = [c.released for c in extra if c is not None]
        end = ex_end + extra_m
        xnT = xs2
        w1 = Work(xnT + 4096)
        U = w1.take(4 * 542)
        cv = w1.take(2048)
        yT_conv = w1.take(2048)
        tp = w1.take(2048)
        assert w1.o <= X
        w2 = Work(X + 4096)
        psb = w2.take(2048 + 64)
        yT_pool = w2.take(2048)
        gf_o = gate1_o
        m_gf = load(act, at(gf_o, 1024), bass.AP(t["g_final_2"].tensor, t["g_final_2"].offset, [[0, 128], [1, 1024]]), "l_gf", *end)

        xsn = xnT + 4096 - 4096
        xs3 = U
        assert xs3 + 4096 <= tp
        m_xs = rms(X, xs3, m_X, end, tp, end)
        m_xn = turn(xs3, m_xs, lambda k: at(xnT + 512 * k, 512), lambda k: vcol("gmix", k), None, [m_vec], end, [0, 1, 2, 3])
        p_t = (pe.name, pe.count)
        xn = lambda k: at(xnT + 512 * k, 512)
        pads = dve.do(lambda e: e.memset(raw(U, [(542, 4), (1, 30)]), 0.0), p_t)
        padp = dve.do(lambda e: e.memset(raw(psb, [(528, 4), (1, 16)]), 0.0), *end)
        u_m = [None] * 4
        tfree = [p_t, p_t, p_t, p_t]
        tn_ = [0]

        def tget():
            i = tn_[0] % 4
            tn_[0] += 1
            return i, tp + 512 * i

        def second_in():
            for n in range(2):
                cg = col_chunk(t["w_in_2"], 2 + n)
                ca = col_chunk(t["w_in_2"], n)
                for j in range(2):
                    ti_ = 2 * n + j
                    bg = next_bank([0, 1, 2, 3])
                    p = dense_T(bg, cg, j, xn, m_xn)
                    i, o = tget()
                    a = act.do(lambda e, bg=bg, o=o, ti_=ti_: e.activation(at(o, 512), bank(bg), ACT.Sigmoid, bias=vcol("bin", 4 + ti_)),
                               p, tfree[i])
                    bfree[bg] = [a]
                    ba = next_bank([0, 1, 2, 3])
                    p = dense_T(ba, ca, j, xn, m_xn)
                    u_m[ti_] = dve.do(lambda e, ba=ba, o=o, ti_=ti_: e.scalar_tensor_tensor(
                        out=at(U + 542 * ti_ + 30, 512), in0=bank(ba), scalar=vcol("bin", ti_), in1=at(o, 512),
                        op0=ALU.add, op1=ALU.mult), p, a, p_t)
                    bfree[ba] = [u_m[ti_]]
                    tfree[i] = u_m[ti_]
                    yield
            for n in range(2):
                c = col_chunk(t["w_in_2"], 4 + n)
                for j in range(2):
                    g = 2 * n + j
                    bk = next_bank([0, 1, 2, 3])
                    p = dense_T(bk, c, j, xn, m_xn)
                    po = psb + 528 * g + 16
                    w = WIN[g]
                    m = act.do(lambda e, bk=bk, po=po, g=g: e.activation(at(po, 512), bank(bk), ACT.Identity, bias=vcol("bin", 8 + g)),
                               p, *end)
                    bfree[bk] = [m]
                    i, o = tget()
                    i2, o2 = tget()
                    src, span = po - 16, 528
                    h = 1
                    cur = src
                    fl = [m, padp, tfree[i], tfree[i2]]
                    nxt = [o, o2]
                    width = 512
                    first = 16
                    dsto = pool_t
                    lead = w - 2
                    n0 = 0
                    cur_o, cur_lead = po, 16
                    while h < w:
                        left = w - 2 * h
                        d_o = dsto[n0 % 2] + 16
                        m = pool.do(lambda e, d_o=d_o, left=left, cur_o=cur_o, h=h: e.tensor_tensor(
                            at(d_o - left, 512 + left), at(cur_o - left, 512 + left), at(cur_o - left - h, 512 + left), ALU.add),
                            m, padp, *pt_free, *end)
                        cur_o = d_o
                        h *= 2
                        n0 += 1
                    b = dve.do(lambda e, cur_o=cur_o, g=g: e.tensor_tensor(at(cur_o, 16), at(cur_o, 16),
                                                                           at(o_cst + CST["popc"][0] + 16 * g, 16), ALU.mult), m)
                    m = dve.do(lambda e, cur_o=cur_o, po=po, w=w: e.scalar_tensor_tensor(
                        out=at(po, 512), in0=at(cur_o, 512), scalar=1.0 / w, in1=at(po, 512), op0=ALU.mult, op1=ALU.subtract), b)
                    pt_free[:] = [m]
                    bk = next_bank([0, 1, 2, 3])
                    p = pe.do(lambda e, bk=bk, g=g, po=po: e.matmul(bank(bk), at(o_vec + VEC["wpool"][0] + 128 * g, 128), at(po, 512),
                                                                    start=True, stop=True), m, *bfree[bk])
                    y_m[4 + g] = act.do(lambda e, bk=bk, g=g: e.activation(at(yT_pool + 512 * g, 512), bank(bk), ACT.Copy,
                                                                           scale=vcol("spool", g)), p, *end)
                    bfree[bk] = [y_m[4 + g]]
                    yield

        pool_t = [w2.take(544), w2.take(544)]
        pt_free = []
        y_m = [None] * 8
        cv_m = [None] * 4

        def conv():
            dg = []
            for k in range(31):
                dg.append(pool.do(lambda e, k=k: e.tensor_scalar(
                    at(DG + 128 * k, 128), ident, at(o_vec + VEC["wdw"][0] + 93 + k, 1), None, ALU.mult), *end))
            for i in range(3):
                tap = lambda k, i=i: at(o_vec + VEC["wdw"][0] + 31 * i + k, 1)
                u = lambda k, i=i: at(U + 542 * i + k, 512)
                v = at(cv + 512 * i, 512)
                NP = 12 if i == 0 else 0
                for k in range(NP):
                    if k == 0:
                        g = pool.do(lambda e, k=k, tap=tap, u=u: e.tensor_scalar(at(cv2, 512), u(k), tap(k), None, ALU.mult),
                                    u_m[i], pads, p_t)
                    else:
                        g = pool.do(lambda e, k=k, tap=tap, u=u: e.tensor_scalar(at(cv2 + 512, 512), u(k), tap(k), None, ALU.mult), g)
                        g = pool.do(lambda e: e.tensor_tensor(at(cv2, 512), at(cv2, 512), at(cv2 + 512, 512), ALU.add), g)
                for k in range(NP, 31):
                    if k == NP:
                        m = dve.do(lambda e, k=k, v=v, tap=tap, u=u, i=i: e.tensor_scalar(v, u(k), tap(k), vcol("bdw", i), ALU.mult, ALU.add),
                                   u_m[i], pads, p_t)
                    else:
                        m = dve.do(lambda e, k=k, v=v, tap=tap, u=u: e.scalar_tensor_tensor(out=v, in0=u(k), scalar=tap(k), in1=v,
                                                                                           op0=ALU.mult, op1=ALU.add), m)
                if NP:
                    late.append((v, m, g))
                cv_m[i] = m
                yield
            for k in range(31):
                p = pe.do(lambda e, k=k: e.matmul(bank(6), at(DG + 128 * k, 128), at(U + 542 * 3 + k, 512),
                                                  start=(k == 0), stop=(k == 30)), u_m[3], pads, dg[k], *bfree[6])
            cv_m[3] = act.do(lambda e: e.activation(at(cv + 1536, 512), bank(6), ACT.Identity, bias=vcol("bdw", 3)), p, p_t)
            bfree[6] = [cv_m[3]]
            yield
            v, m, g = late[0]
            cv_m[0] = dve.do(lambda e: e.tensor_tensor(v, v, at(cv2, 512), ALU.add), m, g)

        late = []
        cv2 = w1.take(1024)
        DG = w1.take(31 * 128)
        assert w1.o <= X
        weave(second_in(), conv())
        for i in range(4):
            f = lambda e, i=i: e.matmul(bank(4), cst("o512"), at(cv + 512 * i, 512), start=(i == 0), stop=(i == 3))
            p = pe.do(f, cv_m[i], *bfree[4])
        d_m, s_m = [], []
        for i in range(4):
            d_m.append(dve.do(lambda e, i=i: e.tensor_tensor(at(cv + 512 * i, 512), at(cv + 512 * i, 512), bank(4), ALU.subtract), p))
            s_m.append(act.do(lambda e, i=i: e.activation(at(tp + 512 * i, 512), at(cv + 512 * i, 512), ACT.Square), d_m[i], *tfree, *pt_free))
        bfree[4] = [d_m[-1]]
        for i in range(4):
            p = pe.do(lambda e, i=i: e.matmul(bank(5), cst("o512"), at(tp + 512 * i, 512), start=(i == 0), stop=(i == 3)), s_m[i], *bfree[5])
        rs = U
        a2, m = rsqrt_tile(at(rs, 512), bank(5), "eps5", p, *cv_m)
        bfree[5] = [a2]
        for i in range(4):
            b = dve.do(lambda e, i=i: e.tensor_tensor(at(cv + 512 * i, 512), at(cv + 512 * i, 512), at(rs, 512), ALU.mult), m, s_m[i])
            y_m[i] = act.do(lambda e, i=i: e.activation(at(yT_conv + 512 * i, 512), at(cv + 512 * i, 512), ACT.Silu,
                                                        bias=vcol("lnb", i), scale=vcol("lng", i)), b, p_t)
        y_lhs = lambda k, tc: at((yT_conv + 512 * k if k < 4 else yT_pool + 512 * (k - 4)) + 128 * tc, 128)
        m_X = residual_out(t["w_out_2"], y_lhs, y_m, X, m_X, None, None, None, None, [0, 1, 2, 3, 6, 7])
        p_o2 = (pe.name, pe.count)

        end2 = [p_o2, (act.name, act.count), (dve.name, dve.count)]
        hid_o = work
        tq = hid_o + FT * 512
        XH = part("xh", tq + 2048, 4096)
        assert tq + 2048 + 4096 <= X
        w2 = Work(X + 4096)
        wo = w2.take(8192)
        WH = [part(f"wh{i}", wo + 4096 * i, 2048) for i in range(2)]
        WL = [part(f"wl{i}", wo + 4096 * i + 2048, 2048) for i in range(2)]
        XL = part("xl", w2.take(4096), 4096)
        hidf = part("hidf", hid_o, FT * 512, F32)
        xs4, scr = wo, wo + 4096
        m_xs = rms(X, xs4, m_X, end2, scr, end2)
        m_xn = turn(xs4, m_xs, lambda k: hidf[:, 512 * k:512 * k + 512], lambda k: vcol("gffn", k), None, [m_vec], end2, [0, 1, 2, 3])
        p_t = (pe.name, pe.count)
        m_x3 = [split(hidf[:, 512 * k:512 * k + 512], XH[:, 512 * k:512 * k + 512], XL[:, 512 * k:512 * k + 512], m_xn[k], free=end2)
                for k in range(KD)]
        w_free = [[p_t, *m_xs], [p_t, *m_xs]]
        wn = [0]

        def split_chunk(c):
            i = wn[0] % 2
            wn[0] += 1
            m = c.released = split(c.flat, WH[i][:, :], WL[i][:, :], c.mark, free=w_free[i])
            return i, m

        def dense_3(bk, i, m, j):
            for k in range(KD):
                o, x = 256 * k + 128 * j, slice(512 * k, 512 * k + 512)
                pe.quiet(lambda e, o=o, x=x, k=k: e.matmul(bank(bk), WH[i][:, o:o + 128], XH[:, x], start=(k == 0), stop=False),
                         m, m_x3[k], *(bfree[bk] if k == 0 else ()))
                pe.quiet(lambda e, o=o, x=x: e.matmul(bank(bk), WH[i][:, o:o + 128], XL[:, x], start=False, stop=False))
                f = lambda e, o=o, x=x, k=k: e.matmul(bank(bk), WL[i][:, o:o + 128], XH[:, x], start=False, stop=(k == KD - 1))
                if k < KD - 1:
                    pe.quiet(f)
                else:
                    p = pe.do(f)
            w_free[i] = [p]
            return p

        def down_chunk(n):
            return chunk(t["w_down_2"][n * 256:(n + 1) * 256, :].rearrange("(k p) n -> p k n", p=128), (2, 1024))

        tqf = [None] * 4
        hm = [None] * FT
        gate_w, up_w = [split_chunk(col_chunk(t[n], 0)) for n in ("w_gate_2", "w_up_2")]
        for n in range(FT // 2):
            sg_m = [None] * 2
            for j in range(2):
                f_ = 2 * n + j
                o = tq + 512 * (f_ % 4)
                bk = next_bank([0, 1, 2, 3])
                p = dense_3(bk, *gate_w, j)
                sg_m[j] = act.do(lambda e, bk=bk, o=o: e.activation(at(o, 512), bank(bk), ACT.Silu), p, tqf[f_ % 4], *end2)
                bfree[bk] = [sg_m[j]]
            gate_w = split_chunk(col_chunk(t["w_gate_2"], n + 1) if n + 1 < FT // 2 else down_chunk(0))
            for j in range(2):
                f_ = 2 * n + j
                o = tq + 512 * (f_ % 4)
                bk = next_bank([0, 1, 2, 3])
                p = dense_3(bk, *up_w, j)
                hm[f_] = dve.do(lambda e, bk=bk, o=o, f_=f_: e.tensor_tensor(hidf[:, 512 * f_:512 * f_ + 512], at(o, 512), bank(bk), ALU.mult),
                                p, sg_m[j], p_t, m_x3[-1])
                bfree[bk] = [hm[f_]]
                tqf[f_ % 4] = hm[f_]
            up_w = split_chunk(col_chunk(t["w_up_2"], n + 1) if n + 1 < FT // 2 else down_chunk(1))
        h_free = [p, p]
        down_w = [gate_w, up_w]

        def hid_parts(n):
            o = 2048 * (n % 2)
            return XH[:, o:o + 1024], XH[:, o + 1024:o + 2048]
        mh_next = split(hidf[:, 0:1024], *hid_parts(0), hm[1], free=[p])
        for n in range(FT // 2):
            i, m = down_w[n % 2]
            z = n % 2
            HH, HL = hid_parts(n)
            mh = mh_next
            if n + 1 < FT // 2:
                mh_next = split(hidf[:, 1024 * n + 1024:1024 * n + 2048], *hid_parts(n + 1), hm[2 * n + 3], free=[h_free[1 - z]])
            for k in range(2):
                f_ = 2 * n + k
                for tc in range(TC):
                    o = slice(512 * k + 128 * tc, 512 * k + 128 * tc + 128)
                    for q, (l, w) in enumerate(((HH, WH), (HH, WL), (HL, WH))):
                        for dh in range(2):
                            f = lambda e, i=i, k=k, f_=f_, tc=tc, dh=dh, o=o, l=l, w=w, q=q: e.matmul(
                                bank(2 * tc + dh), l[:, o], w[i][:, 1024 * k + 512 * dh:1024 * k + 512 * dh + 512],
                                start=(f_ == 0 and q == 0), stop=(f_ == FT - 1 and q == 2))
                            mk = [m, mh] + (bfree[2 * tc + dh] if f_ == 0 and q == 0 else [])
                            if q == 2 and ((k, tc, dh) == (1, 3, 1) or f_ == FT - 1):
                                p = pe.do(f, *mk)
                                if f_ == FT - 1:
                                    st["dn", tc, dh] = p
                            else:
                                pe.quiet(f, *mk)
            w_free[i] = [p]
            h_free[z] = p
            if n + 2 < FT // 2:
                down_w[z] = split_chunk(down_chunk(n + 2))
        fin = small(8)
        so = hid_o
        ov = out.rearrange("b (c p) d -> p (b c) d", p=128)
        p_last = p
        for tc in range(TC):
            for dh in range(2):
                xa = at(X + 1024 * tc + 512 * dh, 512)
                m = dve.do(lambda e, xa=xa, tc=tc, dh=dh: e.tensor_tensor(xa, xa, bank(2 * tc + dh), ALU.add), st["dn", tc, dh], m_X[tc])
            a = act.do(lambda e, tc=tc: e.activation(at(so + 1024 * tc, 1024), at(X + 1024 * tc, 1024), ACT.Square, scale=1.0 / 32,
                                                     accum_out=at(fin + tc, 1)), m, hm[FT - 1])
            _, b = rsqrt(at(fin + 4 + tc, 1), at(fin + tc, 1), "eps6", a)
            b = dve.do(lambda e, tc=tc: e.scalar_tensor_tensor(out=at(so + 1024 * tc, 1024), in0=at(X + 1024 * tc, 1024),
                                                               scalar=at(fin + 4 + tc, 1), in1=at(gf_o, 1024),
                                                               op0=ALU.mult, op1=ALU.mult), b, m_gf)
            load(act, ov[:, tc, :], at(so + 1024 * tc, 1024), "l_out", b)
        act.wait([("l_out", 64)])

        for c in chunks:
            marks = list(c.first) + ([c.prev.released] if c.prev is not None else [])
            for dst, src in c.parts:
                sp.dma(lambda e, dst=dst, src=src: e.dma_start(dst, src), c.mark[0], c.mark[1], *marks)

        sems = {n: ctx.enter_context(nc.semaphore(n)) for n in
                ["pe", "dve", "act", "pool"] + list(dsems) + [f"r{s}" for s in range(len(ring_o))]}
        block = ctx.enter_context(nc.Block())

        @block.sync
        def _(e):
            sp.emit(e, sems)

        @block.scalar
        def _(e):
            act.emit(e, sems)

        @block.vector
        def _(e):
            dve.emit(e, sems)

        @block.gpsimd
        def _(e):
            pool.emit(e, sems)

        @block.tensor
        def _(e):
            pe.emit(e, sems)


def constants():
    p = np.arange(128)
    c = np.zeros((128, NCST), np.float32)

    def put(n, v):
        c[:, CST[n][0]:CST[n][0] + CST[n][1]] = v
    put("ident", np.eye(128))
    put("ones", 1.0)
    put("tri", p[:, None] < p[None, :])
    put("bo64", (p[:, None] // 64 == p[None, :] // 64) / 64.0)
    rot = np.zeros((128, 128))
    for m in range(128):
        if m % 32 < 16:
            rot[m + 16, m] = -1.0
        else:
            rot[m - 16, m] = 1.0
    put("rot", rot)
    put("o128", 1.0 / 128)
    put("o512", 1.0 / 512)
    put("iota", np.arange(64)[None, :])
    tt = np.arange(16)
    put("popc", np.concatenate([w / np.minimum(tt + 1, w) for w in WIN])[None, :])
    f = np.float32
    inv = (f(10000.0) ** (-np.arange(0, 32, 2, dtype=f) / f(32))).astype(f)
    tok = np.arange(S)
    where = np.stack([(tok // 64).astype(f), (tok % 64).astype(f)])
    d = p % 64
    ang = (where[d // 32] * inv[d % 16][:, None]).astype(f)
    put("ropec", np.cos(ang))
    put("ropes", np.sin(ang))
    put("eps6", 1e-6)
    put("eps5", 1e-5)
    x = p[:, None] ^ p[None, :]
    put("lev", np.concatenate([x >= h for h in LEVELS], 1))
    return c


_BIG = ["ada_w", "w_in", "w_branch_att", "w_branch_hg", "w_out", "w_exp_gate", "w_exp_up", "w_exp_down",
        "w_in_2", "w_out_2", "w_gate_2", "w_up_2", "w_down_2"]


def kernel(**inputs):
    import concourse.bacc as _bacc
    from concourse.bass_utils import run_bass_kernel_spmd as _run

    g = {n: np.ascontiguousarray(v) for n, v in inputs.items()}
    arrays = {"x": g["x"], "ada_b": g["ada_b"], "g_final_2": g["g_final_2"]}
    for n in _BIG:
        arrays[n] = g[n].reshape(g[n].shape[1:])

    def cols(a, k):
        return np.ascontiguousarray(a).reshape(k, 128).T
    parts = {
        "nmw": cols(g["norm_mix_w"], 8), "nfw": cols(g["norm_ffn_w"], 8),
        "qn": np.concatenate([g["q_norm_w"][0]] * 2)[:, None], "kn": np.concatenate([g["k_norm_w"][0]] * 2)[:, None],
        "lb": cols(g["hg_lower_bounds"], 8), "hgw": cols(g["hg_norm_w"], 1), "bin": cols(g["b_in_2"], 12),
        "wdw": g["w_dw_2"][0].T.reshape(4, 128, 31).transpose(1, 0, 2).reshape(128, 124),
        "bdw": cols(g["b_dw_2"], 4), "lng": cols(g["ln_g_2"], 4), "lnb": cols(g["ln_b_2"], 4),
        "spool": cols(g["s_pool_2"], 4), "gmix": cols(g["g_mix_2"], 8), "gffn": cols(g["g_ffn_2"], 8), "c": cols(g["c"], 8),
        "wr": g["w_router"][0].reshape(8, 128, 16).transpose(1, 0, 2).reshape(128, 128),
        "wpool": g["w_pool_2"][0].transpose(1, 0, 2).reshape(128, 512),
    }
    arrays["vec"] = np.ascontiguousarray(np.concatenate([parts[n] for n in VEC], 1))
    arrays["cst"] = constants()

    nc = _bacc.Bacc("TRN2", target_bir_lowering=False, num_devices=1)
    feed, t = {}, {}
    for n, a in arrays.items():
        feed[f"in_{n}"] = a
        t[n] = nc.dram_tensor(f"in_{n}", a.shape, mybir.dt.from_np(a.dtype), kind="ExternalInput").ap()
    out = nc.dram_tensor("out_0", (1, S, D), F32, kind="ExternalOutput").ap()
    build(nc, t, out)
    r = _run(nc, [feed], core_ids=[0])
    return r.results[0]["out_0"]
```

```python
from contextlib import ExitStack

import numpy as np

import concourse.bass as bass
from concourse import mybir

F32 = mybir.dt.float32
F32R = mybir.dt.float32r
ALU = mybir.AluOpType
ACT = mybir.ActivationFunctionType
AX = mybir.AxisListType.X

S, D, TC = 512, 1024, 4
BASE = 16512
KD = D // 128
NE, CAP, FF = 16, 64, 2048
EPS = 1e-6
LEVELS = (1, 2, 4, 8, 16, 32, 64)
WIN = (2, 4, 8, 16)
FT = 22

CST = {}
_o = 0
for _n, _w in (("ident", 128), ("ones", 128), ("tri", 128), ("bo64", 128), ("rot", 128), ("o128", 128),
               ("o512", 128), ("iota", 64), ("popc", 64), ("ropec", 512), ("ropes", 512), ("eps6", 1), ("eps5", 1),
               ("lev", 128 * 7)):
    CST[_n] = (_o, _w)
    _o += _w
NCST = _o
VEC = {}
_o = 0
for _n, _w in (("nmw", 8), ("nfw", 8), ("qn", 1), ("kn", 1), ("lb", 8), ("hgw", 1), ("bin", 12), ("wdw", 124),
               ("bdw", 4), ("lng", 4), ("lnb", 4), ("spool", 4), ("gmix", 8), ("gffn", 8), ("c", 8),
               ("wr", 128), ("wpool", 512)):
    VEC[_n] = (_o, _w)
    _o += _w
NVEC = _o


HEAD = -(-(NCST + NVEC + 900) // 8) * 8 + 2048
W, NR0 = 2048, 6
AR = 52992


class Arena:

    def __init__(self, nc):
        self.parts = []
        for name, start, end in (("stay", 0, HEAD), ("ring", HEAD, HEAD + NR0 * W), ("work", HEAD + NR0 * W, AR)):
            self.parts.append((start, end, nc.alloc_sbuf_tensor_at(name, [128, end - start], F32, offset=BASE + 4 * start)))

    def __getitem__(self, where):
        rows, cols = where
        for start, end, tensor in self.parts:
            if start <= cols.start < end:
                assert cols.stop <= end
                return tensor[rows, cols.start - start:cols.stop - start]


class Queue:

    def __init__(self, name):
        self.name, self.items, self.count, self.seen = name, [], 0, {}

    def wait(self, marks):
        for m in marks:
            if m is not None and self.seen.get(m[0], 0) < m[1]:
                self.seen[m[0]] = m[1]
                self.items.append(("wait", m))

    def do(self, fn, *marks):
        self.wait(marks)
        self.count += 1
        self.items.append(("inc", fn, (self.name, 1)))
        return (self.name, self.count)

    def quiet(self, fn, *marks):
        self.wait(marks)
        self.items.append(("run", fn))

    def dma(self, fn, sem, value, *marks):
        self.wait(marks)
        self.items.append(("inc", fn, (sem, 16)))
        return (sem, value)

    def emit(self, eng, sems):
        for it in self.items:
            if it[0] == "wait":
                eng.wait_ge(sems[it[1][0]], it[1][1])
            elif it[0] == "run":
                it[1](eng)
            else:
                it[1](eng).then_inc(sems[it[2][0]], it[2][1])


def build(nc, t, out):
    with ExitStack() as ctx:
        A = Arena(nc)
        PS = ctx.enter_context(nc.psum_tensor("ps", [128, 8, 512], F32))

        pe, dve, act, pool, sp = (Queue(n) for n in ("pe", "dve", "act", "pool", "sp"))
        dsems = {}

        def load(q, dst, src, sem, *marks):
            dsems[sem] = dsems.get(sem, 0) + 16
            return q.dma(lambda e: e.dma_start(dst, src), sem, dsems[sem], *marks)

        top = [0]

        def take(n):
            o = top[0]
            top[0] += n
            assert top[0] <= AR, top[0]
            return o

        def at(o, n):
            return A[:, o:o + n]

        def part(name, o, n, dtype=F32R):
            return nc.alloc_sbuf_tensor_at(name, [128, n], dtype, offset=BASE + 4 * o)

        def raw(o, dims):
            b = A[:, o:o + 1]
            return bass.AP(b.tensor, b.offset, [b.ap[0]] + [list(d) for d in dims])

        def bank(b, n=512, o=0):
            return PS[:, b, o:o + n]

        o_cst, o_vec = take(NCST), take(NVEC)

        def cst(n):
            return at(o_cst + CST[n][0], CST[n][1])

        def vec(n):
            return at(o_vec + VEC[n][0], VEC[n][1])

        def vcol(n, i):
            return at(o_vec + VEC[n][0] + i, 1)

        ident, ones, tri = cst("ident"), cst("ones"), cst("tri")
        sm = take(900)
        sm_top = [sm]

        def small(n):
            o = sm_top[0]
            sm_top[0] += n
            assert sm_top[0] <= sm + 900
            return o

        take(-top[0] % 8)
        gate1_o, gate2_o = take(1024), take(1024)
        base = top[0]

        assert top[0] == HEAD
        ring_o = [take(W) for _ in range(NR0)]
        work = top[0]
        chunks = []
        pos = [0]
        slots = list(range(NR0))
        last_user = {s: None for s in slots}
        slot_free = {s: () for s in slots}
        uses = {s: 0 for s in slots}

        class Chunk:
            pass

        def chunk(src, shape):
            c = Chunk()
            s = slots[pos[0] % len(slots)]
            pos[0] += 1
            parts = src if isinstance(src, list) else [src]
            uses[s] += len(parts)
            c.slot, c.prev, c.first = s, last_user[s], slot_free[s]
            last_user[s] = c
            c.released = None
            c.mark = (f"r{s}", 16 * uses[s])
            ap = at(ring_o[s], W)
            c.flat = ap
            c.ap = ap.rearrange("p (k n) -> p k n", k=shape[0]) if shape[0] > 1 else ap
            n = shape[0] // len(parts)
            c.parts = [(c.ap if len(parts) == 1 else c.ap[:, n * i:n * i + n, :], v) for i, v in enumerate(parts)]
            chunks.append(c)
            return c

        def add_slot(o, marks):
            s = len(ring_o)
            ring_o.append(o)
            slots.append(s)
            last_user[s], uses[s], slot_free[s] = None, 0, tuple(marks)

        def col_chunk(w, n):
            return chunk(w[:, n * 256:(n + 1) * 256].rearrange("(k p) n -> p k n", p=128), (8, 256))

        m_vec = load(act, at(o_vec, NVEC), t["vec"], "l_vec")

        def reuse(lst):
            out = []
            for x in lst:
                out += list(x) if isinstance(x, list) else [x]
            return out

        bfree = {b: [] for b in range(8)}

        def split(src, hi, lo, *marks, free=(), by=dve):
            a = act.do(lambda e: e.activation(hi, src, ACT.Copy), *marks, *free)
            return by.do(lambda e: e.tensor_tensor(lo, src, hi.bitcast(F32), ALU.subtract), a, *marks, *free)

        class Work:

            def __init__(self, start):
                self.o = start

            def take(self, n):
                o = self.o
                self.o += n
                assert self.o <= AR, self.o
                return o

        wk = Work(work)
        hT = wk.take(4096)
        QQ, KK = wk.take(2048), wk.take(2048)
        TTa, TTb = wk.take(2048), wk.take(1024)
        q0 = wk.take(1024)
        PT = wk.take(4096)
        Vp = wk.take(1024)
        qT = wk.take(2048)
        kd = wk.take(1024)
        va = wk.take(512)
        Pb = wk.take(1536)
        PTa = wk.take(2048)
        oatt = wk.take(2048)
        ohg = wk.take(2048)
        sgh = wk.take(1024)
        tmp = wk.take(2048)
        x_o, xs_o = QQ, PT
        assert PT + 4096 <= qT and QQ + 4096 <= PT
        acc_o, adab_o = tmp, PTa

        xv = t["x"].rearrange("b (c p) d -> p (b c) d", p=128)
        m_zero = pool.do(lambda e: e.memset(at(acc_o, 2048), 0.0))
        m_ab = load(act, A[0:1, acc_o:acc_o + 2048], t["ada_b"][:, 0:2048], "l_ab", m_zero)
        m_cst = load(act, at(o_cst, NCST), t["cst"], "l_cst")
        m_x = load(act, at(x_o, 4096).rearrange("p (c d) -> p c d", c=4), xv, "l_x")

        csg, cact = small(8), small(8)
        a = act.do(lambda e: e.activation(at(csg, 8), vec("c"), ACT.Sigmoid), m_vec)
        m_c = dve.do(lambda e: e.tensor_tensor(at(cact, 8), at(csg, 8), vec("c"), ALU.mult), a, m_vec)

        lbe, lbr, lbs, lbv, oml = small(8), small(8), small(8), small(8), small(8)
        b = dve.do(lambda e: e.tensor_tensor(at(lbe, 8), vec("lb"), vec("lb"), ALU.subtract), m_vec)
        a = act.do(lambda e: e.activation(at(lbs, 8), at(lbe, 8), ACT.Exp), b)
        b = dve.do(lambda e: e.reciprocal(at(lbr, 8), at(lbs, 8)), a)
        b = dve.do(lambda e: e.tensor_tensor(at(lbs, 8), at(lbs, 8), at(lbr, 8), ALU.mult), b)
        b = dve.do(lambda e: e.tensor_tensor(at(lbv, 8), at(lbs, 8), at(lbs, 8), ALU.subtract), b)
        m_lb = dve.do(lambda e: e.tensor_scalar(at(oml, 8), at(lbv, 8), -1.0, 1.0, ALU.mult, ALU.add), b)

        def rms(x, xs, marks, free, scr, scr_marks, part=range(TC)):
            st = small(8)
            outm = []
            for c in part:
                a = act.do(lambda e, c=c: e.activation(at(scr + 1024 * (c % 2), 1024), at(x + 1024 * c, 1024), ACT.Square,
                                                       scale=1.0 / 32, accum_out=at(st + c, 1)),
                           marks[c], *(scr_marks if c == part[0] else ()))
                _, b = rsqrt(at(st + 4 + c, 1), at(st + c, 1), "eps6", a)
                outm.append(dve.do(lambda e, c=c: e.tensor_scalar(at(xs + 1024 * c, 1024), at(x + 1024 * c, 1024),
                                                                  at(st + 4 + c, 1), None, ALU.mult),
                                   b, *(free if c == part[0] else ())))
            return outm

        def rsqrt(dst, src, eps, *marks):
            a = act.do(lambda e: e.activation(dst, src, ACT.Sqrt, bias=cst(eps)), *marks, m_cst)
            return a, dve.do(lambda e: e.reciprocal(dst, dst), a)

        def rsqrt_tile(dst, src, eps, *marks):
            a = act.do(lambda e: e.activation(dst, src, ACT.Ln, bias=cst(eps)), *marks, m_cst)
            return a, act.do(lambda e: e.activation(dst, dst, ACT.Exp, scale=-0.5), a)

        def turn(xs, marks, dst, scale, shift, sc_marks, free, banks, then=None):
            outm = []
            for k in range(KD):
                bk = banks[k % len(banks)]
                for c in range(TC):
                    f = lambda e, k=k, c=c, bk=bk: e.transpose(bank(bk, 128, 128 * c), at(xs + 1024 * c + 128 * k, 128), ident)
                    if c < TC - 1:
                        pe.quiet(f, m_cst, marks[c], *(bfree[bk] if c == 0 else ()))
                    else:
                        p = pe.do(f, m_cst, marks[c])
                fr = free if k == 0 else ()
                if k % 2 == 0:
                    m = dve.do(lambda e, k=k, bk=bk: e.tensor_scalar(
                        dst(k), bank(bk), scale(k), shift(k) if shift else None, ALU.mult,
                        *((ALU.add,) if shift else ())), p, *sc_marks, *fr)
                elif shift:
                    m = act.do(lambda e, k=k, bk=bk: e.activation(dst(k), bank(bk), ACT.Identity,
                                                                  bias=shift(k), scale=scale(k)), p, *sc_marks, *free)
                else:
                    m = act.do(lambda e, k=k, bk=bk: e.activation(dst(k), bank(bk), ACT.Copy,
                                                                  scale=scale(k)), p, *sc_marks, *free)
                bfree[bk] = [m]
                outm.append(m)
                if then:
                    then(k, m)
            return outm

        ada_free = [None]

        ada_m = [None]

        def ada_steps(j, acc_o, *marks, add=False):
            for k in range(KD):
                c = chunk(t["ada_w"][k * 128:(k + 1) * 128, j * 2048:(j + 1) * 2048], (1, 2048))
                if k == 0 and not add:
                    m = dve.do(lambda e, c=c: e.tensor_scalar(at(acc_o, 2048), c.ap, at(cact, 1), None, ALU.mult),
                               c.mark, m_c, ada_free[0], *marks)
                else:
                    m = dve.do(lambda e, c=c, k=k: e.scalar_tensor_tensor(
                        out=at(acc_o, 2048), in0=c.ap, scalar=at(cact + k, 1), in1=at(acc_o, 2048),
                        op0=ALU.mult, op1=ALU.add), c.mark, *((m_c, *marks) if k == 0 else (m,)))
                c.released = ada_m[0] = m
                yield

        def ada_cols(acc_o, half, m, m_bias, bk, o):
            for i in range(8):
                n = half * 1024 + 128 * i
                f = lambda e, n=n, i=i: e.matmul(bank(bk, 1, o + i), at(acc_o + n, 128), ones[:, 0:1], start=True, stop=not m_bias)
                mk = [m, m_cst] + (bfree[bk] if i == 0 else [])
                if m_bias:
                    pe.quiet(f, *mk)
                    f = lambda e, n=n, i=i: e.matmul(bank(bk, 1, o + i), A[0:1, adab_o + n:adab_o + n + 128],
                                                     A[0:1, o_cst + CST["ones"][0]:o_cst + CST["ones"][0] + 1],
                                                     start=False, stop=True)
                    mk = [m_bias]
                p = pe.do(f, *mk)
            return p

        def ada_row(acc_o, half, m, m_bias, dst):
            for i in range(2):
                n = half * 1024 + 512 * i
                bk = 2 + i
                pe.quiet(lambda e, n=n, bk=bk: e.matmul(bank(bk), ones, at(acc_o + n, 512), start=True, stop=False),
                         m, m_cst, *bfree[bk])
                p = pe.do(lambda e, n=n, bk=bk: e.matmul(bank(bk), A[0:1, o_cst + CST["ones"][0]:o_cst + CST["ones"][0] + 128],
                                                         A[0:1, adab_o + n:adab_o + n + 512], start=False, stop=True), m_bias)
                r = act.do(lambda e, i=i, bk=bk: e.activation(at(dst + 512 * i, 512), bank(bk), ACT.Copy), p)
                bfree[bk] = [r]
            return p, r

        def scale_shift(bk, o_sh, o_sc, p, wname):
            sh, sc = small(8), small(8)
            m1 = dve.do(lambda e: e.tensor_copy(at(sh, 8), bank(bk, 8, o_sh)), p)
            m2 = dve.do(lambda e: e.scalar_tensor_tensor(out=at(sc, 8), in0=bank(bk, 8, o_sc), scalar=1.0, in1=vec(wname),
                                                         op0=ALU.add, op1=ALU.mult), p, m_vec)
            bfree[bk] = [m2]
            return sh, sc, m2

        for _ in ada_steps(0, acc_o, m_ab, m_zero, add=True):
            pass
        m_xs = rms(x_o, xs_o, [m_x] * 4, (), oatt, ())
        m_acc = ada_m[0]
        p = ada_cols(acc_o, 0, m_acc, None, 7, 0)
        p = ada_cols(acc_o, 1, m_acc, None, 7, 8)
        sh1, sc1, m_ss1 = scale_shift(7, 0, 8, p, "nmw")
        ada_free[0] = p
        m_hT = turn(xs_o, m_xs, lambda k: at(hT + 512 * k, 512), lambda k: at(sc1 + k, 1), lambda k: at(sh1 + k, 1), [m_ss1], (), [0, 1, 2, 3])
        hTk = lambda k: at(hT + 512 * k, 512)
        p_turn = (pe.name, pe.count)

        dbank = [0]

        def next_bank(banks):
            dbank[0] += 1
            return banks[dbank[0] % len(banks)]

        def dense_T(bk, c, j, rhs, marks, nk=8, off=0, release=True):
            for k in range(nk):
                f = lambda e, k=k: e.matmul(bank(bk), c.ap[:, off + k, 128 * j:128 * j + 128], rhs(k),
                                            start=(k == 0), stop=(k == nk - 1))
                mk = [c.mark, marks[k]] + (bfree[bk] if k == 0 else [])
                if k < nk - 1:
                    pe.quiet(f, *mk)
                else:
                    p = pe.do(f, *mk)
            if release:
                c.released = p
            return p

        def dense_tok(bk, c, tc, n, lhs, marks, o=0):
            for k in range(8):
                f = lambda e, k=k: e.matmul(bank(bk, n, o), lhs(k, tc), c.ap[:, k, 0:n], start=(k == 0), stop=(k == 7))
                mk = [c.mark, marks[k]] + (bfree[bk] if k == 0 else [])
                if k < 7:
                    pe.quiet(f, *mk)
                else:
                    p = pe.do(f, *mk)
            c.released = p
            return p

        hT_lhs = lambda k, tc: at(hT + 512 * k + 128 * tc, 128)
        w_in = t["w_in"]
        DB = [0, 1]
        tmp_free = {i: None for i in range(4)}
        ti = [0]

        def tmp_get():
            i = ti[0] % 4
            ti[0] += 1
            return i, tmp + 512 * i

        hg_free = {"QQ": [p_turn], "KK": [p_turn], "TTa": [p_turn], "TTb": [p_turn], "q0": [p_turn], "PT": [p_turn],
                   "V": [p_turn], "sgh": [p_turn]}
        st = {}

        def hg_proj(pr):
            q_m, f_m, k_m = [None] * 2, {}, {}
            c = col_chunk(w_in, 3 + pr)
            for j in range(2):
                bk = next_bank(DB)
                p = dense_T(bk, c, j, hTk, m_hT)
                i, o = tmp_get()
                a = act.do(lambda e, bk=bk, o=o: e.activation(at(o, 512), bank(bk), ACT.Sigmoid), p, tmp_free[i])
                q_m[j] = dve.do(lambda e, bk=bk, o=o, j=j: e.tensor_tensor(at(q0 + 512 * j, 512), at(o, 512), bank(bk), ALU.mult),
                                a, *hg_free["q0"])
                bfree[bk] = [q_m[j]]
                tmp_free[i] = q_m[j]
                yield
            for dr in range(2):
                c = col_chunk(w_in, 5 + 2 * dr + pr)
                for j in range(2):
                    bk = next_bank(DB)
                    p = dense_T(bk, c, j, hTk, m_hT)
                    v = 4 * dr + 2 * pr + j
                    to = TTa + 1024 * (1 - dr) + 512 * j
                    ko = KK + 1024 * dr + 512 * j
                    qo = QQ + 1024 * (1 - dr) + 512 * j
                    a1 = act.do(lambda e, bk=bk, to=to: e.activation(at(to, 512), bank(bk), ACT.Sigmoid), p, *hg_free["TTa"])
                    a2 = act.do(lambda e, bk=bk, ko=ko: e.activation(at(ko, 512), bank(bk), ACT.Sigmoid, scale=-1.0),
                                *hg_free["KK"])
                    bfree[bk] = [a2]
                    b = dve.do(lambda e, to=to, v=v: e.tensor_scalar(at(to, 512), at(to, 512), at(oml + v, 1), at(lbv + v, 1),
                                                                     ALU.mult, ALU.add), a1, m_lb)
                    b = dve.do(lambda e, to=to: e.tensor_scalar(at(to, 512), at(to, 512), 1e-6, None, ALU.max), b)
                    f_m[dr, j] = b
                    k_m[dr, j] = dve.do(lambda e, ko=ko, v=v: e.tensor_scalar(at(ko, 512), at(ko, 512), at(oml + v, 1), None, ALU.mult), a2)
                    st["q1"] = dve.do(lambda e, qo=qo, to=to, j=j: e.tensor_tensor(at(qo, 512), at(q0 + 512 * j, 512), at(to, 512), ALU.mult),
                                      b, q_m[j], *hg_free["QQ"])
                    yield
            c = col_chunk(w_in, 9 + pr)
            for h in range(2):
                bk = next_bank(DB)
                for tc in (2 * h, 2 * h + 1):
                    p = dense_tok(bk, c, tc, 256, hT_lhs, m_hT, 256 * (tc % 2))
                m = act.do(lambda e, bk=bk, h=h: e.activation(at(Vp + 512 * h, 512), bank(bk), ACT.Copy), p, *hg_free["V"])
                bfree[bk] = [m]
                st["v"] = m
                yield

        def hg_gate(pr, banks):
            c = col_chunk(w_in, 11 + pr)
            for j in range(2):
                bk = next_bank(banks)
                p = dense_T(bk, c, j, hTk, m_hT)
                i, o = tmp_get()
                a = act.do(lambda e, bk=bk, o=o: e.activation(at(o, 512), bank(bk), ACT.Sigmoid), p, tmp_free[i])
                m = dve.do(lambda e, bk=bk, o=o, j=j: e.tensor_tensor(at(sgh + 512 * j, 512), at(o, 512), bank(bk), ALU.mult),
                           a, *hg_free["sgh"])
                bfree[bk] = [m]
                tmp_free[i] = m
                st["sgh"] = m
                yield

        gates = {}

        def branch_gates(n):
            s = slots[pos[0] % len(slots)]
            i = slots.index(s)
            slots[:], pos[0] = slots[i + 1:] + slots[:i], 0
            kept[:] = [s]
            rooms = [ring_o[s] + 512 * i for i in range(4)] + [tmp + 512 * i for i in range(4)]
            fr = [last_user[s].released] * 4 + [None] * 4
            for half in range(n):
                for br in range(2):
                    c = col_chunk(w_in, 13 + 4 * br + half)
                    for j in range(2):
                        x = 4 * half + 2 * br + j
                        for k in range(KD):
                            f = lambda e, c=c, j=j, k=k: e.matmul(bank(2), c.ap[:, k, 128 * j:128 * j + 128], hTk(k),
                                                                  start=(k == 0), stop=(k == KD - 1))
                            if k < KD - 1:
                                pe.quiet(f, c.mark, m_hT[k], *bfree[2])
                            else:
                                c.released = p = pe.do(f, m_hT[k])
                            if k in (1, 3, 5):
                                yield
                        a = act.do(lambda e, o=rooms[x]: e.activation(at(o, 512), bank(2), ACT.Sigmoid), p,
                                   fr[x] if x < 4 else tmp_free[x - 4])
                        bfree[2] = [a]
                        gates[2 * half + j, br] = (rooms[x], a)
                        yield

        kept = []

        def level_mask(li):
            return raw(o_cst + CST["lev"][0] + 128 * li, [(0, 4), (1, 128)]).bitcast(mybir.dt.uint32)

        def hg_levels(pr, HB):
            state = st["q1"]
            diag = lambda hh: raw(PT + 2048 * hh, [(640, 4), (1, 128)])
            pt_m = [None] * 2
            for hh in range(2):
                bk = next_bank(HB)
                for c in range(TC):
                    o = 512 * hh + 128 * c
                    pe.quiet(lambda e, bk=bk, c=c, o=o: e.matmul(bank(bk, 128, 128 * c), at(KK + o, 128), at(q0 + o, 128),
                                                                 start=True, stop=False), state, *bfree[bk])
                    p = pe.do(lambda e, bk=bk, c=c, o=o: e.matmul(bank(bk, 128, 128 * c), at(KK + 1024 + o, 128), at(q0 + o, 128),
                                                                  start=False, stop=True))
                pt_m[hh] = act.do(lambda e, bk=bk, hh=hh: e.activation(
                    diag(hh), bank(bk).rearrange("p (c i) -> p c i", c=4), ACT.Copy), p, *hg_free["PT"])
                bfree[bk] = [pt_m[hh]]
            hg_free["q0"] = [p]
            pm, kc = [None] * 2, None
            tcur, tnext = TTa, TTb
            tn = 1024
            yield
            for li, h in enumerate(LEVELS + (128, 256)):
                if h <= 64:
                    kc = act.do(lambda e, h=h: e.activation(
                        raw(KC, [(h, 2), (2 * h, 512 // h), (1, h)]),
                        raw(KK, [(1024 + h, 2), (2 * h, 512 // h), (1, h)]), ACT.Copy), state, st.get("kc"))
                    bks = []
                    for hh in range(2):
                        bk = next_bank(HB)
                        bks.append((hh, bk))
                        for c in range(TC):
                            o = 512 * hh + 128 * c
                            dims = [(2 * h, 64 // h), (1024 + h, 2), (1, h)]
                            f = lambda e, bk=bk, c=c, o=o, dims=dims: e.matmul(
                                bank(bk, 128, 128 * c), at(KC + o, 128), raw(QQ + o, dims), start=True, stop=True)
                            if c < 3:
                                pe.quiet(f, kc, *(bfree[bk] if c == 0 else ()))
                            else:
                                p = st["kc"] = pe.do(f)
                        pm[hh] = p
                elif h == 128:
                    for hh in range(2):
                        bk = next_bank(HB)
                        for c in range(TC):
                            ic = c ^ 1
                            ko = KK + 1024 * (c & 1) + 512 * hh + 128 * c
                            qo = QQ + 1024 * (1 - (c & 1)) + 512 * hh + 128 * ic
                            f = lambda e, bk=bk, c=c, ko=ko, qo=qo: e.matmul(
                                bank(bk, 128, 128 * c), at(ko, 128), at(qo, 128), start=True, stop=True)
                            if c < 3:
                                pe.quiet(f, state, *(bfree[bk] if c == 0 else ()))
                            else:
                                p = pe.do(f, state)
                        for par in range(2):
                            m = act.do(lambda e, bk=bk, hh=hh, par=par: e.activation(
                                raw(PT + 2048 * hh + (128, 512)[par], [(1280, 2), (1, 128)]),
                                raw_ps(bk, 128 * par, [(256, 2), (1, 128)]), ACT.Copy), p, *hg_free["PT"])
                        bfree[bk] = [m]
                else:
                    for hh in range(2):
                        for dr in range(2):
                            bk = next_bank(HB)
                            for n in range(2):
                                c = 2 * dr + n
                                ko = KK + 1024 * dr + 512 * hh + 128 * c
                                qo = QQ + 1024 * (1 - dr) + 512 * hh + 256 * (1 - dr)
                                p = pe.do(lambda e, bk=bk, n=n, ko=ko, qo=qo: e.matmul(
                                    bank(bk, 256, 256 * n), at(ko, 128), at(qo, 256), start=True, stop=True),
                                    state, *(bfree[bk] if n == 0 else ()))
                            m = act.do(lambda e, bk=bk, hh=hh, dr=dr: e.activation(
                                raw(PT + 2048 * hh + 1024 * dr + 256 * (1 - dr), [(512, 2), (1, 256)]),
                                bank(bk).rearrange("p (n i) -> p n i", n=2), ACT.Copy), p, *hg_free["PT"])
                            bfree[bk] = [m]
                        st["pt", hh] = [m, pt_m[hh]]
                    hg_free["QQ"] = hg_free["KK"] = [p]
                if h < 256:
                    nb = 1024 // (2 * h)
                    own = state if h == 1 else st["t"]
                    d1 = dve.do(lambda e, h=h, nb=nb, tcur=tcur, tn=tn: e.tensor_tensor(
                        raw(QQ, [(1024 + h, 2), (2 * h, nb), (1, h)]), raw(QQ, [(1024 + h, 2), (2 * h, nb), (1, h)]),
                        raw(tcur + 1, [(tn - 1, 2), (2, nb), (0, h)]), ALU.mult), p, own, state, kc)
                    d2 = dve.do(lambda e, h=h, nb=nb, tcur=tcur, tn=tn: e.tensor_tensor(
                        raw(KK, [(2 * h, nb), (1, h)]), raw(KK, [(2 * h, nb), (1, h)]),
                        raw(tcur + tn + 1, [(2, nb), (0, h)]), ALU.mult))
                    d3 = dve.do(lambda e, h=h, nb=nb, tcur=tcur, tn=tn: e.tensor_tensor(
                        raw(KK + 1024 + h, [(2 * h, nb), (1, h)]), raw(KK + 1024 + h, [(2 * h, nb), (1, h)]),
                        raw(tcur, [(2, nb), (0, h)]), ALU.mult))
                    state = d3
                    if h < 128:
                        st["t"] = dve.do(lambda e, tcur=tcur, tnext=tnext, tn=tn: e.tensor_tensor(
                            at(tnext, tn), raw(tcur, [(2, tn)]), raw(tcur + 1, [(2, tn)]), ALU.mult), own,
                            *(hg_free["TTb"] if h == 1 else ()))
                        tcur, tnext, tn = tnext, tcur, tn // 2
                    else:
                        hg_free["TTa"] = hg_free["TTb"] = [d3]
                if h <= 64:
                    for hh, bk in bks:
                        pt_m[hh] = dve.do(lambda e, bk=bk, hh=hh, li=li: e.copy_predicated(
                            diag(hh), level_mask(li),
                            bank(bk).rearrange("p (c i) -> p c i", c=4)), pm[hh], pt_m[hh], m_cst)
                        bfree[bk] = [pt_m[hh]]
                yield

        def raw_ps(bk, o, dims):
            b = PS[:, bk, o:o + 1]
            return bass.AP(b.tensor, b.offset, [b.ap[0]] + [list(d) for d in dims])

        ohg_m = [None] * 4
        hgt = wk.take(1024)
        KC = wk.take(1024)

        def hg_out(pr, HB):
            for hh in range(2):
                bk, bk2 = next_bank(HB), next_bank(HB)
                for jc in range(TC):
                    f = lambda e, bk=bk, jc=jc, hh=hh: e.matmul(bank(bk), at(Vp + 256 * jc + 128 * hh, 128),
                                                                at(PT + 2048 * hh + 512 * jc, 512), start=(jc == 0), stop=(jc == 3))
                    if jc < 3:
                        pe.quiet(f, st["v"], *st["pt", hh], *bfree[bk])
                    else:
                        p = pe.do(f)
                hg_free["PT"], hg_free["V"] = [p], [p]
                yield
                o = ohg + 512 * (2 * pr + hh)
                a = act.do(lambda e, bk=bk: e.activation(at(hgt, 512), bank(bk), ACT.Square), p, st.get("hgt"), st.get("hgt2"))
                p2 = pe.do(lambda e, bk2=bk2: e.matmul(bank(bk2), cst("o128"), at(hgt, 512), start=True, stop=True), a, *bfree[bk2])
                a2, b = rsqrt_tile(at(hgt + 512, 512), bank(bk2), "eps6", p2, st.get("hgt"))
                bfree[bk2] = [a2]
                b = dve.do(lambda e, bk=bk, o=o: e.scalar_tensor_tensor(out=at(o, 512), in0=bank(bk), scalar=vcol("hgw", 0),
                                                                        in1=at(hgt + 512, 512), op0=ALU.mult, op1=ALU.mult), b, p)
                bfree[bk] = [b]
                st["hgt"] = b
                st["hgt2"] = p2
                ohg_m[2 * pr + hh] = dve.do(lambda e, o=o, hh=hh: e.tensor_tensor(at(o, 512), at(o, 512), at(sgh + 512 * hh, 512), ALU.mult),
                                            b, st["sgh"])
                hg_free["sgh"] = [ohg_m[2 * pr + hh]]
                yield

        q_marks, kd_marks = [None] * 4, [None] * 2

        def head_norm(bk, p, wcol, put):
            i, o = tmp_get()
            i2, o2 = tmp_get()
            a = act.do(lambda e: e.activation(at(o, 512), bank(bk), ACT.Square), p, tmp_free[i])
            b2 = next_bank(AB)
            p2 = pe.do(lambda e: e.matmul(bank(b2), cst("bo64"), at(o, 512), start=True, stop=True), a, *bfree[b2])
            a2, b = rsqrt_tile(at(o, 512), bank(b2), "eps6", p2)
            bfree[b2] = [a2]
            b = dve.do(lambda e: e.scalar_tensor_tensor(out=at(o2, 512), in0=bank(bk), scalar=wcol, in1=at(o, 512),
                                                        op0=ALU.mult, op1=ALU.mult), b, tmp_free[i2], p)
            bfree[bk] = [b]
            b3 = next_bank(AB)
            p3 = pe.do(lambda e: e.matmul(bank(b3), cst("rot"), at(o2, 512), start=True, stop=True), b, *bfree[b3])
            r = dve.do(lambda e: e.tensor_tensor(at(o, 512), bank(b3), cst("ropes"), ALU.mult), p3)
            bfree[b3] = [r]
            g = pool.do(lambda e: e.tensor_tensor(at(o2, 512), at(o2, 512), cst("ropec"), ALU.mult), b, p3, m_cst)
            m = put(o, o2, r, g)
            tmp_free[i] = tmp_free[i2] = m

        AB = [4, 5]

        def at_proj():
            for n in range(2):
                c = col_chunk(w_in, n)
                for j in range(2):
                    bk = next_bank(DB)
                    p = dense_T(bk, c, j, hTk, m_hT)
                    yield
                    q = 2 * n + j

                    def put(o, o2, r, g, q=q):
                        q_marks[q] = dve.do(lambda e: e.tensor_tensor(at(qT + 512 * q, 512), at(o, 512), at(o2, 512), ALU.add), r, g, p_turn)
                        return q_marks[q]
                    head_norm(bk, p, vcol("qn", 0), put)
                    yield
            c = col_chunk(w_in, 2)
            bk = next_bank(DB)
            p = dense_T(bk, c, 0, hTk, m_hT)

            def put(o, o2, r, g):
                b = dve.do(lambda e: e.tensor_tensor(at(o2, 512), at(o, 512), at(o2, 512), ALU.add), r, g, p_turn)
                for kv in range(2):
                    for half in range(2):
                        m = act.do(lambda e, kv=kv, half=half: e.activation(
                            A[64 * half:64 * half + 64, kd + 512 * kv:kd + 512 * kv + 512],
                            A[64 * kv:64 * kv + 64, o2:o2 + 512], ACT.Copy), b)
                    kd_marks[kv] = m
                return m
            head_norm(bk, p, vcol("kn", 0), put)
            yield
            bk = next_bank(DB)
            for tc in range(TC):
                for k in range(8):
                    f = lambda e, k=k, tc=tc, bk=bk, c=c: e.matmul(bank(bk, 128, 128 * tc), hT_lhs(k, tc), c.ap[:, k, 128:256],
                                                                   start=(k == 0), stop=(k == 7))
                    if k < 7:
                        pe.quiet(f, m_hT[k], *bfree[bk])
                    else:
                        p = pe.do(f, m_hT[k])
            c.released = p
            st["va"] = act.do(lambda e, bk=bk: e.activation(at(va, 512), bank(bk), ACT.Copy), p, p_turn)
            bfree[bk] = [st["va"]]
            yield

        oatt_m = [None] * 4
        ast = small(4 * 8)

        def attention():
            pfree = [None] * 3
            SB = [3, 4, 5]
            ptfree = None
            steps = [(h, ic) for h in range(8) for ic in range(TC)]
            ready = {}
            pt_done = []

            def scores(n):
                h, ic = steps[n]
                g, po = h // 4, 64 * (h % 2)
                bk, P, so = SB[n % 3], Pb + 512 * (n % 3), ast + 4 * (n % 8)
                qo = qT + 512 * (h // 2) + 128 * ic
                p = pe.do(lambda e: e.matmul(bank(bk), A[po:po + 64, qo:qo + 128], A[po:po + 64, kd + 512 * g:kd + 512 * g + 512],
                                             start=True, stop=True), q_marks[h // 2], kd_marks[g], *bfree[bk])
                b = dve.do(lambda e: e.tensor_reduce(at(so, 1), bank(bk), AX, ALU.max), p)
                b = dve.do(lambda e: e.tensor_scalar(at(so + 1, 1), at(so, 1), -0.125, None, ALU.mult), b)
                a = act.do(lambda e: e.activation(at(P, 512), bank(bk), ACT.Exp, bias=at(so + 1, 1), scale=0.125,
                                                  accum_out=at(so + 2, 1)), b, pfree[n % 3])
                bfree[bk] = [a]
                b = dve.do(lambda e: e.reciprocal(at(so + 3, 1), at(so + 2, 1)), a)
                ready[n] = dve.do(lambda e: e.tensor_scalar(at(P, 512), at(P, 512), at(so + 3, 1), None, ALU.mult), b)

            scores(0)
            yield
            scores(1)
            yield
            for n, (h, ic) in enumerate(steps):
                g, po = h // 4, 64 * (h % 2)
                if n + 2 < len(steps):
                    scores(n + 2)
                    yield
                P = Pb + 512 * (n % 3)
                for jc in range(TC):
                    f = lambda e, P=P, jc=jc: e.transpose(bank(6, 128, 128 * jc), at(P + 128 * jc, 128), ident)
                    if jc < 3:
                        pe.quiet(f, ready[n], *bfree[6])
                    else:
                        p = pe.do(f)
                pfree[n % 3] = p
                m = act.do(lambda e, ic=ic: e.activation(raw(PTa + 128 * ic, [(512, 4), (1, 128)]),
                                                         bank(6).rearrange("p (j i) -> p j i", j=4), ACT.Copy), p, ptfree)
                bfree[6] = [m]
                pt_done.append(m)
                if ic < TC - 1:
                    continue
                yield
                for jc in range(TC):
                    f = lambda e, jc=jc, g=g, po=po: e.matmul(PS[po:po + 64, 7, :], at(va + 128 * jc + 64 * g, 64),
                                                              at(PTa + 512 * jc, 512), start=(jc == 0), stop=(jc == 3))
                    if jc < 3:
                        pe.quiet(f, st["va"], *pt_done, *(bfree[7] if h % 2 == 0 else ()))
                    else:
                        p = pe.do(f)
                ptfree = p
                pt_done = []
                if h % 2:
                    oatt_m[h // 2] = act.do(lambda e, h=h: e.activation(at(oatt + 512 * (h // 2), 512), bank(7), ACT.Copy), p, *m_xs)
                    bfree[7] = [oatt_m[h // 2]]

        def weave(*gens, until=None):
            gens = [g if isinstance(g, tuple) else (g, 1) for g in gens]
            while gens:
                for g in list(gens):
                    for _ in range(g[1]):
                        try:
                            next(g[0])
                        except StopIteration:
                            gens.remove(g)
                            if g[0] is until:
                                return
                            break

        def seq(*gens):
            for g in gens:
                yield from g

        weave(hg_proj(0))
        weave(seq(hg_levels(0, [2, 3, 6, 7]), hg_out(0, [2, 3, 6, 7])), seq(hg_gate(0, DB), at_proj()))
        att, hg = attention(), hg_proj(1)
        weave(hg, (att, 2), until=hg)
        lv, fill = seq(hg_levels(1, DB), hg_out(1, DB)), seq(hg_gate(1, [2]), branch_gates(2))
        weave(fill, lv, fill, att, fill, att, fill)

        mg = QQ
        MBK = [0, 1, 2, 3, 4, 5, 6, 7]
        mg_m = [None] * 8
        mt = [PT + 512 * i for i in range(8)]
        phase_m = [ohg_m[0], ohg_m[1], ohg_m[2], ohg_m[3]] + oatt_m
        hg_end = hg_free["QQ"] + hg_free["PT"] + hg_free["TTa"] + hg_free["q0"]
        acc2 = TTa
        m_ab = load(act, A[0:1, adab_o:adab_o + 2048], t["ada_b"][:, 2048:4096], "l_ab", *oatt_m, (pe.name, pe.count))
        sh2, sc2 = small(8), small(8)

        def modulation(m_ab):
            yield from ada_steps(1, acc2, *hg_end)
            _, m_gate1 = ada_row(acc2, 0, ada_m[0], m_ab, gate1_o)
            p = ada_cols(acc2, 1, ada_m[0], m_ab, 7, 0)
            ada_free[0] = p
            m_shift = dve.do(lambda e: e.tensor_copy(at(sh2, 8), bank(7, 8)), p)
            bfree[7] = [m_shift]
            m_ab = load(act, A[0:1, adab_o:adab_o + 2048], t["ada_b"][:, 4096:6144], "l_ab", p)
            yield from ada_steps(2, acc2)
            p = ada_cols(acc2, 0, ada_m[0], m_ab, 7, 0)
            m_scale = dve.do(lambda e: e.scalar_tensor_tensor(out=at(sc2, 8), in0=bank(7, 8), scalar=1.0, in1=vec("nfw"),
                                                              op0=ALU.add, op1=ALU.mult), p, m_vec)
            bfree[7] = [m_scale]
            p, m_gate2 = ada_row(acc2, 1, ada_m[0], m_ab, gate2_o)
            return m_gate1, m_shift, m_scale, p, m_gate2

        mod = modulation(m_ab)

        def mod_step():
            try:
                next(mod)
            except StopIteration as end:
                return end.value

        for half in range(4):
            if half >= 2:
                c0 = col_chunk(w_in, 13 + half)
                c1 = col_chunk(w_in, 17 + half)
            cols = slice(256 * half, 256 * half + 256)
            cb = chunk([t[n][:, cols].rearrange("(k p) n -> p k n", p=128) for n in ("w_branch_att", "w_branch_hg")], (8, 256))
            for j in range(2):
                d = 2 * half + j
                bb = [4 * (d % 2) + i for i in range(4)]
                fr = hg_end if d < 2 else ()
                if half < 2:
                    (s0, a0), (s1, a1) = gates[d, 0], gates[d, 1]
                else:
                    s0, s1 = mt[4 * (d % 2)], mt[4 * (d % 2) + 1]
                    p0 = dense_T(bb[0], c0, j, hTk, m_hT)
                    a0 = act.do(lambda e, s0=s0, b=bb[0]: e.activation(at(s0, 512), bank(b), ACT.Sigmoid), p0, *hg_end, mg_m[d - 2])
                    bfree[bb[0]] = [a0]
                    p1 = dense_T(bb[1], c1, j, hTk, m_hT)
                    a1 = act.do(lambda e, s1=s1, b=bb[1]: e.activation(at(s1, 512), bank(b), ACT.Sigmoid), p1, mg_m[d - 2])
                    bfree[bb[1]] = [a1]
                p2 = dense_T(bb[2], cb, j, lambda k: at(oatt + 512 * k, 512), oatt_m, nk=4)
                b2 = dve.do(lambda e, s0=s0, b=bb[2]: e.tensor_tensor(at(s0, 512), at(s0, 512), bank(b), ALU.mult), p2, a0)
                bfree[bb[2]] = [b2]
                p3 = dense_T(bb[3], cb, j, lambda k: at(ohg + 512 * k, 512), ohg_m, nk=4, off=4)
                b3 = dve.do(lambda e, s1=s1, b=bb[3]: e.tensor_tensor(at(s1, 512), at(s1, 512), bank(b), ALU.mult), p3, a1)
                bfree[bb[3]] = [b3]
                mg_m[d] = dve.do(lambda e, s0=s0, s1=s1, d=d: e.tensor_tensor(at(mg + 512 * d, 512), at(s0, 512), at(s1, 512), ALU.add),
                                 b2, b3, *fr)
                for _ in range(1 if half < 2 else 3):
                    mod_step()
        m_g1, m_sh2, m_sc2, p_ada, m_g2 = mod_step()

        slot_free[kept[0]] = (mg_m[3],)
        slots.insert((pos[0] - 1) % len(slots) + 1, kept[0])
        pos[0] = slots.index(kept[0])
        p_branch = (pe.name, pe.count)

        def residual_out(w, lhs, marks, X, xm, gate, gate_m, tmps, t_free, banks, then):
            cs = [col_chunk(w, n) for n in range(4)]
            for h in range(2):
                for n, c in enumerate(cs):
                    bk = next_bank(banks)
                    for tc in (2 * h, 2 * h + 1):
                        p = dense_tok(bk, c, tc, 256, lhs, marks, 256 * (tc % 2))
                    xa = raw(X + 2048 * h + 256 * n, [(1024, 2), (1, 256)])
                    pv = bank(bk).rearrange("p (a n) -> p a n", a=2)
                    if gate is None:
                        m = dve.do(lambda e, xa=xa, pv=pv: e.tensor_tensor(xa, xa, pv, ALU.add), p, *xm)
                        bfree[bk] = [m]
                    else:
                        i = n % 2
                        ta = at(tmps + 512 * i, 512).rearrange("p (a n) -> p a n", a=2)
                        b = dve.do(lambda e, ta=ta, pv=pv, n=n: e.tensor_tensor(
                            ta, pv, raw(gate + 256 * n, [(0, 2), (1, 256)]), ALU.mult), p, gate_m, t_free[i])
                        bfree[bk] = [b]
                        m = dve.do(lambda e, xa=xa, ta=ta: e.tensor_tensor(xa, xa, ta, ALU.add), b, *xm)
                        t_free[i] = m
                then(h, m)

        X = qT
        assert X + 4096 <= oatt
        m_x2 = load(act, at(X, 4096).rearrange("p (c d) -> p c d", c=4), xv, "l_x", *oatt_m, (pe.name, pe.count))
        mg_lhs = lambda k, tc: at(mg + 512 * k + 128 * tc, 128)
        w1 = Work(hT)
        xs2 = w1.take(4096)
        h2T = w1.take(4096)
        assert w1.o <= X
        m_X, m_xs2 = [], []

        def first_norm(h, m):
            m_X.extend([m, m])
            m_xs2.extend(rms(X, xs2, [m] * 4, [p_branch], oatt, [p_branch], (2 * h, 2 * h + 1)))

        residual_out(t["w_out"], mg_lhs, mg_m, X, [m_x2] * 4, gate1_o, m_g1, PT, [mg_m[7], mg_m[7]], [0, 1, 2, 3, 4, 5], first_norm)
        p_wout = (pe.name, pe.count)

        lg, aff, rst = small(64), small(64), small(16)
        m_h2 = []

        def logits(k):
            p = None
            for tc in range(TC):
                f = lambda e, tc=tc: e.matmul(bank(4 + tc, 16), at(h2T + 512 * k + 128 * tc, 128),
                                              at(o_vec + VEC["wr"][0] + 16 * k, 16), start=(k == 0), stop=(k == KD - 1))
                if (k, tc) != (KD - 1, TC - 1):
                    pe.quiet(f, m_h2[k], *(bfree[4 + tc] if k == 0 else ()))
                else:
                    p = pe.do(f, m_h2[k])
            return p

        def behind(k, m):
            m_h2.append(m)
            if k >= 2:
                logits(k - 2)

        turn(xs2, m_xs2, lambda k: at(h2T + 512 * k, 512), lambda k: at(sc2 + k, 1), lambda k: at(sh2 + k, 1), [m_sc2, m_sh2], [p_wout],
             [0, 1, 2, 3], behind)
        logits(KD - 2)
        p_lg = p = logits(KD - 1)
        lg_ps = PS[:, 4:8, 0:16]
        r3 = lambda o: at(o, 64).rearrange("p (c e) -> p c e", c=4)
        r16 = lambda o: raw(o, [(1, 4), (0, 16)])
        b = dve.do(lambda e: e.tensor_reduce(at(rst, 4), lg_ps, AX, ALU.max), p)
        b = dve.do(lambda e: e.tensor_tensor(r3(lg), lg_ps, r16(rst), ALU.subtract), b)
        for i in range(4, 8):
            bfree[i] = [b]
        a = act.do(lambda e: e.activation(at(lg, 64), at(lg, 64), ACT.Exp), b)
        b = dve.do(lambda e: e.tensor_reduce(at(rst + 4, 4), r3(lg), AX, ALU.add), a)
        b = dve.do(lambda e: e.reciprocal(at(rst + 8, 4), at(rst + 4, 4)), b)
        m_aff = dve.do(lambda e: e.tensor_tensor(r3(aff), r3(lg), r16(rst + 8), ALU.mult), b)
        w2 = Work(X + 4096)
        affT, wkT, m8, mskT = w2.take(512), w2.take(512), small(8), small(64)
        for tc in range(TC):
            f = lambda e, tc=tc: e.transpose(PS[0:16, 5, 128 * tc:128 * tc + 128], at(aff + 16 * tc, 16), ident)
            if tc < 3:
                pe.quiet(f, m_aff, *bfree[5], *m_xs2)
            else:
                p = pe.do(f)
        m = dve.do(lambda e: e.tensor_copy(A[0:16, affT:affT + 512], PS[0:16, 5, :]), p, *m_xs2)
        bfree[5] = [m]
        for r in range(CAP // 8):
            src = affT if r % 2 == 0 else wkT
            dst = wkT if r % 2 == 0 else affT
            m = dve.do(lambda e, src=src: e.max(A[0:16, m8:m8 + 8], A[0:16, src:src + 512]), m)
            m = dve.do(lambda e, src=src, dst=dst: e.match_replace(A[0:16, dst:dst + 512], A[0:16, m8:m8 + 8],
                                                                   A[0:16, src:src + 512], -1.0), m)
        m = dve.do(lambda e: e.tensor_scalar(A[0:16, wkT:wkT + 512], A[0:16, affT:affT + 512], 0.0, None, ALU.is_lt), m)
        for tc in range(TC):
            f = lambda e, tc=tc: e.transpose(bank(5, 16, 16 * tc), A[0:16, wkT + 128 * tc:wkT + 128 * tc + 128],
                                             A[0:16, o_cst:o_cst + 16])
            if tc < 3:
                pe.quiet(f, m, *bfree[5])
            else:
                p = pe.do(f)
        m_msk = dve.do(lambda e: e.tensor_copy(at(mskT, 64), bank(5, 64)), p)
        bfree[5] = [m_msk]
        for tc in range(TC):
            for c in range(tc + 1):
                f = lambda e, tc=tc, c=c: e.matmul(bank(4, 16, 16 * tc), tri if c == tc else ones, at(mskT + 16 * c, 16),
                                                   start=(c == 0), stop=(c == tc))
                if c < tc:
                    pe.quiet(f, m_msk, *bfree[4])
                else:
                    p = pe.do(f, m_msk, *bfree[4])
        posf = small(64)
        b = dve.do(lambda e: e.scalar_tensor_tensor(out=at(posf, 64), in0=bank(4, 64), scalar=1.0, in1=at(mskT, 64),
                                                    op0=ALU.add, op1=ALU.mult), p, m_msk)
        bfree[4] = [b]
        m_pos = dve.do(lambda e: e.tensor_scalar(at(posf, 64), at(posf, 64), -1.0, None, ALU.add), b)
        route_end = [m_pos, p]

        w1 = Work(xs2 + 4096)
        sg, hid = w1.take(2048), w1.take(2048)
        oldest = pos[0] % len(slots)
        old = slots[oldest:] + slots[:oldest]
        for _ in range((X - w1.o) // W):
            add_slot(w1.take(W), [p_wout, p_ada, *m_X])
        assert w1.o <= X
        w2 = Work(X + 4096)
        xeT = [w2.take(512), w2.take(512)]
        hidT = [w2.take(1024), w2.take(1024)]
        YE = w2.take(1024)
        OH = [w2.take(256), w2.take(256)]
        OHW = w2.take(512)
        OHWT = w2.take(512)
        while w2.o + W <= AR:
            add_slot(w2.take(W), [p_branch])
        n_w1 = (X - xs2 - 8192) // W
        slots[:] = slots[NR0 + n_w1:] + old + slots[NR0:NR0 + n_w1]
        pos[0] = 0
        xe_free, oh_free, hid_free, hidT_free = [None] * 2, [None] * 2, list(route_end), [None] * 2
        ohw_free, ohwt_free, ye_free, ct_free = None, None, None, [None] * 2
        iota = cst("iota")
        sg_free = list(route_end) + m_h2 + [p_lg]
        one_hot = {}
        xe_m = {}

        def gather(ex):
            nonlocal ohw_free
            z = ex % 2
            for c in range(TC):
                b = dve.do(lambda e, c=c: e.tensor_scalar(
                    at(OH[z] + 64 * c, 64), iota, at(posf + 16 * c + ex, 1), None, ALU.is_equal), m_pos, oh_free[z], *route_end)
            for k in range(KD):
                for c in range(TC):
                    bk = 5 - k // 4
                    f = lambda e, k=k, c=c, bk=bk: e.matmul(bank(bk, 64, 64 * (k % 4)), at(xs2 + 1024 * c + 128 * k, 128),
                                                            at(OH[z] + 64 * c, 64), start=(c == 0), stop=(c == 3))
                    if (k % 4, c) != (3, 3):
                        pe.quiet(f, b, *bfree[bk])
                    else:
                        p = pe.do(f)
                        if k == 3:
                            p5 = p
            oh_free[z] = p
            xe_m[ex] = []
            for k in range(KD):
                if k >= 4:
                    m = dve.do(lambda e, k=k: e.tensor_scalar(at(xeT[z] + 64 * k, 64), bank(4, 64, 64 * (k - 4)), at(sc2 + k, 1),
                                                              at(sh2 + k, 1), ALU.mult, ALU.add), p, xe_free[z], *route_end)
                    bfree[4] = [m]
                else:
                    m = act.do(lambda e, k=k: e.activation(at(xeT[z] + 64 * k, 64), bank(5, 64, 64 * k), ACT.Identity,
                                                           bias=at(sh2 + k, 1), scale=at(sc2 + k, 1)), p5, xe_free[z], *route_end)
                    bfree[5] = [m]
                xe_m[ex].append(m)
            for c in range(TC):
                one_hot[ex] = dve.do(lambda e, c=c: e.tensor_scalar(
                    at(OHW + 128 * c + 64 * z, 64), iota, at(posf + 16 * c + ex, 1), at(aff + 16 * c + ex, 1),
                    ALU.is_equal, ALU.mult), ohw_free, *route_end)
            if z == 1:
                for c in range(TC):
                    f = lambda e, c=c: e.transpose(bank(5, 128, 128 * c), at(OHW + 128 * c, 128), ident)
                    if c < 3:
                        pe.quiet(f, one_hot[ex], *bfree[5])
                    else:
                        p = pe.do(f)
                ohw_free = p
                one_hot["T"] = act.do(lambda e: e.activation(at(OHWT, 512), bank(5), ACT.Copy), p, ohwt_free, *route_end)
                bfree[5] = [one_hot["T"]]

        def combine(ym):
            for tc in range(TC):
                for dh in range(2):
                    bk = 6 + dh
                    p = pe.do(lambda e, tc=tc, dh=dh, bk=bk: e.matmul(
                        bank(bk), at(OHWT + 128 * tc, 128), at(YE + 512 * dh, 512), start=True, stop=True),
                        one_hot["T"], *ym, *bfree[bk])
                    xa = at(X + 1024 * tc + 512 * dh, 512)
                    m = dve.do(lambda e, xa=xa, bk=bk: e.tensor_tensor(xa, xa, bank(bk), ALU.add), p, *m_xs2)
                    bfree[bk] = [m]
                    m_X[tc] = m
            return p

        gather(0)
        ym = pending = None
        for ex in range(NE):
            z = ex % 2
            for k in range(KD):
                cg = chunk(t["w_exp_gate"][ex, k * 128:(k + 1) * 128, :], (1, 2048))
                cu = chunk(t["w_exp_up"][ex, k * 128:(k + 1) * 128, :], (1, 2048))
                for fb in range(4):
                    for gu, c in ((0, cg), (1, cu)):
                        f = lambda e, gu=gu, c=c, fb=fb, k=k, z=z: e.matmul(
                            PS[64 * gu:64 * gu + 64, fb, :], at(xeT[z] + 64 * k, 64), c.ap[:, 512 * fb:512 * fb + 512],
                            start=(k == 0), stop=(k == 7))
                        if fb == 3:
                            c.released = pe.do(f, c.mark, xe_m[ex][k], *(bfree[fb] if k == 0 else ()))
                        else:
                            pe.quiet(f, c.mark, xe_m[ex][k], *(bfree[fb] if k == 0 else ()))
                if k == 3 and pending:
                    ohwt_free = ye_free = combine(pending)
                    pending = None
            p = (pe.name, pe.count)
            xe_free[z] = p
            hg = []
            for fb in range(4):
                a = act.do(lambda e, fb=fb: e.activation(A[64:128, sg + 512 * fb:sg + 512 * fb + 512], PS[0:64, fb, :], ACT.Silu),
                           p, *sg_free)
                m = dve.do(lambda e, fb=fb: e.tensor_tensor(
                    A[64:128, hid + 512 * fb:hid + 512 * fb + 512], A[64:128, sg + 512 * fb:sg + 512 * fb + 512],
                    PS[64:128, fb, :], ALU.mult), a, p, *hid_free)
                bfree[fb] = [m]
                hg.append(m)
            sg_free = [m]
            if ex + 1 < NE:
                gather(ex + 1)
            for fb in range(4):
                bk = 6 + fb % 2
                for q in range(4):
                    f = lambda e, fb=fb, q=q, bk=bk: e.transpose(
                        bank(bk, 64, 64 * q), A[64:128, hid + 512 * fb + 128 * q:hid + 512 * fb + 128 * q + 128],
                        A[64:128, o_cst + 64:o_cst + 128])
                    if q < 3:
                        pe.quiet(f, hg[fb], *bfree[bk])
                    else:
                        pt = pe.do(f)
                hm = act.do(lambda e, fb=fb, bk=bk, z=z: e.activation(at(hidT[z] + 256 * fb, 256), bank(bk, 256), ACT.Copy),
                            pt, hidT_free[z], *route_end)
                bfree[bk] = [hm]
            hid_free = [pt]
            for n in range(8):
                cd = chunk(t["w_exp_down"][ex, n * 256:(n + 1) * 256, :].rearrange("(k p) n -> p k n", p=128), (2, 1024))
                for k in range(2):
                    for dh in range(2):
                        f = lambda e, n=n, k=k, dh=dh, cd=cd, z=z: e.matmul(
                            PS[64 * dh:64 * dh + 64, 4, :], at(hidT[z] + 64 * (2 * n + k), 64), cd.ap[:, k, 512 * dh:512 * dh + 512],
                            start=(n + k == 0), stop=(n + k == 8))
                        if (k, dh) == (1, 1):
                            p = cd.released = pe.do(f, cd.mark, hm, *bfree[4])
                        else:
                            pe.quiet(f, cd.mark, hm, *bfree[4])
            hidT_free[z] = p
            if z == 0:
                ym = []
            for dh in range(2):
                ym.append(dve.do(lambda e, dh=dh, z=z: e.tensor_tensor(
                    A[64 * z:64 * z + 64, YE + 512 * dh:YE + 512 * dh + 512], PS[64 * dh:64 * dh + 64, 4, :],
                    A[64 * dh:64 * dh + 64, gate2_o + 512 * dh:gate2_o + 512 * dh + 512], ALU.mult),
                    p, ye_free, m_g2, *route_end))
            bfree[4] = ym[-1:]
            if z == 1:
                pending = ym
        p = combine(pending)
        p_ex = p
        ex_end = [p_ex, m_X[3], ym[-1], (dve.name, dve.count), (act.name, act.count)]

        slots[:] = list(range(NR0))
        extra = [last_user[s] for s in range(NR0, len(ring_o))]
        extra_m = [c.released for c in extra if c is not None]
        end = ex_end + extra_m
        xnT = xs2
        w1 = Work(xnT + 4096)
        U = w1.take(4 * 542)
        cv = w1.take(2048)
        yT_conv = w1.take(2048)
        tp = w1.take(2048)
        assert w1.o <= X
        w2 = Work(X + 4096)
        psb = w2.take(2048 + 64)
        yT_pool = w2.take(2048)
        gf_o = gate1_o
        m_gf = load(act, at(gf_o, 1024), bass.AP(t["g_final_2"].tensor, t["g_final_2"].offset, [[0, 128], [1, 1024]]), "l_gf", *end)

        xsn = xnT + 4096 - 4096
        xs3 = U
        assert xs3 + 4096 <= tp
        m_xs = rms(X, xs3, m_X, end, tp, end)
        m_xn = turn(xs3, m_xs, lambda k: at(xnT + 512 * k, 512), lambda k: vcol("gmix", k), None, [m_vec], end, [0, 1, 2, 3])
        p_t = (pe.name, pe.count)
        xn = lambda k: at(xnT + 512 * k, 512)
        pads = dve.do(lambda e: e.memset(raw(U, [(542, 4), (1, 30)]), 0.0), p_t)
        padp = dve.do(lambda e: e.memset(raw(psb, [(528, 4), (1, 16)]), 0.0), *end)
        u_m = [None] * 4
        tfree = [p_t, p_t, p_t, p_t]
        tn_ = [0]

        def tget():
            i = tn_[0] % 4
            tn_[0] += 1
            return i, tp + 512 * i

        pool_t = [w2.take(544), w2.take(544)]
        DG = w1.take(31 * 128)
        assert w1.o <= X
        y_m, cv_m, po_m = [None] * 8, [None] * 4, [None] * 4
        w2c = t["w_in_2"]
        tap = lambda i, k: at(o_vec + VEC["wdw"][0] + 31 * i + k, 1)
        dg = [pool.do(lambda e, k=k: e.tensor_scalar(at(DG + 128 * k, 128), ident, tap(3, k), None, ALU.mult), *end)
              for k in range(31)]

        def glu(i, cg, ca):
            bg, ba = next_bank([0, 1, 2, 3]), next_bank([0, 1, 2, 3])
            p = dense_T(bg, cg, i % 2, xn, m_xn)
            n, o = tget()
            a = act.do(lambda e: e.activation(at(o, 512), bank(bg), ACT.Sigmoid, bias=vcol("bin", 4 + i)), p, tfree[n])
            bfree[bg] = [a]
            p = dense_T(ba, ca, i % 2, xn, m_xn)
            u_m[i] = dve.do(lambda e: e.scalar_tensor_tensor(
                out=at(U + 542 * i + 30, 512), in0=bank(ba), scalar=vcol("bin", i), in1=at(o, 512),
                op0=ALU.add, op1=ALU.mult), p, a, p_t)
            bfree[ba] = [u_m[i]]
            tfree[n] = u_m[i]

        def conv(*runs):
            for n in range(max(last - first for _, first, last in runs)):
                for i, first, last in runs:
                    k = first + n
                    if k >= last:
                        continue
                    v, u = at(cv + 512 * i, 512), at(U + 542 * i + k, 512)
                    if k == 0:
                        cv_m[i] = dve.do(lambda e, i=i, u=u, v=v: e.tensor_scalar(v, u, tap(i, 0), vcol("bdw", i), ALU.mult, ALU.add),
                                         u_m[i], pads, p_t)
                    else:
                        cv_m[i] = dve.do(lambda e, i=i, k=k, u=u, v=v: e.scalar_tensor_tensor(
                            out=v, in0=u, scalar=tap(i, k), in1=v, op0=ALU.mult, op1=ALU.add), cv_m[i])

        def pool_in(g, c):
            pool_dense(g, c)
            pool_window(g)

        def pool_dense(g, c):
            bk = next_bank([0, 1, 2, 3])
            po_m[g] = bk, dense_T(bk, c, g % 2, xn, m_xn)

        def pool_window(g):
            bk, p = po_m[g]
            po, w = psb + 528 * g + 16, WIN[g]
            m = act.do(lambda e: e.activation(at(po, 512), bank(bk), ACT.Identity, bias=vcol("bin", 8 + g)), p, *end)
            bfree[bk] = [m]
            cur, h, n = po, 1, 0
            while h < w:
                left, d = w - 2 * h, pool_t[n % 2] + 16
                m = dve.do(lambda e, d=d, left=left, cur=cur, h=h: e.tensor_tensor(
                    at(d - left, 512 + left), at(cur - left, 512 + left), at(cur - left - h, 512 + left), ALU.add), m, padp, *end)
                cur, h, n = d, 2 * h, n + 1
            m = dve.do(lambda e: e.tensor_tensor(at(cur, 16), at(cur, 16), at(o_cst + CST["popc"][0] + 16 * g, 16), ALU.mult), m)
            po_m[g] = dve.do(lambda e: e.scalar_tensor_tensor(
                out=at(po, 512), in0=at(cur, 512), scalar=1.0 / w, in1=at(po, 512), op0=ALU.mult, op1=ALU.subtract), m)

        def pool_out(g):
            bk = next_bank([0, 1, 2, 3])
            p = pe.do(lambda e: e.matmul(bank(bk), at(o_vec + VEC["wpool"][0] + 128 * g, 128), at(psb + 528 * g + 16, 512),
                                         start=True, stop=True), po_m[g], *bfree[bk])
            y_m[4 + g] = act.do(lambda e: e.activation(at(yT_pool + 512 * g, 512), bank(bk), ACT.Copy, scale=vcol("spool", g)), p, *end)
            bfree[bk] = [y_m[4 + g]]

        cg, ca = col_chunk(w2c, 3), col_chunk(w2c, 1)
        glu(3, cg, ca)
        glu(2, cg, ca)
        conv((2, 0, 17))
        cg, ca = col_chunk(w2c, 2), col_chunk(w2c, 0)
        glu(0, cg, ca)
        conv((2, 17, 31), (0, 0, 14))
        glu(1, cg, ca)
        for k in range(31):
            p = pe.do(lambda e, k=k: e.matmul(bank(6), at(DG + 128 * k, 128), at(U + 542 * 3 + k, 512),
                                              start=(k == 0), stop=(k == 30)), u_m[3], pads, dg[k], *bfree[6])
        cv_m[3] = act.do(lambda e: e.activation(at(cv + 1536, 512), bank(6), ACT.Identity, bias=vcol("bdw", 3)), p, p_t)
        bfree[6] = [cv_m[3]]
        conv((0, 14, 31), (1, 0, 17))
        conv((1, 17, 31))
        c = col_chunk(w2c, 5)
        pool_in(3, c)
        pool_in(2, c)
        for i in (3, 2, 0, 1):
            f = lambda e, i=i: e.matmul(bank(4), cst("o512"), at(cv + 512 * i, 512), start=(i == 3), stop=(i == 1))
            p = pe.do(f, cv_m[i], *bfree[4])
        d_m, s_m = [], []
        for i in range(4):
            d_m.append(dve.do(lambda e, i=i: e.tensor_tensor(at(cv + 512 * i, 512), at(cv + 512 * i, 512), bank(4), ALU.subtract), p))
            s_m.append(act.do(lambda e, i=i: e.activation(at(tp + 512 * i, 512), at(cv + 512 * i, 512), ACT.Square), d_m[i], *tfree))
        bfree[4] = [d_m[-1]]
        c = col_chunk(w2c, 4)
        pool_in(1, c)
        pool_out(3)
        pool_out(2)
        for i in range(4):
            p = pe.do(lambda e, i=i: e.matmul(bank(5), cst("o512"), at(tp + 512 * i, 512), start=(i == 0), stop=(i == 3)), s_m[i], *bfree[5])
        p_var = p
        pool_dense(0, c)
        rs = U
        a2, m = rsqrt_tile(at(rs, 512), bank(5), "eps5", p_var, *cv_m)
        bfree[5] = [a2]
        for i in range(4):
            b = dve.do(lambda e, i=i: e.tensor_tensor(at(cv + 512 * i, 512), at(cv + 512 * i, 512), at(rs, 512), ALU.mult), m, s_m[i])
            y_m[i] = act.do(lambda e, i=i: e.activation(at(yT_conv + 512 * i, 512), at(cv + 512 * i, 512), ACT.Silu,
                                                        bias=vcol("lnb", i), scale=vcol("lng", i)), b, p_t)
        pool_window(0)
        pool_out(1)
        pool_out(0)
        y_lhs = lambda k, tc: at((yT_conv + 512 * k if k < 4 else yT_pool + 512 * (k - 4)) + 128 * tc, 128)
        hid_o = work
        tq = hid_o + FT * 512
        XH = part("xh", tq + 2048, 4096)
        assert tq + 2048 + 4096 <= X
        w2 = Work(X + 4096)
        wo = w2.take(8192)
        WH = [part(f"wh{i}", wo + 4096 * i, 2048) for i in range(2)]
        WL = [part(f"wl{i}", wo + 4096 * i + 2048, 2048) for i in range(2)]
        XL = part("xl", w2.take(4096), 4096)
        hidf = part("hidf", hid_o, FT * 512, F32)
        xs4, scr = xnT, DG
        m_X2, m_xs = [], []
        y_end = [(act.name, act.count), (dve.name, dve.count), (pe.name, pe.count)]

        def second_norm(h, m):
            m_X2.extend([m, m])
            m_xs.extend(rms(X, xs4, [m] * 4, y_end, scr, y_end, (2 * h, 2 * h + 1)))

        residual_out(t["w_out_2"], y_lhs, y_m, X, m_X, None, None, None, None, [0, 1, 2, 3, 6, 7], second_norm)
        m_X = m_X2
        p_o2 = (pe.name, pe.count)
        end2 = [p_o2, (act.name, act.count), (dve.name, dve.count)]
        w_free = [end2, end2]
        wn = [0]

        def split_chunk(c, by=dve):
            i = wn[0] % 2
            wn[0] += 1
            m = c.released = split(c.flat, WH[i][:, :], WL[i][:, :], c.mark, free=w_free[i], by=by)
            return i, m

        def dense_3(bk, i, m, j):
            for k in range(KD):
                o, x = 256 * k + 128 * j, slice(512 * k, 512 * k + 512)
                pe.quiet(lambda e, o=o, x=x, k=k: e.matmul(bank(bk), WH[i][:, o:o + 128], XH[:, x], start=(k == 0), stop=False),
                         m, m_x3[k], *(bfree[bk] if k == 0 else ()))
                pe.quiet(lambda e, o=o, x=x: e.matmul(bank(bk), WH[i][:, o:o + 128], XL[:, x], start=False, stop=False))
                f = lambda e, o=o, x=x, k=k: e.matmul(bank(bk), WL[i][:, o:o + 128], XH[:, x], start=False, stop=(k == KD - 1))
                if k < KD - 1:
                    pe.quiet(f)
                else:
                    p = pe.do(f)
            w_free[i] = [p]
            return p

        def down_chunk(n):
            return chunk(t["w_down_2"][n * 256:(n + 1) * 256, :].rearrange("(k p) n -> p k n", p=128), (2, 1024))

        tqf = [None] * 4
        hm = [None] * FT
        m_x3 = []

        def split_x(k, m):
            nonlocal gate_w
            if k == 0:
                gate_w = split_chunk(col_chunk(t["w_gate_2"], 0), pool)
            m_x3.append(split(hidf[:, 4096 + 512 * k:4608 + 512 * k], XH[:, 512 * k:512 * k + 512], XL[:, 512 * k:512 * k + 512], m, free=end2))

        gate_w = None
        m_xn = turn(xs4, m_xs, lambda k: hidf[:, 4096 + 512 * k:4608 + 512 * k], lambda k: vcol("gffn", k), None, [m_vec], end2,
                    [0, 1, 2, 3], split_x)
        p_t = (pe.name, pe.count)
        up_w = split_chunk(col_chunk(t["w_up_2"], 0))
        for n in range(FT // 2):
            sg_m = [None] * 2
            for j in range(2):
                f_ = 2 * n + j
                o = tq + 512 * (f_ % 4)
                bk = next_bank([0, 1, 2, 3])
                p = dense_3(bk, *gate_w, j)
                sg_m[j] = act.do(lambda e, bk=bk, o=o: e.activation(at(o, 512), bank(bk), ACT.Silu), p, tqf[f_ % 4], *end2)
                bfree[bk] = [sg_m[j]]
            gate_w = split_chunk(col_chunk(t["w_gate_2"], n + 1) if n + 1 < FT // 2 else down_chunk(0))
            for j in range(2):
                f_ = 2 * n + j
                o = tq + 512 * (f_ % 4)
                bk = next_bank([0, 1, 2, 3])
                p = dense_3(bk, *up_w, j)
                hm[f_] = dve.do(lambda e, bk=bk, o=o, f_=f_: e.tensor_tensor(hidf[:, 512 * f_:512 * f_ + 512], at(o, 512), bank(bk), ALU.mult),
                                p, sg_m[j], p_t, m_x3[-1])
                bfree[bk] = [hm[f_]]
                tqf[f_ % 4] = hm[f_]
            up_w = split_chunk(col_chunk(t["w_up_2"], n + 1) if n + 1 < FT // 2 else down_chunk(1))
        h_free = [p, p]
        down_w = [gate_w, up_w]

        def hid_parts(n):
            o = 2048 * (n % 2)
            return XH[:, o:o + 1024], XH[:, o + 1024:o + 2048]
        mh_next = split(hidf[:, 0:1024], *hid_parts(0), hm[1], free=[p])
        for n in range(FT // 2):
            i, m = down_w[n % 2]
            z = n % 2
            HH, HL = hid_parts(n)
            mh = mh_next
            if n + 1 < FT // 2:
                mh_next = split(hidf[:, 1024 * n + 1024:1024 * n + 2048], *hid_parts(n + 1), hm[2 * n + 3], free=[h_free[1 - z]])
            for k in range(2):
                f_ = 2 * n + k
                for tc in range(TC):
                    o = slice(512 * k + 128 * tc, 512 * k + 128 * tc + 128)
                    for q, (l, w) in enumerate(((HH, WH), (HH, WL), (HL, WH))):
                        for dh in range(2):
                            f = lambda e, i=i, k=k, f_=f_, tc=tc, dh=dh, o=o, l=l, w=w, q=q: e.matmul(
                                bank(2 * tc + dh), l[:, o], w[i][:, 1024 * k + 512 * dh:1024 * k + 512 * dh + 512],
                                start=(f_ == 0 and q == 0), stop=(f_ == FT - 1 and q == 2))
                            mk = [m, mh] + (bfree[2 * tc + dh] if f_ == 0 and q == 0 else [])
                            if q == 2 and ((k, tc, dh) == (1, 3, 1) or f_ == FT - 1):
                                p = pe.do(f, *mk)
                                if f_ == FT - 1:
                                    st["dn", tc, dh] = p
                            else:
                                pe.quiet(f, *mk)
            w_free[i] = [p]
            h_free[z] = p
            if n + 2 < FT // 2:
                down_w[z] = split_chunk(down_chunk(n + 2))
        fin = small(8)
        so = hid_o
        ov = out.rearrange("b (c p) d -> p (b c) d", p=128)
        for tc in range(TC):
            for dh in range(2):
                xa = at(X + 1024 * tc + 512 * dh, 512)
                m = dve.do(lambda e, xa=xa, tc=tc, dh=dh: e.tensor_tensor(xa, xa, bank(2 * tc + dh), ALU.add), st["dn", tc, dh], m_X[tc])
            a = act.do(lambda e, tc=tc: e.activation(at(so + 1024 * tc, 1024), at(X + 1024 * tc, 1024), ACT.Square, scale=1.0 / 32,
                                                     accum_out=at(fin + tc, 1)), m, hm[FT - 1])
            _, b = rsqrt(at(fin + 4 + tc, 1), at(fin + tc, 1), "eps6", a)
            b = dve.do(lambda e, tc=tc: e.scalar_tensor_tensor(out=at(so + 1024 * tc, 1024), in0=at(X + 1024 * tc, 1024),
                                                               scalar=at(fin + 4 + tc, 1), in1=at(gf_o, 1024),
                                                               op0=ALU.mult, op1=ALU.mult), b, m_gf)
            load(act, ov[:, tc, :], at(so + 1024 * tc, 1024), "l_out", b)
        act.wait([("l_out", 64)])

        for c in chunks:
            marks = list(c.first) + ([c.prev.released] if c.prev is not None else [])
            for dst, src in c.parts:
                sp.dma(lambda e, dst=dst, src=src: e.dma_start(dst, src), c.mark[0], c.mark[1], *marks)

        sems = {n: ctx.enter_context(nc.semaphore(n)) for n in
                ["pe", "dve", "act", "pool"] + list(dsems) + [f"r{s}" for s in range(len(ring_o))]}
        block = ctx.enter_context(nc.Block())

        @block.sync
        def _(e):
            sp.emit(e, sems)

        @block.scalar
        def _(e):
            act.emit(e, sems)

        @block.vector
        def _(e):
            dve.emit(e, sems)

        @block.gpsimd
        def _(e):
            pool.emit(e, sems)

        @block.tensor
        def _(e):
            pe.emit(e, sems)


def constants():
    p = np.arange(128)
    c = np.zeros((128, NCST), np.float32)

    def put(n, v):
        c[:, CST[n][0]:CST[n][0] + CST[n][1]] = v
    put("ident", np.eye(128))
    put("ones", 1.0)
    put("tri", p[:, None] < p[None, :])
    put("bo64", (p[:, None] // 64 == p[None, :] // 64) / 64.0)
    rot = np.zeros((128, 128))
    for m in range(128):
        if m % 32 < 16:
            rot[m + 16, m] = -1.0
        else:
            rot[m - 16, m] = 1.0
    put("rot", rot)
    put("o128", 1.0 / 128)
    put("o512", 1.0 / 512)
    put("iota", np.arange(64)[None, :])
    tt = np.arange(16)
    put("popc", np.concatenate([w / np.minimum(tt + 1, w) for w in WIN])[None, :])
    f = np.float32
    inv = (f(10000.0) ** (-np.arange(0, 32, 2, dtype=f) / f(32))).astype(f)
    tok = np.arange(S)
    where = np.stack([(tok // 64).astype(f), (tok % 64).astype(f)])
    d = p % 64
    ang = (where[d // 32] * inv[d % 16][:, None]).astype(f)
    put("ropec", np.cos(ang))
    put("ropes", np.sin(ang))
    put("eps6", 1e-6)
    put("eps5", 1e-5)
    x = p[:, None] ^ p[None, :]
    put("lev", np.concatenate([x >= h for h in LEVELS], 1))
    return c


_BIG = ["ada_w", "w_in", "w_branch_att", "w_branch_hg", "w_out", "w_exp_gate", "w_exp_up", "w_exp_down",
        "w_in_2", "w_out_2", "w_gate_2", "w_up_2", "w_down_2"]


def kernel(**inputs):
    import concourse.bacc as _bacc
    from concourse.bass_utils import run_bass_kernel_spmd as _run

    g = {n: np.ascontiguousarray(v) for n, v in inputs.items()}
    arrays = {"x": g["x"], "ada_b": g["ada_b"], "g_final_2": g["g_final_2"]}
    for n in _BIG:
        arrays[n] = g[n].reshape(g[n].shape[1:])

    def cols(a, k):
        return np.ascontiguousarray(a).reshape(k, 128).T
    parts = {
        "nmw": cols(g["norm_mix_w"], 8), "nfw": cols(g["norm_ffn_w"], 8),
        "qn": np.concatenate([g["q_norm_w"][0]] * 2)[:, None], "kn": np.concatenate([g["k_norm_w"][0]] * 2)[:, None],
        "lb": cols(g["hg_lower_bounds"], 8), "hgw": cols(g["hg_norm_w"], 1), "bin": cols(g["b_in_2"], 12),
        "wdw": g["w_dw_2"][0].T.reshape(4, 128, 31).transpose(1, 0, 2).reshape(128, 124),
        "bdw": cols(g["b_dw_2"], 4), "lng": cols(g["ln_g_2"], 4), "lnb": cols(g["ln_b_2"], 4),
        "spool": cols(g["s_pool_2"], 4), "gmix": cols(g["g_mix_2"], 8), "gffn": cols(g["g_ffn_2"], 8), "c": cols(g["c"], 8),
        "wr": g["w_router"][0].reshape(8, 128, 16).transpose(1, 0, 2).reshape(128, 128),
        "wpool": g["w_pool_2"][0].transpose(1, 0, 2).reshape(128, 512),
    }
    arrays["vec"] = np.ascontiguousarray(np.concatenate([parts[n] for n in VEC], 1))
    arrays["cst"] = constants()

    nc = _bacc.Bacc("TRN2", target_bir_lowering=False, num_devices=1)
    feed, t = {}, {}
    for n, a in arrays.items():
        feed[f"in_{n}"] = a
        t[n] = nc.dram_tensor(f"in_{n}", a.shape, mybir.dt.from_np(a.dtype), kind="ExternalInput").ap()
    out = nc.dram_tensor("out_0", (1, S, D), F32, kind="ExternalOutput").ap()
    build(nc, t, out)
    r = _run(nc, [feed], core_ids=[0])
    return r.results[0]["out_0"]
```
